# Optimizing a Trainium2 kernel written in Bass

```python
import jax, jax.numpy as jnp
from jax import lax
import numpy as np

D_MODEL = 1024
BATCH = 1
SEQ = 512
DEPTH = 2

N_MIXERS = 2
EPS = 1e-6
Q_BLOCK = 128
NEG_INF = -1e30
MEM_LEN = 256
XATTN_HEADS = 4
XATTN_WIDTH = D_MODEL // 4
XATTN_HEAD_DIM = XATTN_WIDTH // XATTN_HEADS
TOKEN_MIX_WIDTH = D_MODEL - XATTN_WIDTH
QK_NOPE_DIM = 64
QK_ROPE_DIM = 32
QK_HEAD_DIM = QK_NOPE_DIM + QK_ROPE_DIM
V_HEAD_DIM = 64
MLA_HEADS = TOKEN_MIX_WIDTH // V_HEAD_DIM
Q_LORA_RANK = D_MODEL // 4
KV_LORA_RANK = D_MODEL // 8
MLA_IN = Q_LORA_RANK + KV_LORA_RANK + QK_ROPE_DIM
ROPE_THETA = 10000.0
POOL_WINDOWS = (2, 4, 8, 16)
POOL_GROUPS = len(POOL_WINDOWS)
POOL_GROUP_WIDTH = TOKEN_MIX_WIDTH // POOL_GROUPS
N_EXPERT_GROUPS = 4
EXPERTS_PER_GROUP = 8
N_EXPERTS = N_EXPERT_GROUPS * EXPERTS_PER_GROUP
TOP_K = 2
D_EXPERT = D_MODEL // 4

kernel_name = 'hybrid_mla_pool_memxattn_hmoe'

def rmsnorm(x, g):
    x32 = x.astype(jnp.float32)
    y = x32 * lax.rsqrt(jnp.mean(x32 * x32, axis=-1, keepdims=True) + EPS)
    return (y * g.astype(jnp.float32)).astype(x.dtype)

def apply_rope(x, cos, sin):
    x1, x2 = jnp.split(x, 2, axis=-1)
    return jnp.concatenate([x1 * cos - x2 * sin, x2 * cos + x1 * sin], axis=-1)

def causal_mla_attention(q_nope, q_rope, k_nope, k_rope, v):
    S = q_nope.shape[1]
    scale = QK_HEAD_DIM ** -0.5
    outs = []
    for blk in range(S // Q_BLOCK):
        lo, hi = blk * Q_BLOCK, (blk + 1) * Q_BLOCK
        s = (jnp.einsum('bqhd,bkhd->bhqk', q_nope[:, lo:hi], k_nope[:, :hi])
             + jnp.einsum('bqhr,bkr->bhqk', q_rope[:, lo:hi], k_rope[:, :hi]))
        s = s.astype(jnp.float32) * scale
        q_idx = lo + jnp.arange(Q_BLOCK)[:, None]
        k_idx = jnp.arange(hi)[None, :]
        s = jnp.where(k_idx <= q_idx, s, NEG_INF)
        p = jax.nn.softmax(s, axis=-1).astype(v.dtype)
        outs.append(jnp.einsum('bhqk,bkhd->bqhd', p, v[:, :hi]))
    return jnp.concatenate(outs, axis=1)

def mla_mixer(z, g_q_lat, w_uq, g_kv_lat, w_ukv, cos, sin):
    B, S, _ = z.shape
    q_lat = z[..., :Q_LORA_RANK]
    kv_lat = z[..., Q_LORA_RANK:Q_LORA_RANK + KV_LORA_RANK]
    k_r = z[..., Q_LORA_RANK + KV_LORA_RANK:]
    q = (rmsnorm(q_lat, g_q_lat) @ w_uq).reshape(B, S, MLA_HEADS, QK_HEAD_DIM)
    q_nope = q[..., :QK_NOPE_DIM]
    q_rope = apply_rope(q[..., QK_NOPE_DIM:], cos[:, :, None, :], sin[:, :, None, :])
    kv = (rmsnorm(kv_lat, g_kv_lat) @ w_ukv).reshape(B, S, MLA_HEADS, QK_NOPE_DIM + V_HEAD_DIM)
    k_nope = kv[..., :QK_NOPE_DIM]
    v = kv[..., QK_NOPE_DIM:]
    k_rope = apply_rope(k_r, cos, sin)
    o = causal_mla_attention(q_nope, q_rope, k_nope, k_rope, v)
    return o.reshape(B, S, MLA_HEADS * V_HEAD_DIM)

def multiscale_pool(u, w_group, scale):
    B, S, C = u.shape
    ug = u.reshape(B, S, POOL_GROUPS, POOL_GROUP_WIDTH).astype(jnp.float32)
    csum = jnp.cumsum(ug, axis=1)
    steps = jnp.arange(1, S + 1)
    outs = []
    for g, win in enumerate(POOL_WINDOWS):
        cg = csum[:, :, g]
        shifted = jnp.pad(cg, ((0, 0), (win, 0), (0, 0)))[:, :S]
        count = jnp.minimum(steps, win).astype(jnp.float32)[None, :, None]
        outs.append((cg - shifted) / count - ug[:, :, g])
    d = jnp.stack(outs, axis=2).astype(u.dtype)
    y = jnp.einsum('bsgc,gcd->bsgd', d, w_group).reshape(B, S, C)
    return y * scale

def memory_cross_attention(qc, mem_k, mem_v):
    B, S, _ = qc.shape
    q = qc.reshape(B, S, XATTN_HEADS, XATTN_HEAD_DIM)
    s = jnp.einsum('bshd,bmhd->bhsm', q, mem_k).astype(jnp.float32) * (XATTN_HEAD_DIM ** -0.5)
    p = jax.nn.softmax(s, axis=-1).astype(qc.dtype)
    return jnp.einsum('bhsm,bmhd->bshd', p, mem_v).reshape(B, S, XATTN_WIDTH)

def hierarchical_moe(h, w_rg, b_rg, w_re, b_re, w_gate, w_up, w_down):
    B, S, D = h.shape
    t = h.reshape(-1, D)
    t32 = t.astype(jnp.float32)
    lg = t32 @ w_rg.astype(jnp.float32) + b_rg.astype(jnp.float32)
    pg = jax.nn.softmax(lg, axis=-1)
    g_sel = jnp.argmax(lg, axis=-1)
    gate_g = jnp.take_along_axis(pg, g_sel[:, None], axis=1)
    le = (t32 @ w_re.astype(jnp.float32) + b_re.astype(jnp.float32)).reshape(-1, N_EXPERT_GROUPS, EXPERTS_PER_GROUP)
    le_sel = jnp.take_along_axis(le, g_sel[:, None, None], axis=1)[:, 0]
    pe = jax.nn.softmax(le_sel, axis=-1)
    top_p, top_i = lax.top_k(pe, TOP_K)
    wts = gate_g * top_p / jnp.sum(top_p, axis=-1, keepdims=True)
    eid = g_sel[:, None] * EXPERTS_PER_GROUP + top_i
    comb = jnp.sum(jax.nn.one_hot(eid, N_EXPERTS, dtype=jnp.float32) * wts[..., None], axis=1).astype(t.dtype)
    y = jnp.zeros_like(t)
    for e in range(N_EXPERTS):
        a = jax.nn.silu(t @ w_gate[e]) * (t @ w_up[e])
        y = y + comb[:, e:e + 1] * (a @ w_down[e])
    return y.reshape(B, S, D)

def setup_inputs(seed: int = 0) -> dict:
    key = jax.random.key(seed)
    ks = iter(jax.random.split(key, 32))
    f32 = jnp.float32
    n_mla = (DEPTH + 1) // 2
    n_pool = DEPTH // 2

    def w(shape, fan_in):
        return jax.random.normal(next(ks), shape, f32) * (fan_in ** -0.5)

    def gain(shape, s=0.05):
        return 1.0 + s * jax.random.normal(next(ks), shape, f32)

    x = jax.random.normal(next(ks), (BATCH, SEQ, D_MODEL), f32)
    mem = jax.random.normal(next(ks), (BATCH, MEM_LEN, D_MODEL), f32)
    offset = jax.random.randint(next(ks), (BATCH, 1), 0, 4096, dtype=jnp.int32)
    positions = (offset + jnp.arange(SEQ, dtype=jnp.int32)[None, :]).astype(jnp.int32)
    return {
        'x': x,
        'mem': mem,
        'positions': positions,
        'g_mix': gain((DEPTH, D_MODEL)),
        'w_in_mla': w((n_mla, D_MODEL, MLA_IN + XATTN_WIDTH), D_MODEL),
        'g_q_lat': gain((n_mla, Q_LORA_RANK)),
        'w_uq': w((n_mla, Q_LORA_RANK, MLA_HEADS * QK_HEAD_DIM), Q_LORA_RANK),
        'g_kv_lat': gain((n_mla, KV_LORA_RANK)),
        'w_ukv': w((n_mla, KV_LORA_RANK, MLA_HEADS * (QK_NOPE_DIM + V_HEAD_DIM)), KV_LORA_RANK),
        'w_in_pool': w((n_pool, D_MODEL, TOKEN_MIX_WIDTH + XATTN_WIDTH), D_MODEL),
        'w_pool_mix': w((n_pool, POOL_GROUPS, POOL_GROUP_WIDTH, POOL_GROUP_WIDTH), POOL_GROUP_WIDTH),
        'pool_scale': gain((n_pool, TOKEN_MIX_WIDTH), 0.1),
        'g_mem': gain((D_MODEL,)),
        'w_mem_kv': w((D_MODEL, 2 * XATTN_WIDTH), D_MODEL),
        'w_o': w((DEPTH, D_MODEL, D_MODEL), D_MODEL),
        'g_ffn': gain((DEPTH, D_MODEL)),
        'w_router_group': w((DEPTH, D_MODEL, N_EXPERT_GROUPS), D_MODEL),
        'b_router_group': 0.01 * jax.random.normal(next(ks), (DEPTH, N_EXPERT_GROUPS), f32),
        'w_router_expert': w((DEPTH, D_MODEL, N_EXPERTS), D_MODEL),
        'b_router_expert': 0.01 * jax.random.normal(next(ks), (DEPTH, N_EXPERTS), f32),
        'w_expert_gate': w((DEPTH, N_EXPERTS, D_MODEL, D_EXPERT), D_MODEL),
        'w_expert_up': w((DEPTH, N_EXPERTS, D_MODEL, D_EXPERT), D_MODEL),
        'w_expert_down': w((DEPTH, N_EXPERTS, D_EXPERT, D_MODEL), D_EXPERT),
        'g_final': gain((D_MODEL,)),
    }

def reference(x, mem, positions, g_mix, w_in_mla, g_q_lat, w_uq, g_kv_lat, w_ukv, w_in_pool, w_pool_mix, pool_scale, g_mem, w_mem_kv, w_o, g_ffn, w_router_group, b_router_group, w_router_expert, b_router_expert, w_expert_gate, w_expert_up, w_expert_down, g_final):
    B = x.shape[0]
    M = mem.shape[1]
    mem_kv = rmsnorm(mem, g_mem) @ w_mem_kv
    mem_k = mem_kv[..., :XATTN_WIDTH].reshape(B, M, XATTN_HEADS, XATTN_HEAD_DIM)
    mem_v = mem_kv[..., XATTN_WIDTH:].reshape(B, M, XATTN_HEADS, XATTN_HEAD_DIM)
    inv_freq = ROPE_THETA ** (-jnp.arange(0, QK_ROPE_DIM, 2, dtype=jnp.float32) / QK_ROPE_DIM)
    ang = positions.astype(jnp.float32)[..., None] * inv_freq
    cos = jnp.cos(ang).astype(x.dtype)
    sin = jnp.sin(ang).astype(x.dtype)
    for i in range(DEPTH):
        h = rmsnorm(x, g_mix[i])
        j = i // N_MIXERS
        if i % N_MIXERS == 0:
            z = h @ w_in_mla[j]
            mix = mla_mixer(z[..., :MLA_IN], g_q_lat[j], w_uq[j], g_kv_lat[j], w_ukv[j], cos, sin)
            qc = z[..., MLA_IN:]
        else:
            z = h @ w_in_pool[j]
            mix = multiscale_pool(z[..., :TOKEN_MIX_WIDTH], w_pool_mix[j], pool_scale[j])
            qc = z[..., TOKEN_MIX_WIDTH:]
        xa = memory_cross_attention(qc, mem_k, mem_v)
        x = x + jnp.concatenate([mix, xa], axis=-1) @ w_o[i]
        x = x + hierarchical_moe(rmsnorm(x, g_ffn[i]), w_router_group[i], b_router_group[i], w_router_expert[i], b_router_expert[i], w_expert_gate[i], w_expert_up[i], w_expert_down[i])
    return rmsnorm(x, g_final)


_drawn_inputs = setup_inputs


def setup_inputs(seed=0):
    import zlib

    import numpy as np

    out = dict(_drawn_inputs(seed))
    spreads = {}
    factors = {'b_router_group': 6.074, 'g_mem': 3.908}
    for name, (base, spread) in spreads.items():
        noise = np.random.default_rng([zlib.crc32(name.encode()), seed]).standard_normal(out[name].shape)
        drawn = base * np.exp(spread * noise) if base else spread * noise
        out[name] = __import__('jax').numpy.asarray(drawn.astype(out[name].dtype))
    for name, factor in factors.items():
        out[name] = (out[name] * factor).astype(out[name].dtype)
    return out
```

```python
from contextlib import ExitStack

import numpy as np

import concourse.bass as bass
from concourse import mybir

F32 = mybir.dt.float32
BF16 = mybir.dt.bfloat16
I32 = mybir.dt.int32
ALU = mybir.AluOpType
ACT = mybir.ActivationFunctionType
AX = mybir.AxisListType

P = 128
EPS = 1e-6
NEG_INF = -1e30
THETA = 10000.0
WINDOWS = (2, 4, 8, 16)
XHEADS = 4
GROUPS = 4
PER_GROUP = 8
SLOTS = 64
RING = 4
NO_TOKEN = 1 << 20


def program(nc, x, mem, positions, g_mix, w_in_mla, g_q_lat, w_uq, g_kv_lat, w_ukv, w_in_pool, w_pool_mix,
            pool_scale, g_mem, w_mem_kv, w_o, g_ffn, w_router_group, b_router_group, w_router_expert,
            b_router_expert, w_expert_gate, w_expert_up, w_expert_down, g_final, out):
    S, D = x.shape[1:]
    M = mem.shape[1]
    NT, MT, KD = S // P, M // P, D // P
    QR, KVR = g_q_lat.shape[1], g_kv_lat.shape[1]
    XW = w_mem_kv.shape[1] // 2
    XD = XW // XHEADS
    MW = D - XW
    ROPE = w_in_mla.shape[2] - QR - KVR - XW
    HALF = ROPE // 2
    VD = 64
    NOPE = 64
    H = MW // VD
    QKD = NOPE + ROPE
    ZW = w_in_mla.shape[2]
    ZA = QR + KVR + ROPE
    KQ = QR // P
    E = w_expert_gate.shape[1]
    FE = w_expert_gate.shape[3]
    KF = FE // P
    NR = GROUPS + E
    GW = MW // len(WINDOWS)
    HW = GW // 2
    ROUNDS = S // SLOTS
    HALO = P + max(WINDOWS) - 1
    QSCALE = QKD ** -0.5
    XSCALE = XD ** -0.5
    assert (S, D, M, QR, KVR, XD, ROPE, H, E, FE) == (512, 1024, 256, 256, 128, 64, 32, 12, 32, 256)
    inv_freq = (THETA ** (-np.arange(0, ROPE, 2, dtype=np.float64) / ROPE)).astype(np.float32)

    with ExitStack() as ctx:
        def sb(name, shape, dt=F32):
            return ctx.enter_context(nc.sbuf_tensor(name, shape, dt))

        sems = {}

        def sem(name):
            if name not in sems:
                sems[name] = ctx.enter_context(nc.semaphore(name))
            return sems[name]

        xn_dram = [nc.dram_tensor(f"xn_rows_{l}", (S, D), F32, kind="Internal").ap() for l in range(2)]
        slot_dram = [nc.dram_tensor(f"slot_table_{l}", (S * E, 1), I32, kind="Internal").ap() for l in range(2)]
        y_dram = [nc.dram_tensor(f"expert_rows_{l}", (2 * S, D), F32, kind="Internal").ap() for l in range(2)]

        X = sb("X", [P, NT, D])
        XN = sb("XN", [P, NT, D])
        HT = sb("HT", [P, KD * S])
        WIN = sb("WIN", [P, KD * D])
        WE = sb("WE", [P, RING, 3 * KD * FE])
        T = sb("T", [P, 5376])
        MK = sb("MK", [P, XW // P, M])
        MV = sb("MV", [P, MT, XW])
        WR = sb("WR", [P, KD, NR])
        ident = sb("ident", [P, P])
        identb = sb("identb", [P, P], BF16)
        causal = sb("causal", [P, P], BF16)
        before = sb("before", [P, P], BF16)
        onesb = sb("onesb", [P, P], BF16)
        iota_e = sb("iota_e", [P, E])
        tie = sb("tie", [P, PER_GROUP])
        thresh = sb("thresh", [P, ROUNDS - 1])
        dest = sb("dest", [P, 2 * NT], I32)
        slot_pos = sb("slot_pos", [P, 2 * NT], I32)
        SIDX = sb("SIDX", [P, ROUNDS * E], I32)
        GIDX = sb("GIDX", [P, ROUNDS * E], I32)
        gidx = sb("gidx", [P, RING], I32)
        sidx = sb("sidx", [P, 2], I32)
        extra = sb("extra", [P, 1], I32)
        GN = sb("GN", [P, 5, KD])
        gq = sb("gq", [P, KQ])
        gkv = sb("gkv", [P, 1])
        bias_r = sb("bias_r", [P, 2, NR])
        stat = sb("stat", [P, 64])
        wtok = sb("wtok", [P, 2, NT])

        def view(base, at, *shape):
            n = int(np.prod(shape))
            v = base[:, at:at + n]
            if len(shape) == 2:
                v = v.rearrange("p (a b) -> p a b", a=shape[0])
            if len(shape) == 3:
                v = v.rearrange("p (a b c) -> p a b c", a=shape[0], b=shape[1])
            return v

        hT = view(HT, 0, KD, S)
        WEflat = WE[:, :, :].rearrange("p r n -> p (r n)")
        RB = 3 * KD * FE
        memhT = view(HT, 0, KD, M)
        MEM = view(HT, KD * M, MT, D)
        w_mkv = view(WEflat, 2 * RB, KD, 2 * XW)
        w_out = view(WEflat, 2 * RB + KD * 2 * XW, KD, D)
        w_mla = view(WIN, 0, KD, ZW)
        ZS = view(WIN, KD * ZW, NT, ZW)
        w_q = view(WEflat, RB, KQ, H * QKD)
        w_kv = view(WEflat, RB + 2304, H * 2 * VD)
        QLT = view(WEflat, RB + 3840, KQ, S)
        KVT = view(WEflat, RB + 4864, S)
        TBL = view(WEflat, RB + 5376, S)
        V = view(HT, 0, NT, MW)
        QCT0 = view(HT, NT * MW, XW // P, S)
        PR = view(T, 0, 1280)
        PT = view(T, 1280, 2, S)
        qT = [view(T, 2304 + 512 * s, S) for s in range(2)]
        kT = [view(T, 3328 + 512 * s, S) for s in range(2)]
        wqh = [view(T, 4352 + 256 * s, KQ, P) for s in range(2)]
        wkh = [view(T, 4864 + 64 * s, 64) for s in range(2)]
        posf = view(T, 0, NT)
        freq = view(T, 8, HALF)
        ang = view(T, 64, NT, HALF)
        turns = view(T, 128, 2, NT * HALF)
        rang = view(T, 256, 2, NT * HALF)
        trig = view(T, 384, 2, NT * HALF)
        tbl_tok = view(T, 512, NT, P)
        kr_tok = view(T, 1024, NT, P)
        posi = T[:, 1536:1536 + NT].bitcast(I32)
        XP0, XPT0 = view(T, 0, NT, M), view(T, NT * M, MT, S)
        w_pool = view(WIN, 0, KD, D)
        U = view(T, 0, NT, MW)
        QC = view(T, NT * MW, NT, XW)
        band = view(T, NT * D, len(WINDOWS), HALO)
        band0 = view(T, NT * D + len(WINDOWS) * HALO, len(WINDOWS), max(WINDOWS))
        ramp = view(T, NT * D + len(WINDOWS) * (HALO + 16), len(WINDOWS), max(WINDOWS))
        dT = view(HT, 0, 2 * len(WINDOWS), S)
        QCT1 = view(WEflat, RB, XW // P, S)
        XP1 = view(WEflat, RB + 1024, NT, M)
        XPT1 = view(WEflat, RB + 2048, MT, S)
        w_mix = view(WEflat, RB + 3072, 2 * len(WINDOWS), GW)
        scale_b = view(WEflat, RB + 3072 + 8 * GW, MW)
        XG = view(HT, 0, RING, D)
        XGT = view(T, 0, 2, KD * SLOTS)
        YS = view(T, D, 2, D)
        SG = view(T, 3 * D, 2, FE)
        AE = view(T, 3 * D + 2 * FE, 2, FE)
        AT = view(T, 3 * D + 4 * FE, 2, KF * SLOTS)
        YL = view(HT, 0, 2, 2 * D)
        gfin = view(WIN, 0, D)
        LG = view(T, 0, NT, NR)
        LS = view(T, 256, NT, GROUPS)
        EG = view(T, 272, NT, GROUPS)
        SC = view(T, 288, NT, PER_GROUP)
        OG = view(T, 320, NT, GROUPS)
        LE = view(T, 384, NT, E)
        SEL = view(T, 512, NT, PER_GROUP)
        O1 = view(T, 544, NT, PER_GROUP)
        O2 = view(T, 576, NT, PER_GROUP)
        A1 = view(T, 640, NT, E)
        A2 = view(T, 768, NT, E)
        POS = view(T, 896, NT, E)
        PM = view(T, 1024, NT, E)
        AB = T[:, 1152:1152 + NT * E // 2].bitcast(BF16).rearrange("p (t e) -> p t e", t=NT)
        small = view(T, 1280, 64)
        INV = T[:, 1408:1536].bitcast(I32)
        CF = view(T, 2560, ROUNDS * E)

        banks = [ctx.enter_context(nc.psum_tensor(f"bank{i}", [P, 512], F32)) for i in range(8)]

        def bank(i, *shape):
            v = banks[i][:, :]
            if shape:
                v = v[:, 0:int(np.prod(shape))].rearrange("p (a b) -> p a b", a=shape[0])
            return v

        def wide(ap, *shape):
            return ap.to_broadcast(list(shape))

        def wait(eng, name, count):
            if not isinstance(count, int) or count > 0:
                eng.wait_ge(sem(name), count)

        def feat(w):
            return w.rearrange("(p k) n -> p (k n)", p=P)

        def row(v):
            return v.rearrange("(a n) -> a n", a=1)

        TILES = [0] + [MT + NT * n for n in range(5)]
        block = ctx.enter_context(nc.Block())

        @block.sync
        def _(sp):
            for t in range(MT):
                sp.dma_start(MEM[:, t, :], mem[0, t * P:(t + 1) * P, :]).then_inc(sem("mem_in"), 16)
            sp.dma_start(w_mkv.rearrange("p k n -> p (k n)"), feat(w_mem_kv)).then_inc(sem("w_mkv_in"), 16)
            for t in range(NT):
                sp.dma_start(X[:, t, :], x[0, t * P:(t + 1) * P, :]).then_inc(sem("x_in"), 16)
            sp.dma_start(w_mla.rearrange("p k n -> p (k n)"), feat(w_in_mla[0])).then_inc(sem("w_mla_in"), 16)
            sp.dma_start(w_kv, w_ukv[0]).then_inc(sem("w_qkv_in"), 16)
            sp.dma_start(w_q.rearrange("p k n -> p (k n)"), feat(w_uq[0])).then_inc(sem("w_qkv_in"), 16)
            sp.dma_start(w_out.rearrange("p k n -> p (k n)"), feat(w_o[0])).then_inc(sem("w_out_in"), 16)

            def load_expert(l, u, e, free_at):
                ready = sem(f"w_ready_{l}_{u}")
                if free_at is not None:
                    sp.wait_ge(sem(f"y_full_{l}"), free_at)
                for j, w in enumerate((w_expert_gate, w_expert_up)):
                    src = w[l, bass.ds(e, 1)].rearrange("a (p k) n -> p (a k n)", p=P)
                    sp.dma_start(WE[:, u, j * KD * FE:(j + 1) * KD * FE], src).then_inc(ready, 16)
                src = w_expert_down[l, bass.ds(e, 1)].rearrange("a (p k) n -> p (a k n)", p=P)
                sp.dma_start(WE[:, u, 2 * KD * FE:], src).then_inc(ready, 16)

            for l in range(2):
                load_expert(l, 0, 0, None)
                sp.dma_start(WR[:, :, 0:GROUPS], w_router_group[l].rearrange("(p k) n -> p k n", p=P))\
                    .then_inc(sem("wr_in"), 16)
                sp.dma_start(WR[:, :, GROUPS:], w_router_expert[l].rearrange("(p k) n -> p k n", p=P))\
                    .then_inc(sem("wr_in"), 16)
                for t in range(NT):
                    sp.wait_ge(sem("xn"), TILES[2 * l + 2] + t + 1)
                    sp.dma_start(xn_dram[l][t * P:(t + 1) * P, :], XN[:, t, :]).then_inc(sem("xn_out"), 16)
                for u in range(1, RING):
                    load_expert(l, u, u, None)
                sp.wait_ge(sem("inv_ready"), l + 1)
                sp.dma_start(slot_dram[l].rearrange("(p n) a -> p (n a)", p=P), INV)\
                    .then_inc(sem("slot_cleared"), 16)
                sp.wait_ge(sem("slot_scattered"), 16 * 2 * NT * (l + 1))
                sp.dma_start(SIDX[0:SLOTS, :].rearrange("s (r e) -> s r e", r=ROUNDS),
                             slot_dram[l].rearrange("(r s e) a -> s r (e a)", r=ROUNDS, s=SLOTS))\
                    .then_inc(sem("sidx_in"), 16)
                if l == 0:
                    sp.dma_start(w_pool.rearrange("p k n -> p (k n)"), feat(w_in_pool[0])).then_inc(sem("w_pool_in"), 16)
                with sp.Fori(0, E // RING - 1) as i:
                    for u in range(RING):
                        e = sp.snap(RING * i + RING + u)
                        at = sp.snap(RING * i + (u + 1))
                        load_expert(l, u, e, at)
                sp.wait_ge(sem("extra_ready"), l + 1)
                rounds = sp.value_load(extra[0:1, 0:1], min_val=0, max_val=ROUNDS - 1)
                with sp.If(rounds > 0):
                    with sp.Fori(0, rounds) as r:
                        with sp.Fori(0, E // RING) as q:
                            for u in range(RING):
                                e = sp.snap(RING * q + u)
                                at = sp.snap(E * r + RING * q + (E + u - RING + 1))
                                load_expert(l, u, e, at)
                sp.wait_ge(sem("moe_done"), l + 1)
                for t in range(NT):
                    if t >= 2:
                        sp.wait_ge(sem("x_moe"), NT * l + t - 1)
                    for j in range(2):
                        sp.dma_start(YL[:, t % 2, j * D:(j + 1) * D], y_dram[l][j * S + t * P:j * S + (t + 1) * P, :])\
                            .then_inc(sem(f"yl_in_{t % 2}"), 16)
                    if l == 0 and t == 1:
                        sp.dma_start(w_mix[0:HW].rearrange("p (g c) n -> p g c n", c=2),
                                     w_pool_mix[0].rearrange("g (c p) n -> p g c n", c=2)).then_inc(sem("w_mix_in"), 16)
                        sp.dma_start(scale_b, row(pool_scale[0]).to_broadcast([P, MW])).then_inc(sem("w_mix_in"), 16)
                        sp.dma_start(w_out.rearrange("p k n -> p (k n)"), feat(w_o[1])).then_inc(sem("w_out_in"), 16)
                if l == 1:
                    sp.dma_start(gfin, row(g_final).to_broadcast([P, D])).then_inc(sem("gfin_in"), 16)
            for t in range(NT):
                sp.wait_ge(sem("fin"), t + 1)
                sp.dma_start(out[0, t * P:(t + 1) * P, :], XN[:, t, :]).then_inc(sem("out_done"), 16)
            sp.wait_ge(sem("out_done"), 16 * NT)

        @block.gpsimd
        def _(pool):
            steps = [0]

            def link(ins):
                steps[0] += 1
                ins.then_inc(sem("pool_step"), 1)
                pool.wait_ge(sem("pool_step"), steps[0])

            def small_loads():
                for j, g in enumerate((g_mem, g_mix[0], g_ffn[0], g_mix[1], g_ffn[1])):
                    pool.dma_start(GN[:, j, :], g.rearrange("(p k) -> p k", p=P)).then_inc(sem("small_in"), 16)
                pool.dma_start(gq[:, :], g_q_lat[0].rearrange("(p k) -> p k", p=P)).then_inc(sem("small_in"), 16)
                pool.dma_start(gkv[:, :], g_kv_lat[0].rearrange("(p k) -> p k", p=P)).then_inc(sem("small_in"), 16)
                pool.dma_start(posi, positions[0].rearrange("(t p) -> p t", p=P)).then_inc(sem("small_in"), 16)
                for l in range(2):
                    pool.dma_start(bias_r[:, l, 0:GROUPS], row(b_router_group[l]).to_broadcast([P, GROUPS]))\
                        .then_inc(sem("small_in"), 16)
                    pool.dma_start(bias_r[:, l, GROUPS:], row(b_router_expert[l]).to_broadcast([P, E]))\
                        .then_inc(sem("small_in"), 16)

            with nc.allow_non_contiguous_dma(reason="a few small vectors, once"):
                small_loads()
            link(pool.memset(ident[:, :], 0.0))
            pool.affine_select(out=ident[:, :], in_=ident[:, :], compare_op=ALU.not_equal, fill=1.0, base=0,
                               pattern=[[-1, P]], channel_multiplier=1).then_inc(sem("constants"), 1)
            for i, f in enumerate(inv_freq):
                last = pool.memset(freq[:, i:i + 1], float(f))
            last.then_inc(sem("constants"), 1)
            link(pool.memset(tbl_tok, 0.0))
            link(pool.memset(kr_tok, 0.0))
            pool.memset(stat[:, 48:49], 0.0).then_inc(sem("constants"), 1)
            link(pool.memset(identb[:, :], 0.0))
            link(pool.affine_select(out=identb[:, :], in_=identb[:, :], compare_op=ALU.not_equal, fill=1.0, base=0,
                                    pattern=[[-1, P]], channel_multiplier=1))
            link(pool.memset(causal[:, :], 0.0))
            link(pool.affine_select(out=causal[:, :], in_=causal[:, :], compare_op=ALU.is_ge, fill=NEG_INF, base=0,
                                    pattern=[[-1, P]], channel_multiplier=1))
            link(pool.memset(onesb[:, :], 1.0))
            link(pool.affine_select(out=before[:, :], in_=onesb[:, :], compare_op=ALU.is_gt, fill=0.0, base=0,
                                    pattern=[[1, P]], channel_multiplier=-1))
            link(pool.iota(iota_e[:, :], pattern=[[1, E]], base=0, channel_multiplier=0,
                           allow_small_or_imprecise_dtypes=True))
            link(pool.iota(tie[:, :], pattern=[[-1, PER_GROUP]], base=PER_GROUP, channel_multiplier=0,
                           allow_small_or_imprecise_dtypes=True))
            link(pool.iota(thresh[:, :], pattern=[[SLOTS, ROUNDS - 1]], base=SLOTS, channel_multiplier=0,
                           allow_small_or_imprecise_dtypes=True))
            pool.iota(dest[:, :], pattern=[[S, 2], [P, NT]], base=0, channel_multiplier=1)\
                .then_inc(sem("constants"), 1)

            pool.wait_ge(sem("z_key"), NT)
            kr = ZS[:, :, QR + KVR:ZA]
            pool.tensor_copy(kr_tok[:, :, NOPE:QKD], kr).then_inc(sem("kr_ready"), 1)
            pool.tensor_copy(kr_tok[:, :, QKD:QKD + HALF], kr[:, :, HALF:]).then_inc(sem("kr_ready"), 1)
            pool.tensor_copy(kr_tok[:, :, QKD + HALF:], kr[:, :, 0:HALF]).then_inc(sem("kr_ready"), 1)

            def head_weights(s, h, used):
                if used is not None:
                    pool.wait_ge(sem("qk_full"), used)
                src = w_q[:, :, bass.ds(h * QKD, QKD)]
                pool.tensor_copy(wqh[s][:, :, 0:QKD], src).then_inc(sem("wh_ready"), 1)
                a = w_q[:, :, bass.ds(h * QKD + (NOPE + HALF), HALF)]
                pool.tensor_copy(wqh[s][:, :, QKD:QKD + HALF], a).then_inc(sem("wh_ready"), 1)
                b = w_q[:, :, bass.ds(h * QKD + NOPE, HALF)]
                pool.tensor_copy(wqh[s][:, :, QKD + HALF:], b).then_inc(sem("wh_ready"), 1)
                c = w_kv[:, bass.ds(h * 2 * VD, NOPE)]
                pool.tensor_copy(wkh[s], c).then_inc(sem("wh_ready"), 1)

            pool.wait_ge(sem("w_qkv_in"), 32)
            for s in range(2):
                head_weights(s, s, None)
            with pool.Fori(0, H // 2 - 1) as i:
                for s in range(2):
                    head_weights(s, 2 * i + (2 + s), 2 * i + (s + 1))

            def band_matrices():
                for g, w in enumerate(WINDOWS):
                    link(pool.memset(band[:, g, :], 1.0))
                    link(pool.affine_select(out=band[:, g, :], in_=band[:, g, :], compare_op=ALU.is_ge, fill=0.0,
                                            base=0, pattern=[[1, HALO]], channel_multiplier=-1))
                    link(pool.affine_select(out=band[:, g, :], in_=band[:, g, :], compare_op=ALU.is_gt, fill=0.0,
                                            base=w, pattern=[[-1, HALO]], channel_multiplier=1))
                    link(pool.iota(ramp[:, g, :], pattern=[[1, 16]], base=1, channel_multiplier=0,
                                   allow_small_or_imprecise_dtypes=True))
                    link(pool.tensor_scalar(ramp[:, g, :], ramp[:, g, :], float(w), None, ALU.min))
                pool.tensor_copy(band0, band[:, :, 0:16]).then_inc(sem("band_sums"), 1)

            for l in range(2):
                pool.wait_ge(sem("router_full"), l + 1)
                pool.memset(INV, NO_TOKEN).then_inc(sem("inv_ready"), 1)
                pool.wait_ge(sem("slot_cleared"), 16 * (l + 1))
                pool.wait_ge(sem("slot_pos_ready"), 2 * (l + 1))
                for c in range(2 * NT):
                    pool.indirect_dma_start(
                        out=slot_dram[l], out_offset=bass.IndirectOffsetOnAxis(ap=slot_pos[:, c:c + 1], axis=0),
                        in_=dest[:, c:c + 1], in_offset=None, bounds_check=S * E - 1, oob_is_err=False)\
                        .then_inc(sem("slot_scattered"), 16)
                pool.wait_ge(sem("sidx_in"), 16 * (l + 1))
                pool.wait_ge(sem("gidx_ready"), l + 1)
                pool.memset(XG[0:SLOTS, :, :], 0.0).then_inc(sem("xg_cleared"), 1)
                pool.wait_ge(sem("xg_cleared"), l + 1)
                pool.wait_ge(sem("xn_out"), 16 * NT * (l + 1))
                gather_bound = pool.to_reg(S - 1)
                scatter_bound = pool.to_reg(2 * S - 1)

                def settle():
                    pool.sem_inc(sem("pool_settled"), 1)

                def gather(u, e):
                    u %= RING
                    wait(pool, f"xg_full{l}", e - (RING - 1))
                    pool.tensor_copy(gidx[0:SLOTS, u:u + 1], GIDX[0:SLOTS, bass.ds(e, 1)])\
                        .then_inc(sem(f"gidx_set{l}"), 1)
                    pool.wait_ge(sem(f"gidx_set{l}"), e + 1)
                    settle()
                    pool.indirect_dma_start(
                        out=XG[0:SLOTS, u, :], out_offset=None, in_=xn_dram[l],
                        in_offset=bass.IndirectOffsetOnAxis(ap=gidx[0:SLOTS, u:u + 1], axis=0),
                        bounds_check=gather_bound, oob_is_err=False).then_inc(sem(f"xg_in{l}_{u}"), 16)

                def scatter(u, e, turn):
                    b = u % 2
                    wait(pool, f"scattered{l}_{b}", 16 * turn)
                    pool.tensor_copy(sidx[0:SLOTS, b:b + 1], SIDX[0:SLOTS, bass.ds(e, 1)])\
                        .then_inc(sem(f"sidx_set{l}"), 1)
                    pool.wait_ge(sem(f"sidx_set{l}"), e + 1)
                    pool.wait_ge(sem(f"ys_act{l}"), e + 1)
                    pool.wait_ge(sem(f"ys_dve{l}"), e + 1)
                    settle()
                    pool.indirect_dma_start(
                        out=y_dram[l], out_offset=bass.IndirectOffsetOnAxis(ap=sidx[0:SLOTS, b:b + 1], axis=0),
                        in_=YS[0:SLOTS, b, :], in_offset=None, bounds_check=scatter_bound, oob_is_err=False)\
                        .then_inc(sem(f"scattered{l}_{b}"), 16)

                for e in range(RING):
                    gather(e, e)
                for e in range(RING):
                    gather(e, e + RING)
                    scatter(e, e, e // 2)
                with pool.Fori(0, E // RING - 2) as i:
                    for u in range(RING):
                        gather(u, pool.snap(RING * i + (2 * RING + u)))
                        scatter(u, pool.snap(RING * i + (RING + u)), pool.snap(2 * i + (RING + u) // 2))
                for e in range(E - RING, E):
                    scatter(e, e, e // 2)
                pool.wait_ge(sem("extra_ready"), l + 1)
                rounds = pool.value_load(extra[0:1, 0:1], min_val=0, max_val=ROUNDS - 1)
                for b in range(2):
                    pool.wait_ge(sem(f"scattered{l}_{b}"), 16 * E // 2)
                with pool.If(rounds > 0):
                    with pool.Fori(0, rounds) as r:
                        with pool.Fori(0, E // RING) as q:
                            for u in range(RING):
                                e = pool.snap(E * r + RING * q + (E + u))
                                turn = pool.snap(E // 2 * r + 2 * q + (E + u) // 2)
                                gather(u, e)
                                scatter(u, e, turn)
                                pool.wait_ge(sem(f"scattered{l}_{u % 2}"), 16 * turn + 16)
                pool.sem_inc(sem("moe_done"), 1)
                if l == 0:
                    pool.wait_ge(sem("moe_done"), 1)
                    band_matrices()

        NORM_TILES = [MT] + [NT] * 5

        def norm_source(n):
            return MEM if n == 0 else X

        def wait_tile(eng, n, t):
            if n == 0:
                eng.wait_ge(sem("mem_in"), 16 * MT)
            elif n == 1:
                eng.wait_ge(sem("x_in"), 16 * NT)
            elif n % 2 == 0:
                eng.wait_ge(sem("o_added"), 2 * NT * (n // 2 - 1) + 2 * t + 2)
            else:
                eng.wait_ge(sem("x_moe"), NT * (n // 2 - 1) + t + 1)

        def ht_of(n):
            return memhT if n == 0 else hT

        @block.scalar
        def _(act):
            def norm_squares(n):
                nt = NORM_TILES[n]
                src = norm_source(n)
                for t in range(nt):
                    wait_tile(act, n, t)
                    if n in (2, 4) and t == 0:
                        act.wait_ge(sem("mixT_full"), KD * (n // 2))
                    act.activation(XN[:, t, :], src[:, t, :], ACT.Square, accum_out=stat[:, t:t + 1])\
                        .then_inc(sem("squares"), 1)
                act.wait_ge(sem("var"), n + 1)
                act.activation(stat[:, 8:8 + nt], stat[:, 4:4 + nt], ACT.Sqrt).then_inc(sem("root"), 1)

            def norm_turned(n):
                width = NORM_TILES[n] * P
                for k in range(0, KD, 2):
                    act.wait_ge(sem("tok_T"), KD * n + k + 1)
                    if k == 0:
                        act.wait_ge(sem("small_in"), 16 * 12)
                    act.activation(ht_of(n)[:, k, :], bank(0)[:, 0:width], ACT.Copy, scale=GN[:, n, k:k + 1])\
                        .then_inc(sem("hT_act"), 1)

            def cross_attention(l):
                XP, XPT = (XP0, XPT0) if l == 0 else (XP1, XPT1)
                for h in range(XHEADS):
                    act.wait_ge(sem("x_max"), 2 * XHEADS * l + 2 * h + 2)
                    if h >= 1:
                        act.wait_ge(sem("xp_T"), MT * XHEADS * l + MT * h)
                    if l == 0 and h == 0:
                        act.wait_ge(sem("rope_done"), 1)
                    for t in range(NT):
                        s = bank(2 * (h % 2) + t // 2)[:, (t % 2) * M:(t % 2 + 1) * M]
                        act.activation(XP[:, t, :], s, ACT.Exp, bias=stat[:, 16 + t:17 + t],
                                       accum_out=stat[:, 20 + t:21 + t]).then_inc(sem("x_exp"), 1)
                    for c in range(MT):
                        act.wait_ge(sem("xp_T"), MT * XHEADS * l + MT * h + c + 1)
                        if h >= 1:
                            act.wait_ge(sem("xo_full"), XHEADS * l + h)
                        act.activation(XPT[:, c, :], bank(4 + c), ACT.Copy).then_inc(sem("xpt_ready"), 1)

            def mix_turned(l):
                for k in range(0, KD, 2):
                    act.wait_ge(sem("mixT_full"), KD * l + k + 1)
                    act.activation(hT[:, k, :], bank(0), ACT.Copy).then_inc(sem("mixT_act"), 1)

            def head_nope(s, h):
                act.wait_ge(sem("qk_full"), h + 1)
                wait(act, "scores_full", 3 * h)
                act.activation(qT[s][0:NOPE, :], bank(4)[0:NOPE, :], ACT.Copy).then_inc(sem("q_nope"), 1)
                act.activation(kT[s][0:NOPE, :], bank(5)[0:NOPE, :], ACT.Copy).then_inc(sem("k_nope"), 1)

            SLOT_OF = [(1, 0, 0), (2, 0, 128), (1, 128, 384), (0, 0, 768)]

            def head_exp(h):
                for t in range(NT):
                    b, at, to = SLOT_OF[t]
                    n = (t + 1) * P
                    act.wait_ge(sem("row_max"), 4 * h + (2, 3, 2, 4)[t])
                    wait(act, "p_T", 4 * h)
                    act.activation(PR[:, to:to + n], bank(b)[:, at:at + n], ACT.Exp, bias=stat[:, 16 + t:17 + t],
                                   accum_out=stat[:, 20 + t:21 + t]).then_inc(sem("probs"), 1)

            def head_pt(h):
                for j, t in enumerate((1, 3)):
                    act.wait_ge(sem("p_T"), 4 * h + t + 1)
                    wait(act, "o_done", 4 * h + t - 1)
                    act.activation(PT[:, 1, 0:(t + 1) * P], bank(7)[:, 0:(t + 1) * P], ACT.Copy)\
                        .then_inc(sem("pt_act"), 1)

            norm_squares(0)
            norm_turned(0)
            act.wait_ge(sem("mk_full"), 1)
            act.activation(MK[:, 0, :], bank(2)[:, 0:M], ACT.Copy).then_inc(sem("mem_ready"), 1)
            act.wait_ge(sem("mk_full"), 2)
            act.activation(MK[:, 1, :], bank(3)[:, 0:M], ACT.Copy).then_inc(sem("mem_ready"), 1)
            act.wait_ge(sem("rang_ready"), 1)
            act.activation(trig, rang, ACT.Sin).then_inc(sem("trig_ready"), 1)
            norm_squares(1)
            norm_turned(1)
            for t in range(NT):
                act.wait_ge(sem("z_full"), 2 * t + 1)
                act.activation(ZS[:, t, 0:ZA], bank(2 + 2 * (t % 2))[:, 0:ZA], ACT.Copy).then_inc(sem("z_key"), 1)
            for t in range(NT):
                act.wait_ge(sem("z_key"), t + 1)
                act.activation(PR[:, 0:QR], ZS[:, t, 0:QR], ACT.Square, accum_out=stat[:, 24 + t:25 + t])\
                    .then_inc(sem("lat_squares"), 1)
                act.wait_ge(sem("lat_squares"), 2 * t + 1)
                act.activation(PR[:, 0:KVR], ZS[:, t, QR:QR + KVR], ACT.Square, accum_out=stat[:, 28 + t:29 + t])\
                    .then_inc(sem("lat_squares"), 1)
                act.wait_ge(sem("lat_squares"), 2 * t + 2)
            act.wait_ge(sem("lat_var"), 2)
            act.activation(stat[:, 32:40], stat[:, 24:32], ACT.Sqrt).then_inc(sem("lat_root"), 1)
            for k in range(KQ):
                act.wait_ge(sem("lat_T"), k + 1)
                act.activation(QLT[:, k, :], bank(k), ACT.Copy, scale=gq[:, k:k + 1]).then_inc(sem("lat_ready"), 1)
            act.wait_ge(sem("lat_T"), 3)
            act.activation(KVT, bank(2), ACT.Copy, scale=gkv[:, 0:1]).then_inc(sem("lat_ready"), 1)
            for t in range(NT):
                act.wait_ge(sem("v_full"), 2 * t + 1)
                act.activation(V[:, t, 0:MW // 2], bank(0)[:, 0:MW // 2], ACT.Copy).then_inc(sem("v_act"), 1)
            cross_attention(0)
            act.wait_ge(sem("xpt_ready"), MT * XHEADS)
            act.wait_ge(sem("xo_full"), XHEADS)
            head_nope(0, 0)
            head_exp(0)
            head_nope(1, 1)
            head_pt(0)
            with act.Fori(0, H // 2 - 1) as i:
                for s in (1, 0):
                    h = act.snap(2 * i + (2 - s))
                    head_exp(h)
                    head_nope(1 - s, act.snap(2 * i + (3 - s)))
                    head_pt(h)
            head_exp(H - 1)
            head_pt(H - 1)
            mix_turned(0)

            def experts(l):

                def gate(u, e):
                    b = u % 2
                    act.wait_ge(sem(f"gu_full{l}"), e + 1)
                    wait(act, f"a_ready{l}", e - 1)
                    act.activation(SG[0:SLOTS, b, :], bank(2 + b)[0:SLOTS, 0:FE], ACT.Silu)\
                        .then_inc(sem(f"sg_ready{l}"), 1)

                def hidden_T(u, e):
                    b = u % 2
                    act.wait_ge(sem(f"at_full{l}"), e + 1)
                    wait(act, f"y_full_{l}", e - 1)
                    act.activation(AT[:, b, :], bank(4 + b)[:, 0:KF * SLOTS], ACT.Copy).then_inc(sem(f"at_ready{l}"), 1)

                def rows_out(u, e, turn):
                    b = u % 2
                    act.wait_ge(sem(f"y_full_{l}"), e + 1)
                    wait(act, f"scattered{l}_{b}", 16 * turn)
                    act.activation(YS[0:SLOTS, b, 0:D // 2], bank(6)[0:SLOTS, :], ACT.Copy).then_inc(sem(f"ys_act{l}"), 1)

                def step(u, e, turn, before):
                    gate(u, e)
                    if before is not None:
                        rows_out(u - 1, before, turn)
                    hidden_T(u, e)

                for e in range(RING):
                    step(e, e, (e - 1) // 2, e - 1 if e else None)
                with act.Fori(0, E // RING - 2) as i:
                    for u in range(RING):
                        step(u + RING, act.snap(RING * i + (RING + u)), act.snap(2 * i + (RING + u - 1) // 2),
                             act.snap(RING * i + (RING + u - 1)))
                for e in range(E - RING, E):
                    step(e, e, (e - 1) // 2, e - 1)
                rows_out(E - 1, E - 1, (E - 1) // 2)
                act.wait_ge(sem("extra_ready"), l + 1)
                rounds = act.value_load(extra[0:1, 0:1], min_val=0, max_val=ROUNDS - 1)
                with act.If(rounds > 0):
                    with act.Fori(0, rounds) as r:
                        with act.Fori(0, E // RING) as q:
                            for u in range(RING):
                                e = act.snap(E * r + RING * q + (E + u))
                                gate(u, e)
                                hidden_T(u, e)
                                rows_out(u, e, act.snap(E // 2 * r + 2 * q + (E + u) // 2))

            def router(l):
                act.wait_ge(sem("group_logits"), l + 1)
                act.activation(EG, LS, ACT.Exp).then_inc(sem("group_exp"), 1)
                act.wait_ge(sem("second"), l + 1)
                act.activation(small[:, 4:8], small[:, 0:4], ACT.Exp).then_inc(sem("second_exp"), 1)

            norm_squares(2)
            norm_turned(2)
            router(0)
            experts(0)
            norm_squares(3)
            norm_turned(3)
            for t in range(NT):
                act.wait_ge(sem("zp_full"), 2 * t + 1)
                act.activation(U[:, t, 0:512], bank(2 + 2 * (t % 2)), ACT.Copy).then_inc(sem("u_act"), 1)
            act.wait_ge(sem("qcT_full1"), 1)
            act.activation(QCT1[:, 0, :], bank(0), ACT.Copy).then_inc(sem("qct_act"), 1)
            for j in range(0, 2 * len(WINDOWS), 2):
                act.wait_ge(sem("d_full"), j + 1)
                act.activation(dT[0:HW, j, :], bank(6)[0:HW, :], ACT.Copy, scale=1.0 / WINDOWS[j // 2])\
                    .then_inc(sem("d_act"), 1)
            cross_attention(1)
            mix_turned(1)
            norm_squares(4)
            norm_turned(4)
            router(1)
            experts(1)
            norm_squares(5)

        @block.vector
        def _(dve):
            steps = [0]

            def link(ins):
                steps[0] += 1
                ins.then_inc(sem("dve_step"), 1)
                dve.wait_ge(sem("dve_step"), steps[0])

            def norm_scale(n):
                nt = NORM_TILES[n]
                src = norm_source(n)
                dve.wait_ge(sem("squares"), TILES[n] + nt)
                dve.tensor_scalar(stat[:, 4:4 + nt], stat[:, 0:nt], 1.0 / D, EPS, ALU.mult, ALU.add)\
                    .then_inc(sem("var"), 1)
                dve.wait_ge(sem("root"), n + 1)
                link(dve.reciprocal(stat[:, 12:12 + nt], stat[:, 8:8 + nt]))
                if n == 5:
                    dve.wait_ge(sem("gfin_in"), 16)
                for t in range(nt):
                    if n == 5:
                        dve.scalar_tensor_tensor(out=XN[:, t, :], in0=X[:, t, :], scalar=stat[:, 12 + t:13 + t],
                                                 in1=gfin, op0=ALU.mult, op1=ALU.mult).then_inc(sem("fin"), 1)
                    else:
                        dve.tensor_scalar(XN[:, t, :], src[:, t, :], stat[:, 12 + t:13 + t], None, ALU.mult)\
                            .then_inc(sem("xn"), 1)

            def norm_turned(n):
                width = NORM_TILES[n] * P
                for k in range(1, KD, 2):
                    dve.wait_ge(sem("tok_T"), KD * n + k + 1)
                    if k == 1:
                        dve.wait_ge(sem("small_in"), 16 * 12)
                    dve.tensor_scalar(ht_of(n)[:, k, :], bank(1)[:, 0:width], GN[:, n, k:k + 1], None, ALU.mult)\
                        .then_inc(sem("hT_dve"), 1)

            def cross_attention(l):
                for h in range(XHEADS):
                    for j in range(2):
                        dve.wait_ge(sem("xs_full"), 2 * XHEADS * l + 2 * h + j + 1)
                        if h >= 1 and j == 0:
                            dve.wait_ge(sem("x_exp"), NT * XHEADS * l + NT * h)
                        b = bank(2 * (h % 2) + j, 2, M)
                        dve.tensor_reduce(stat[:, 16 + 2 * j:18 + 2 * j], b, AX.X, ALU.max, negate=True)\
                            .then_inc(sem("x_max"), 1)
                    if h >= 1:
                        xo(l, h - 1)
                    dve.wait_ge(sem("x_exp"), NT * XHEADS * l + NT * (h + 1))
                    link(dve.reciprocal(stat[:, 40 + 4 * (h % 2):44 + 4 * (h % 2)], stat[:, 20:24]))
                xo(l, XHEADS - 1)

            def xo(l, h):
                dve.wait_ge(sem("xo_full"), XHEADS * l + h + 1)
                o = bank(6 + h % 2, NT, XD)
                r = stat[:, 40 + 4 * (h % 2):44 + 4 * (h % 2)].rearrange("p (t a) -> p t a", a=1)
                dve.tensor_tensor(XN[:, :, MW + h * XD:MW + (h + 1) * XD], o, wide(r, P, NT, XD), ALU.mult)\
                    .then_inc(sem("xmix"), 1)

            def mix_turned(l):
                for k in range(1, KD, 2):
                    dve.wait_ge(sem("mixT_full"), KD * l + k + 1)
                    dve.tensor_copy(hT[:, k, :], bank(1)).then_inc(sem("mixT_dve"), 1)

            def residual(l):
                for t in range(NT):
                    for j in range(2):
                        dve.wait_ge(sem("o_full"), 2 * NT * l + 2 * t + j + 1)
                        part = X[:, t, j * 512:(j + 1) * 512]
                        dve.tensor_tensor(part, bank(2 + (2 * t + j) % 4), part, ALU.add).then_inc(sem("o_added"), 1)

            def router(l):
                dve.wait_ge(sem("router_full"), l + 1)
                if l == 0:
                    dve.wait_ge(sem("constants"), 4)
                logits = bank(6, NT, NR)
                b = bias_r[:, l, :].rearrange("p (a n) -> p a n", a=1)
                link(dve.tensor_tensor(LG, logits, wide(b, P, NT, NR), ALU.add))

                def col(at, n=1):
                    return small[:, at:at + NT].rearrange("p (t a) -> p t a", a=1)

                def first_of(best_of, n, out_):
                    w = tie[:, 0:n].rearrange("p (a n) -> p a n", a=1)
                    link(dve.scalar_tensor_tensor(out=SC[:, :, 0:n], in0=best_of, scalar=0.0, in1=wide(w, P, NT, n),
                                                  op0=ALU.is_equal, op1=ALU.mult))
                    link(dve.tensor_reduce(small[:, 16:20], SC[:, :, 0:n], AX.X, ALU.max))
                    link(dve.tensor_tensor(out_, SC[:, :, 0:n], wide(col(16), P, NT, n), ALU.is_equal))

                link(dve.tensor_reduce(small[:, 8:12], LG[:, :, 0:GROUPS], AX.X, ALU.max))
                dve.tensor_tensor(LS, LG[:, :, 0:GROUPS], wide(col(8), P, NT, GROUPS), ALU.subtract)\
                    .then_inc(sem("group_logits"), 1)
                dve.wait_ge(sem("group_logits"), l + 1)
                first_of(LS, GROUPS, OG)

                def by_group(ap):
                    return ap.rearrange("p t (g j) -> p (t g) j", g=GROUPS)

                def og():
                    return OG.rearrange("p t (g a) -> p (t g) a", a=1)

                link(dve.tensor_copy(LE, LG[:, :, GROUPS:]))
                link(dve.tensor_tensor(by_group(LE), by_group(LE), wide(og(), P, NT * GROUPS, PER_GROUP), ALU.mult))
                link(dve.tensor_reduce(SEL, LE.rearrange("p t (g j) -> p t j g", g=GROUPS), AX.X, ALU.add))
                link(dve.tensor_reduce(small[:, 8:12], SEL, AX.X, ALU.max))
                link(dve.tensor_tensor(SEL, SEL, wide(col(8), P, NT, PER_GROUP), ALU.subtract))
                first_of(SEL, PER_GROUP, O1)
                link(dve.scalar_tensor_tensor(out=SEL, in0=O1, scalar=NEG_INF, in1=SEL, op0=ALU.mult, op1=ALU.add))
                dve.tensor_reduce(small[:, 0:4], SEL, AX.X, ALU.max).then_inc(sem("second"), 1)
                dve.wait_ge(sem("second"), l + 1)
                link(dve.tensor_tensor(SEL, SEL, wide(col(0), P, NT, PER_GROUP), ALU.subtract))
                first_of(SEL, PER_GROUP, O2)
                for o, a in ((O1, A1), (O2, A2)):
                    for t in range(NT):
                        g = OG[:, t, :].rearrange("p (g a) -> p g a", a=1)
                        j = o[:, t, :].rearrange("p (a j) -> p a j", a=1)
                        ins = dve.tensor_tensor(a[:, t, :].rearrange("p (g j) -> p g j", g=GROUPS),
                                                wide(g, P, GROUPS, PER_GROUP), wide(j, P, GROUPS, PER_GROUP), ALU.mult)
                        link(ins)
                dve.tensor_tensor(AB, A1, A2, ALU.add).then_inc(sem("assigned"), 1)
                dve.wait_ge(sem("group_exp"), l + 1)
                link(dve.tensor_reduce(small[:, 12:16], EG, AX.X, ALU.add))
                dve.wait_ge(sem("second_exp"), l + 1)
                link(dve.scalar_tensor_tensor(out=small[:, 20:24], in0=small[:, 4:8], scalar=1.0, in1=small[:, 12:16],
                                              op0=ALU.add, op1=ALU.mult))
                link(dve.reciprocal(wtok[:, 0, :], small[:, 20:24]))
                link(dve.tensor_tensor(wtok[:, 1, :], wtok[:, 0, :], small[:, 4:8], ALU.mult))
                dve.wait_ge(sem("ranks_full"), l + 1)
                ie = iota_e[:, :].rearrange("p (a e) -> p a e", a=1)
                link(dve.scalar_tensor_tensor(out=POS, in0=bank(7, NT, E), scalar=float(E), in1=wide(ie, P, NT, E),
                                              op0=ALU.mult, op1=ALU.add))
                for j, a in enumerate((A1, A2)):
                    link(dve.tensor_tensor(PM, POS, a, ALU.mult))
                    with nc.allow_low_precision(reason="small whole numbers"):
                        dve.tensor_reduce(slot_pos[:, j * NT:(j + 1) * NT], PM, AX.X, ALU.add)\
                            .then_inc(sem("slot_pos_ready"), 1)
                    dve.wait_ge(sem("slot_pos_ready"), 2 * l + j + 1)
                link(dve.tensor_reduce(small[:, 24:25], banks[7][:, NT * E:(NT + 1) * E], AX.X, ALU.max))
                link(dve.tensor_scalar(small[:, 32:32 + ROUNDS - 1], thresh[:, :], small[:, 24:25], None, ALU.is_lt))
                with nc.allow_low_precision(reason="small whole numbers"):
                    dve.tensor_reduce(extra[:, 0:1], small[:, 32:32 + ROUNDS - 1], AX.X, ALU.add)\
                        .then_inc(sem("extra_ready"), 1)
                dve.wait_ge(sem("sidx_in"), 16 * (l + 1))
                link(dve.tensor_scalar(CF[0:SLOTS, :], SIDX[0:SLOTS, :], float(S), -float(S), ALU.is_ge, ALU.mult))
                dve.tensor_tensor(GIDX[0:SLOTS, :], SIDX[0:SLOTS, :], CF[0:SLOTS, :], ALU.add)\
                    .then_inc(sem("gidx_ready"), 1)

            def experts(l):

                def rows_T(u, e):
                    b = u % 2
                    dve.wait_ge(sem(f"xg_full{l}"), e + 1)
                    wait(dve, f"gu_full{l}", e - 1)
                    g = GN[:, 2 * l + 2, :].rearrange("p (k a) -> p k a", a=1)
                    dve.tensor_tensor(XGT[:, b, :].rearrange("p (k s) -> p k s", k=KD), bank(b, KD, SLOTS),
                                      wide(g, P, KD, SLOTS), ALU.mult).then_inc(sem(f"xgt_ready{l}"), 1)

                def hidden(u, e):
                    b = u % 2
                    dve.wait_ge(sem(f"sg_ready{l}"), e + 1)
                    wait(dve, f"at_full{l}", e - 1)
                    dve.tensor_tensor(AE[0:SLOTS, b, :], bank(2 + b)[0:SLOTS, FE:2 * FE], SG[0:SLOTS, b, :], ALU.mult)\
                        .then_inc(sem(f"a_ready{l}"), 1)

                def rows_out(u, e, turn):
                    b = u % 2
                    dve.wait_ge(sem(f"y_full_{l}"), e + 1)
                    wait(dve, f"scattered{l}_{b}", 16 * turn)
                    dve.tensor_copy(YS[0:SLOTS, b, D // 2:], bank(7)[0:SLOTS, :]).then_inc(sem(f"ys_dve{l}"), 1)

                def step(u, e, turn, before, after):
                    hidden(u, e)
                    if after is not None:
                        rows_T(u + 1, after)
                    if before is not None:
                        rows_out(u - 1, before, turn)

                rows_T(0, 0)
                for e in range(RING):
                    step(e, e, (e - 1) // 2, e - 1 if e else None, e + 1)
                with dve.Fori(0, E // RING - 2) as i:
                    for u in range(RING):
                        step(u + RING, dve.snap(RING * i + (RING + u)), dve.snap(2 * i + (RING + u - 1) // 2),
                             dve.snap(RING * i + (RING + u - 1)), dve.snap(RING * i + (RING + u + 1)))
                for e in range(E - RING, E):
                    step(e, e, (e - 1) // 2, e - 1, e + 1 if e + 1 < E else None)
                rows_out(E - 1, E - 1, (E - 1) // 2)
                dve.wait_ge(sem("extra_ready"), l + 1)
                rounds = dve.value_load(extra[0:1, 0:1], min_val=0, max_val=ROUNDS - 1)
                with dve.If(rounds > 0):
                    with dve.Fori(0, rounds) as r:
                        with dve.Fori(0, E // RING) as q:
                            for u in range(RING):
                                e = dve.snap(E * r + RING * q + (E + u))
                                rows_T(u, e)
                                hidden(u, e)
                                rows_out(u, e, dve.snap(E // 2 * r + 2 * q + (E + u) // 2))
                for t in range(NT):
                    dve.wait_ge(sem(f"yl_in_{t % 2}"), 64 * l + 32 * (t // 2 + 1))
                    for j in range(2):
                        ins = dve.scalar_tensor_tensor(
                            out=X[:, t, :], in0=YL[:, t % 2, j * D:(j + 1) * D], scalar=wtok[:, j, t:t + 1],
                            in1=X[:, t, :], op0=ALU.mult, op1=ALU.add)
                        if j == 0:
                            link(ins)
                    ins.then_inc(sem("x_moe"), 1)

            def rope(src, dst, scratch):
                lo, hi = slice(NOPE, QKD), slice(QKD, P)
                a = scratch
                return (dve.tensor_tensor(a[lo, :], src[hi, :], TBL[hi, :], ALU.mult),
                        dve.tensor_tensor(dst[lo, :], src[lo, :], TBL[lo, :], ALU.mult))

            norm_scale(0)
            norm_turned(0)
            for c in range(MT):
                dve.wait_ge(sem("mv_full"), c + 1)
                dve.tensor_copy(MV[:, c, :], bank(4 + c)[:, 0:XW]).then_inc(sem("mv_ready"), 1)
            two_pi = 2 * np.pi
            c1 = 6.28125
            c2 = float(np.float32(np.round((two_pi - c1) * 2 ** 21) / 2 ** 21))
            c3 = float(np.float32(two_pi - c1 - c2))
            MAGIC = 1.5 * 2 ** 23
            dve.wait_ge(sem("small_in"), 16 * 12)
            dve.wait_ge(sem("constants"), 2)
            link(dve.tensor_copy(posf, posi))
            p3 = posf.rearrange("p (t a) -> p t a", a=1)
            f3 = freq.rearrange("p (a i) -> p a i", a=1)
            link(dve.tensor_tensor(ang, wide(p3, P, NT, HALF), wide(f3, P, NT, HALF), ALU.mult))
            flat = ang.rearrange("p t i -> p (t i)")
            for j, shift in ((0, 0.25), (1, 0.0)):
                link(dve.tensor_scalar(turns[:, j, :], flat, float(np.float32(1 / two_pi)), shift, ALU.mult, ALU.add))
                link(dve.tensor_scalar(turns[:, j, :], turns[:, j, :], MAGIC, None, ALU.add))
                link(dve.tensor_scalar(turns[:, j, :], turns[:, j, :], MAGIC, None, ALU.subtract))
                link(dve.scalar_tensor_tensor(out=rang[:, j, :], in0=turns[:, j, :], scalar=-c1, in1=flat,
                                              op0=ALU.mult, op1=ALU.add))
                link(dve.scalar_tensor_tensor(out=rang[:, j, :], in0=turns[:, j, :], scalar=-c2, in1=rang[:, j, :],
                                              op0=ALU.mult, op1=ALU.add))
                link(dve.scalar_tensor_tensor(out=rang[:, j, :], in0=turns[:, j, :], scalar=-c3, in1=rang[:, j, :],
                                              op0=ALU.mult, op1=ALU.add))
                if j == 0:
                    link(dve.tensor_scalar(rang[:, j, :], rang[:, j, :], float(np.float32(np.pi / 2)), None, ALU.add))
            lim = float(np.nextafter(np.float32(np.pi), np.float32(0)))
            dve.tensor_scalar(rang, rang, lim, -lim, ALU.min, ALU.max).then_inc(sem("rang_ready"), 1)
            dve.wait_ge(sem("trig_ready"), 1)
            dve.wait_ge(sem("constants"), 3)
            cos = trig[:, 0, :].rearrange("p (t i) -> p t i", t=NT)
            sin = trig[:, 1, :].rearrange("p (t i) -> p t i", t=NT)
            for at, src, s in ((NOPE, cos, 1.0), (NOPE + HALF, cos, 1.0), (QKD, sin, -1.0), (QKD + HALF, sin, 1.0)):
                dve.tensor_scalar(tbl_tok[:, :, at:at + HALF], src, s, None, ALU.mult).then_inc(sem("tbl_ready"), 1)
            norm_scale(1)
            norm_turned(1)
            for t in range(NT):
                dve.wait_ge(sem("z_full"), 2 * t + 2)
                dve.tensor_scalar(ZS[:, t, ZA:ZW], bank(3 + 2 * (t % 2))[:, 0:XW], XSCALE, None, ALU.mult)\
                    .then_inc(sem("z_xq"), 1)
            dve.wait_ge(sem("tblT_full"), 1)
            link(dve.tensor_copy(TBL[NOPE:P, :], bank(7)[NOPE:P, :]))
            dve.wait_ge(sem("lat_squares"), 2 * NT)
            dve.tensor_scalar(stat[:, 24:28], stat[:, 24:28], 1.0 / QR, EPS, ALU.mult, ALU.add).then_inc(sem("lat_var"), 1)
            dve.tensor_scalar(stat[:, 28:32], stat[:, 28:32], 1.0 / KVR, EPS, ALU.mult, ALU.add).then_inc(sem("lat_var"), 1)
            dve.wait_ge(sem("lat_root"), 1)
            link(dve.reciprocal(stat[:, 40:48], stat[:, 32:40]))
            link(dve.tensor_scalar(stat[:, 40:44], stat[:, 40:44], QSCALE, None, ALU.mult))
            for t in range(NT):
                for a, b, c in ((0, QR, 40), (QR, QR + KVR, 44)):
                    dve.tensor_scalar(ZS[:, t, a:b], ZS[:, t, a:b], stat[:, c + t:c + t + 1], None, ALU.mult)\
                        .then_inc(sem("lat_normed"), 1)
            for m in range(2):
                dve.wait_ge(sem("lat_T"), 4 + m)
                dve.tensor_copy(QCT0[:, m, :], bank(3 + m)).then_inc(sem("qct0"), 1)
            dve.wait_ge(sem("lat_T"), 6)
            for s in range(2):
                for ins in rope(bank(5), kT[s], qT[s]):
                    link(ins)
                ins = dve.tensor_tensor(kT[s][NOPE:QKD, :], kT[s][NOPE:QKD, :], qT[s][NOPE:QKD, :], ALU.add)
                if s == 0:
                    link(ins)
                else:
                    ins.then_inc(sem("rope_done"), 1)
            for t in range(NT):
                dve.wait_ge(sem("v_full"), 2 * t + 2)
                dve.tensor_copy(V[:, t, MW // 2:], bank(1)[:, 0:MW // 2]).then_inc(sem("v_dve"), 1)
            cross_attention(0)

            def head_rope(s, h):
                dve.wait_ge(sem("qk_full"), h + 1)
                wait(dve, "scores_full", 3 * h)
                for ins in rope(bank(4), qT[s], rope_scratch):
                    ins.then_inc(sem("q_rot"), 1)
                dve.wait_ge(sem("q_rot"), 2 * h + 2)
                dve.tensor_tensor(qT[s][NOPE:QKD, :], qT[s][NOPE:QKD, :], rope_scratch[NOPE:QKD, :], ALU.add)\
                    .then_inc(sem("q_rope"), 1)

            SLOT_OF = [(1, 0, 1), (2, 0, 2), (1, 128, 1), (0, 0, 3)]

            def head_max(h):
                wait(dve, "probs", 4 * h)
                for t in (0, 2, 1, 3):
                    b, at, n_full = SLOT_OF[t]
                    dve.wait_ge(sem("scores_full"), 3 * h + n_full)
                    dve.tensor_reduce(stat[:, 16 + t:17 + t], bank(b)[:, at:at + (t + 1) * P], AX.X, ALU.max,
                                      negate=True).then_inc(sem("row_max"), 1)

            def head_pt(h):
                for t in (0, 2):
                    dve.wait_ge(sem("p_T"), 4 * h + t + 1)
                    if t == 2:
                        dve.wait_ge(sem("o_done"), 4 * h + 1)
                    dve.tensor_copy(PT[:, 0, 0:(t + 1) * P], bank(6)[:, 0:(t + 1) * P]).then_inc(sem("pt_dve"), 1)

            def head_out(h, col):
                dve.wait_ge(sem("probs"), 4 * h + 4)
                dve.reciprocal(stat[:, 40:44], stat[:, 20:24]).then_inc(sem("inv_sum"), 1)
                dve.wait_ge(sem("inv_sum"), h + 1)
                dve.wait_ge(sem("o_done"), 4 * h + 4)
                r = stat[:, 40:44].rearrange("p (t a) -> p t a", a=1)
                dve.tensor_tensor(XN[:, :, bass.ds(col, VD)], bank(3, NT, VD), wide(r, P, NT, VD), ALU.mult)\
                    .then_inc(sem("mixed"), 1)

            rope_scratch = view(WIN, 0, S)
            head_rope(0, 0)
            head_max(0)
            head_rope(1, 1)
            head_pt(0)
            head_out(0, 0)
            with dve.Fori(0, H // 2 - 1) as i:
                for s in (1, 0):
                    h = dve.snap(2 * i + (2 - s))
                    head_max(h)
                    head_rope(1 - s, dve.snap(2 * i + (3 - s)))
                    head_pt(h)
                    head_out(h, dve.snap(2 * VD * i + (2 - s) * VD))
            head_max(H - 1)
            head_pt(H - 1)
            head_out(H - 1, (H - 1) * VD)
            mix_turned(0)
            residual(0)
            norm_scale(2)
            norm_turned(2)
            router(0)
            experts(0)
            norm_scale(3)
            norm_turned(3)
            for t in range(NT):
                b = bank(3 + 2 * (t % 2))
                dve.wait_ge(sem("zp_full"), 2 * t + 2)
                dve.tensor_copy(U[:, t, 512:MW], b[:, 0:MW - 512]).then_inc(sem("u_dve"), 1)
                dve.tensor_scalar(QC[:, t, :], b[:, MW - 512:512], XSCALE, None, ALU.mult).then_inc(sem("u_dve"), 1)
            dve.wait_ge(sem("qcT_full1"), 2)
            dve.tensor_copy(QCT1[:, 1, :], bank(1)).then_inc(sem("qct_dve"), 1)
            dve.wait_ge(sem("band_sums"), 1)
            link(dve.reciprocal(ramp, ramp))
            for g, w in enumerate(WINDOWS):
                dve.scalar_tensor_tensor(out=band0[:, g, :], in0=ramp[:, g, :], scalar=float(w), in1=band0[:, g, :],
                                         op0=ALU.mult, op1=ALU.mult).then_inc(sem("band_scaled"), 1)
            dve.wait_ge(sem("band_scaled"), len(WINDOWS))
            for g, w in enumerate(WINDOWS):
                for m, n in ((band, P), (band0, 16)):
                    dve.scalar_tensor_tensor(out=m[:, g, 0:n], in0=ident[:, 0:n], scalar=-float(w), in1=m[:, g, 0:n],
                                             op0=ALU.mult, op1=ALU.add).then_inc(sem("bands_ready"), 1)
            for j in range(1, 2 * len(WINDOWS), 2):
                dve.wait_ge(sem("d_full"), j + 1)
                dve.tensor_scalar(dT[0:HW, j, :], bank(7)[0:HW, :], 1.0 / WINDOWS[j // 2], None, ALU.mult)\
                    .then_inc(sem("d_dve"), 1)
            dve.wait_ge(sem("w_mix_in"), 32)
            for t in range(NT):
                for j in range(2):
                    dve.wait_ge(sem("y_pool"), 2 * t + j + 1)
                    c = slice(j * MW // 2, (j + 1) * MW // 2)
                    dve.tensor_tensor(XN[:, t, c], bank(2 + 2 * (t % 2) + j)[:, 0:MW // 2], scale_b[:, c], ALU.mult)\
                        .then_inc(sem("pool_mixed"), 1)
            cross_attention(1)
            mix_turned(1)
            residual(1)
            norm_scale(4)
            norm_turned(4)
            router(1)
            experts(1)
            norm_scale(5)

        @block.tensor
        def _(pe):
            def norm_turned(n):
                for k in range(KD):
                    if k >= 2:
                        pe.wait_ge(sem("hT_act" if k % 2 == 0 else "hT_dve"), KD // 2 * n + k // 2)
                    for t in range(NORM_TILES[n]):
                        if k == 0:
                            pe.wait_ge(sem("xn"), TILES[n] + t + 1)
                        ins = pe.transpose(bank(k % 2)[:, t * P:(t + 1) * P], XN[:, t, k:D:KD], ident[:, :])
                    ins.then_inc(sem("tok_T"), 1)

            def wait_turned(n, k):
                pe.wait_ge(sem("hT_act" if k % 2 == 0 else "hT_dve"), KD // 2 * n + k // 2 + 1)

            def project(n, w, splits, banks_of, full, free):
                for t in range(NT):
                    for j, (a, b) in enumerate(splits):
                        free(t, j)
                        for k in range(KD):
                            if t == 0 and j == 0:
                                wait_turned(n, k)
                            ins = pe.matmul(bank(banks_of(t, j))[:, 0:b - a], hT[:, k, t * P:(t + 1) * P],
                                            w[:, k, a:b], start=(k == 0), stop=(k == KD - 1))
                        ins.then_inc(sem(full), 1)

            def cross_attention(l):
                QCT = QCT0 if l == 0 else QCT1
                XP, XPT = (XP0, XPT0) if l == 0 else (XP1, XPT1)

                def scores(h):
                    at = slice((h % 2) * XD, (h % 2 + 1) * XD)
                    if h >= 2:
                        pe.wait_ge(sem("x_exp"), NT * XHEADS * l + NT * (h - 1))
                    for t in range(NT):
                        ins = pe.matmul(bank(2 * (h % 2) + t // 2)[:, (t % 2) * M:(t % 2 + 1) * M],
                                        QCT[at, h // 2, t * P:(t + 1) * P], MK[at, h // 2, :], start=True, stop=True)
                        if t % 2:
                            ins.then_inc(sem("xs_full"), 1)

                scores(0)
                for h in range(XHEADS):
                    if h + 1 < XHEADS:
                        scores(h + 1)
                    pe.wait_ge(sem("x_exp"), NT * XHEADS * l + NT * (h + 1))
                    for c in range(MT):
                        if h >= 1:
                            pe.wait_ge(sem("xpt_ready"), MT * XHEADS * l + MT * (h - 1) + c + 1)
                        for t in range(NT):
                            ins = pe.transpose(bank(4 + c)[:, t * P:(t + 1) * P], XP[:, t, c * P:(c + 1) * P], ident[:, :])
                        ins.then_inc(sem("xp_T"), 1)
                    pe.wait_ge(sem("xpt_ready"), MT * XHEADS * l + MT * (h + 1))
                    if h >= 2:
                        pe.wait_ge(sem("xmix"), XHEADS * l + h - 1)
                    for t in range(NT):
                        for c in range(MT):
                            ins = pe.matmul(bank(6 + h % 2)[:, t * XD:(t + 1) * XD], XPT[:, c, t * P:(t + 1) * P],
                                            MV[:, c, h * XD:(h + 1) * XD], start=(c == 0), stop=(c == MT - 1))
                    ins.then_inc(sem("xo_full"), 1)

            def output_projection(l):
                pe.wait_ge(sem("xmix"), XHEADS * l + XHEADS)
                for k in range(KD):
                    if k >= 2:
                        pe.wait_ge(sem("mixT_act" if k % 2 == 0 else "mixT_dve"), KD // 2 * l + k // 2)
                    for t in range(NT):
                        ins = pe.transpose(bank(k % 2)[:, t * P:(t + 1) * P], XN[:, t, k:D:KD], ident[:, :])
                    ins.then_inc(sem("mixT_full"), 1)
                pe.wait_ge(sem("w_out_in"), 16 * (l + 1))
                for t in range(NT):
                    for j in range(2):
                        n = 2 * t + j
                        if n >= 4:
                            pe.wait_ge(sem("o_added"), 2 * NT * l + n - 3)
                        for k in range(KD):
                            if n == 0:
                                pe.wait_ge(sem("mixT_act" if k % 2 == 0 else "mixT_dve"), KD // 2 * l + k // 2 + 1)
                            ins = pe.matmul(bank(2 + n % 4), hT[:, k, t * P:(t + 1) * P],
                                            w_out[:, k, j * 512:(j + 1) * 512], start=(k == 0), stop=(k == KD - 1))
                        ins.then_inc(sem("o_full"), 1)

            def router(l):
                pe.wait_ge(sem("wr_in"), 32 * (l + 1))
                for t in range(NT):
                    for k in range(KD):
                        if t == 0:
                            wait_turned(2 * l + 2, k)
                        ins = pe.matmul(bank(6)[:, t * NR:(t + 1) * NR], hT[:, k, t * P:(t + 1) * P], WR[:, k, :],
                                        start=(k == 0), stop=(k == KD - 1))
                ins.then_inc(sem("router_full"), 1)
                pe.wait_ge(sem("assigned"), l + 1)
                for t in range(NT + 1):
                    for s in range(min(t + 1, NT)):
                        ins = pe.matmul(banks[7][:, t * E:(t + 1) * E], (before if s == t else onesb)[:, :], AB[:, s, :],
                                        start=(s == 0), stop=(s == min(t, NT - 1)))
                ins.then_inc(sem("ranks_full"), 1)

            def experts(l):

                def settle():
                    pe.sem_inc(sem("pe_settled"), 1)

                def rows_T(u, e, lap):
                    u, b = u % RING, u % 2
                    pe.wait_ge(sem(f"xg_in{l}_{u}"), 16 * lap + 16)
                    wait(pe, f"xgt_ready{l}", e - 1)
                    settle()
                    for k in range(KD):
                        ins = pe.transpose(bank(b)[:, k * SLOTS:(k + 1) * SLOTS], XG[0:SLOTS, u, k:D:KD],
                                           ident[0:SLOTS, 0:SLOTS])
                    ins.then_inc(sem(f"xg_full{l}"), 1)

                def gate_up(u, e, lap):
                    u, b = u % RING, u % 2
                    pe.wait_ge(sem(f"w_ready_{l}_{u}"), 48 * lap + 48)
                    pe.wait_ge(sem(f"xgt_ready{l}"), e + 1)
                    wait(pe, f"a_ready{l}", e - 1)
                    w = WE[:, u, 0:2 * KD * FE].rearrange("p (j k n) -> p j k n", j=2, k=KD)
                    for k in range(KD):
                        ins = pe.matmul(bank(2 + b, 2, FE)[0:SLOTS], XGT[:, b, k * SLOTS:(k + 1) * SLOTS],
                                        w[:, :, k, :], start=(k == 0), stop=(k == KD - 1))
                    ins.then_inc(sem(f"gu_full{l}"), 1)

                def hidden_T(u, e):
                    b = u % 2
                    pe.wait_ge(sem(f"a_ready{l}"), e + 1)
                    wait(pe, f"at_ready{l}", e - 1)
                    settle()
                    for k in range(KF):
                        ins = pe.transpose(bank(4 + b)[:, k * SLOTS:(k + 1) * SLOTS], AE[0:SLOTS, b, k:FE:KF],
                                           ident[0:SLOTS, 0:SLOTS])
                    ins.then_inc(sem(f"at_full{l}"), 1)

                def down(u, e):
                    u, b = u % RING, u % 2
                    pe.wait_ge(sem(f"at_ready{l}"), e + 1)
                    wait(pe, f"ys_act{l}", e)
                    wait(pe, f"ys_dve{l}", e)
                    w = WE[:, u, 2 * KD * FE:].rearrange("p (k n) -> p k n", k=KF)
                    for j in range(2):
                        for k in range(KF):
                            ins = pe.matmul(bank(6 + j)[0:SLOTS, :], AT[:, b, k * SLOTS:(k + 1) * SLOTS],
                                            w[:, k, j * 512:(j + 1) * 512], start=(k == 0), stop=(k == KF - 1))
                    ins.then_inc(sem(f"y_full_{l}"), 1)

                def step(u, e, lap, before, after, after_lap):
                    gate_up(u, e, lap)
                    if after is not None:
                        rows_T(u + 1, after, after_lap)
                    if before is not None:
                        down(u - 1, before)
                    hidden_T(u, e)

                rows_T(0, 0, 0)
                for e in range(RING):
                    step(e, e, 0, e - 1 if e else None, e + 1, (e + 1) // RING)
                with pe.Fori(0, E // RING - 2) as i:
                    for u in range(RING):
                        step(u + RING, pe.snap(RING * i + (RING + u)), pe.snap(i + 1), pe.snap(RING * i + (RING + u - 1)),
                             pe.snap(RING * i + (RING + u + 1)), pe.snap(i + (RING + u + 1) // RING))
                for e in range(E - RING, E):
                    step(e, e, e // RING, e - 1, e + 1 if e + 1 < E else None, (e + 1) // RING)
                down(E - 1, E - 1)
                pe.wait_ge(sem("extra_ready"), l + 1)
                rounds = pe.value_load(extra[0:1, 0:1], min_val=0, max_val=ROUNDS - 1)
                with pe.If(rounds > 0):
                    with pe.Fori(0, rounds) as r:
                        with pe.Fori(0, E // RING) as q:
                            for u in range(RING):
                                e = pe.snap(E * r + RING * q + (E + u))
                                lap = pe.snap(E // RING * r + q + E // RING)
                                rows_T(u, e, lap)
                                gate_up(u, e, lap)
                                hidden_T(u, e)
                                down(u, e)

            pe.wait_ge(sem("constants"), 1)
            norm_turned(0)
            for k in range(KD):
                wait_turned(0, k)
            pe.wait_ge(sem("w_mkv_in"), 16)
            for m in range(XW // P):
                for k in range(KD):
                    ins = pe.matmul(bank(2 + m)[:, 0:M], w_mkv[:, k, m * P:(m + 1) * P], memhT[:, k, :],
                                    start=(k == 0), stop=(k == KD - 1))
                ins.then_inc(sem("mk_full"), 1)
            for c in range(MT):
                for k in range(KD):
                    ins = pe.matmul(bank(4 + c)[:, 0:XW], memhT[:, k, c * P:(c + 1) * P], w_mkv[:, k, XW:],
                                    start=(k == 0), stop=(k == KD - 1))
                ins.then_inc(sem("mv_full"), 1)
            pe.wait_ge(sem("tbl_ready"), 4)
            for t in range(NT):
                ins = pe.transpose(bank(7)[:, t * P:(t + 1) * P], tbl_tok[:, t, :], ident[:, :])
            ins.then_inc(sem("tblT_full"), 1)
            norm_turned(1)
            pe.wait_ge(sem("w_mla_in"), 16)

            def z_free(t, j):
                if t == 0:
                    pe.wait_ge(sem("mem_ready"), 2)
                    pe.wait_ge(sem("mv_ready"), 2)
                if t >= 2:
                    pe.wait_ge(sem("z_key" if j == 0 else "z_xq"), t - 1)

            project(1, w_mla, ((0, ZA), (ZA, ZW)), lambda t, j: 2 + 2 * (t % 2) + j, "z_full", z_free)
            pe.wait_ge(sem("z_key"), NT)
            pe.wait_ge(sem("z_xq"), NT)
            pe.wait_ge(sem("lat_normed"), 2 * NT)
            for k in range(KQ):
                for t in range(NT):
                    ins = pe.transpose(bank(k)[:, t * P:(t + 1) * P], ZS[:, t, k:QR:KQ], ident[:, :])
                ins.then_inc(sem("lat_T"), 1)
            for b, at in ((2, QR), (3, ZA), (4, ZA + P)):
                for t in range(NT):
                    ins = pe.transpose(bank(b)[:, t * P:(t + 1) * P], ZS[:, t, at:at + P], ident[:, :])
                ins.then_inc(sem("lat_T"), 1)
            pe.wait_ge(sem("kr_ready"), 3)
            for t in range(NT):
                ins = pe.transpose(bank(5)[:, t * P:(t + 1) * P], kr_tok[:, t, :], ident[:, :])
            ins.then_inc(sem("lat_T"), 1)
            pe.wait_ge(sem("lat_ready"), 3)
            pe.wait_ge(sem("w_qkv_in"), 32)
            wv = w_kv.rearrange("p (h n) -> p h n", h=H)
            for t in range(NT):
                for j in range(2):
                    if t >= 1:
                        pe.wait_ge(sem("v_act" if j == 0 else "v_dve"), t)
                    ins = pe.matmul(bank(j, H // 2, VD), KVT[:, t * P:(t + 1) * P],
                                    wv[:, j * H // 2:(j + 1) * H // 2, NOPE:], start=True, stop=True)
                    ins.then_inc(sem("v_full"), 1)
            pe.wait_ge(sem("v_act"), NT)
            pe.wait_ge(sem("v_dve"), NT)
            pe.wait_ge(sem("qct0"), 2)
            pe.wait_ge(sem("rope_done"), 1)
            cross_attention(0)
            pe.wait_ge(sem("xmix"), XHEADS)

            def head_project(s, h):
                pe.wait_ge(sem("wh_ready"), 4 * h + 4)
                wait(pe, "q_nope", h)
                wait(pe, "k_nope", h)
                wait(pe, "q_rope", h)
                for k in range(KQ):
                    pe.matmul(bank(4), wqh[s][:, k, :], QLT[:, k, :], start=(k == 0), stop=(k == KQ - 1))
                pe.matmul(bank(5)[0:NOPE, :], wkh[s], KVT, start=True, stop=True).then_inc(sem("qk_full"), 1)

            def head_scores(s, h):
                pe.wait_ge(sem("q_nope"), h + 1)
                pe.wait_ge(sem("k_nope"), h + 1)
                pe.wait_ge(sem("q_rope"), h + 1)
                wait(pe, "probs", 4 * h)
                for b, at, t, done in ((1, 0, 0, 0), (1, 128, 2, 1), (2, 0, 1, 1), (0, 0, 3, 1)):
                    n = (t + 1) * P
                    pe.matmul(bank(b)[:, at:at + n], qT[s][0:QKD, t * P:(t + 1) * P], kT[s][0:QKD, 0:n],
                              start=True, stop=False)
                    ins = pe.matmul(bank(b)[:, at + t * P:at + n], identb[:, :], causal[:, :], start=False, stop=True)
                    if done:
                        ins.then_inc(sem("scores_full"), 1)

            AT_OF = (0, 128, 384, 768)

            def head_values(h, col):
                def turn(t):
                    pe.wait_ge(sem("probs"), 4 * h + t + 1)
                    wait(pe, "pt_dve" if t % 2 == 0 else "pt_act", 2 * h + t // 2)
                    for c in range(t + 1):
                        a = AT_OF[t] + c * P
                        ins = pe.transpose(bank(6 + t % 2)[:, c * P:(c + 1) * P], PR[:, a:a + P], ident[:, :])
                    ins.then_inc(sem("p_T"), 1)

                def product(t):
                    pe.wait_ge(sem("pt_dve" if t % 2 == 0 else "pt_act"), 2 * h + t // 2 + 1)
                    if t == 0:
                        wait(pe, "mixed", h)
                    for c in range(t + 1):
                        ins = pe.matmul(bank(3)[:, t * VD:(t + 1) * VD], PT[:, t % 2, c * P:(c + 1) * P],
                                        V[:, c, bass.ds(col, VD)], start=(c == 0), stop=(c == t))
                    ins.then_inc(sem("o_done"), 1)

                turn(0)
                turn(1)
                product(0)
                turn(2)
                product(1)
                turn(3)
                product(2)
                product(3)

            head_project(0, 0)
            head_scores(0, 0)
            head_project(1, 1)
            head_values(0, 0)
            with pe.Fori(0, H // 2 - 1) as i:
                for s in (1, 0):
                    h = pe.snap(2 * i + (2 - s))
                    head_scores(s, h)
                    head_project(1 - s, pe.snap(2 * i + (3 - s)))
                    head_values(h, pe.snap(2 * VD * i + (2 - s) * VD))
            head_scores(1, H - 1)
            head_values(H - 1, (H - 1) * VD)
            pe.wait_ge(sem("mixed"), H)
            output_projection(0)
            norm_turned(2)
            router(0)
            experts(0)
            norm_turned(3)
            pe.wait_ge(sem("w_pool_in"), 16)

            def zp_free(t, j):
                if t >= 2:
                    pe.wait_ge(sem("u_act" if j == 0 else "u_dve"), t - 1 if j == 0 else 2 * (t - 1))

            project(3, w_pool, ((0, 512), (512, D)), lambda t, j: 2 + 2 * (t % 2) + j, "zp_full", zp_free)
            pe.wait_ge(sem("u_act"), NT)
            pe.wait_ge(sem("u_dve"), 2 * NT)
            for m in range(XW // P):
                for t in range(NT):
                    ins = pe.transpose(bank(m)[:, t * P:(t + 1) * P], QC[:, t, m * P:(m + 1) * P], ident[:, :])
                ins.then_inc(sem("qcT_full1"), 1)
            pe.wait_ge(sem("bands_ready"), 2 * len(WINDOWS))
            for j in range(2 * len(WINDOWS)):
                g, b = j // 2, bank(6 + j % 2)[0:HW, :]
                if j >= 2:
                    pe.wait_ge(sem("d_act" if j % 2 == 0 else "d_dve"), j // 2)
                for t in range(NT):
                    lhs = U[:, t, j * HW:(j + 1) * HW]
                    if t == 0:
                        pe.matmul(b[:, 0:16], lhs, band0[:, g, :], start=True, stop=False, skip_group_check=True)
                        pe.matmul(b[:, 16:HALO], lhs, band[:, g, 16:HALO], start=False, stop=False,
                                  skip_group_check=True)
                    else:
                        end = min(S, t * P + HALO)
                        ins = pe.matmul(b[:, t * P:end], lhs, band[:, g, 0:end - t * P], start=False,
                                        stop=(t == NT - 1), skip_group_check=True)
                ins.then_inc(sem("d_full"), 1)
            pe.wait_ge(sem("w_mix_in"), 32)
            pe.wait_ge(sem("d_act"), len(WINDOWS))
            pe.wait_ge(sem("d_dve"), len(WINDOWS))
            for t in range(NT):
                for j in range(2):
                    if t >= 2:
                        pe.wait_ge(sem("pool_mixed"), 2 * (t - 2) + j + 1)
                    for g in range(2):
                        for c in range(2):
                            jj = 2 * (2 * j + g) + c
                            ins = pe.matmul(bank(2 + 2 * (t % 2) + j)[:, g * GW:(g + 1) * GW],
                                            dT[0:HW, jj, t * P:(t + 1) * P], w_mix[0:HW, jj, :],
                                            start=(c == 0), stop=(c == 1))
                    ins.then_inc(sem("y_pool"), 1)
            pe.wait_ge(sem("qct_act"), 1)
            pe.wait_ge(sem("qct_dve"), 1)
            pe.wait_ge(sem("pool_mixed"), 2 * NT)
            cross_attention(1)
            output_projection(1)
            norm_turned(4)
            router(1)
            experts(1)


_INS = ['x', 'mem', 'positions', 'g_mix', 'w_in_mla', 'g_q_lat', 'w_uq', 'g_kv_lat', 'w_ukv', 'w_in_pool',
        'w_pool_mix', 'pool_scale', 'g_mem', 'w_mem_kv', 'w_o', 'g_ffn', 'w_router_group', 'b_router_group',
        'w_router_expert', 'b_router_expert', 'w_expert_gate', 'w_expert_up', 'w_expert_down', 'g_final']


def kernel(**inputs):
    import numpy as _np
    import concourse.bacc as _bacc
    from concourse import mybir as _mybir
    from concourse.bass_utils import run_bass_kernel_spmd as _run

    nc = _bacc.Bacc("TRN2", target_bir_lowering=False, num_devices=1)
    arrays, args = {}, []
    for name in _INS:
        a = _np.ascontiguousarray(inputs[name])
        arrays[f"in_{name}_dram"] = a
        args.append(nc.dram_tensor(f"in_{name}_dram", a.shape, _mybir.dt.from_np(a.dtype), kind="ExternalInput").ap())
    shape = inputs['x'].shape
    out = nc.dram_tensor("out_0_dram", shape, _mybir.dt.float32, kind="ExternalOutput").ap()
    program(nc, *args, out)
    r = _run(nc, [arrays], core_ids=[0])
    return r.results[0]["out_0_dram"]
```

```python
from contextlib import ExitStack

import numpy as np

import concourse.bass as bass
from concourse import mybir

F32 = mybir.dt.float32
F32R = mybir.dt.float32r
BF16 = mybir.dt.bfloat16
I32 = mybir.dt.int32
ALU = mybir.AluOpType
ACT = mybir.ActivationFunctionType
AX = mybir.AxisListType

P = 128
EPS = 1e-6
NEG_INF = -1e30
THETA = 10000.0
WINDOWS = (2, 4, 8, 16)
XHEADS = 4
GROUPS = 4
PER_GROUP = 8
SLOTS = 64
RING = 4
NO_TOKEN = 1 << 20


def program(nc, x, mem, positions, g_mix, w_in_mla, g_q_lat, w_uq, g_kv_lat, w_ukv, w_in_pool, w_pool_mix,
            pool_scale, g_mem, w_mem_kv, w_o, g_ffn, w_router_group, b_router_group, w_router_expert,
            b_router_expert, w_expert_gate, w_expert_up, w_expert_down, g_final, out):
    S, D = x.shape[1:]
    M = mem.shape[1]
    NT, MT, KD = S // P, M // P, D // P
    QR, KVR = g_q_lat.shape[1], g_kv_lat.shape[1]
    XW = w_mem_kv.shape[1] // 2
    XD = XW // XHEADS
    MW = D - XW
    ROPE = w_in_mla.shape[2] - QR - KVR - XW
    HALF = ROPE // 2
    VD = 64
    NOPE = 64
    H = MW // VD
    QKD = NOPE + ROPE
    ZW = w_in_mla.shape[2]
    ZA = QR + KVR + ROPE
    KQ = QR // P
    E = w_expert_gate.shape[1]
    FE = w_expert_gate.shape[3]
    KF = FE // P
    NR = GROUPS + E
    GW = MW // len(WINDOWS)
    HW = GW // 2
    ROUNDS = S // SLOTS
    HALO = P + max(WINDOWS) - 1
    QSCALE = QKD ** -0.5
    XSCALE = XD ** -0.5
    assert (S, D, M, QR, KVR, XD, ROPE, H, E, FE) == (512, 1024, 256, 256, 128, 64, 32, 12, 32, 256)
    inv_freq = (THETA ** (-np.arange(0, ROPE, 2, dtype=np.float64) / ROPE)).astype(np.float32)

    with ExitStack() as ctx:
        place = {}

        def sb(name, shape, dt=F32):
            place[name] = nc.sbuf_base
            return ctx.enter_context(nc.sbuf_tensor(name, shape, dt))

        def over(base, at, name, shape, dt):
            return nc.alloc_sbuf_tensor_at(name, shape, dt, offset=place[base] + 4 * at)

        sems = {}

        def sem(name):
            if name not in sems:
                sems[name] = ctx.enter_context(nc.semaphore(name))
            return sems[name]

        xn_dram = [nc.dram_tensor(f"xn_rows_{l}", (S, D), F32, kind="Internal").ap() for l in range(2)]
        slot_dram = [nc.dram_tensor(f"slot_table_{l}", (S * E, 1), I32, kind="Internal").ap() for l in range(2)]
        y_dram = [nc.dram_tensor(f"expert_rows_{l}", (2 * S, D), F32, kind="Internal").ap() for l in range(2)]

        X = sb("X", [P, NT, D])
        XN = sb("XN", [P, NT, D])
        HT = sb("HT", [P, KD * S])
        WIN = sb("WIN", [P, KD * D])
        WE = sb("WE", [P, RING, 3 * KD * FE])
        T = sb("T", [P, 5376])
        MK = sb("MK", [P, XW // P, M])
        MV = sb("MV", [P, MT, XW])
        WR = sb("WR", [P, KD, NR])
        ident = sb("ident", [P, P])
        identb = sb("identb", [P, P], BF16)
        causal = sb("causal", [P, P], BF16)
        before = sb("before", [P, P], BF16)
        onesb = sb("onesb", [P, P], BF16)
        iota_e = sb("iota_e", [P, E])
        tie = sb("tie", [P, PER_GROUP])
        thresh = sb("thresh", [P, ROUNDS - 1])
        dest = sb("dest", [P, 2 * NT], I32)
        slot_pos = sb("slot_pos", [P, 2 * NT], I32)
        SIDX = sb("SIDX", [P, ROUNDS * E], I32)
        INV = SIDX[:, 0:S * E // P]
        GIDX = sb("GIDX", [P, ROUNDS * E], I32)
        gidx = sb("gidx", [P, RING], I32)
        sidx = sb("sidx", [P, 2], I32)
        extra = sb("extra", [P, 1], I32)
        GN = sb("GN", [P, 3, KD])
        gq = sb("gq", [P, KQ])
        gkv = sb("gkv", [P, 1])
        bias_r = sb("bias_r", [P, 2, NR])
        stat = sb("stat", [P, 64])
        wtok = sb("wtok", [P, 2, NT])

        def view(base, at, *shape):
            n = int(np.prod(shape))
            v = base[:, at:at + n]
            if len(shape) == 2:
                v = v.rearrange("p (a b) -> p a b", a=shape[0])
            if len(shape) == 3:
                v = v.rearrange("p (a b c) -> p a b c", a=shape[0], b=shape[1])
            return v

        hT = view(HT, 0, KD, S)
        WEflat = WE[:, :, :].rearrange("p r n -> p (r n)")
        RB = 3 * KD * FE
        memhT = view(HT, 0, KD, M)
        MEM = view(HT, KD * M, MT, D)
        w_mkv = view(WEflat, 2 * RB, KD, 2 * XW)
        w_out = view(WEflat, 2 * RB + KD * 2 * XW, KD, D)
        w_mla = view(WIN, 0, KD, ZW)
        ZS = view(WIN, KD * ZW, NT, ZW)
        w_q = view(WEflat, RB, KQ, H * QKD)
        w_kv = view(WEflat, RB + 2304, H * 2 * VD)
        QLT = view(WEflat, RB + 3840, KQ, S)
        KVT = view(WEflat, RB + 4864, S)
        TBL = view(WEflat, RB + 5376, S)
        V = view(HT, 0, NT, MW)
        QCT0 = view(HT, NT * MW, XW // P, S)
        rope_scratch = view(WIN, 0, S)
        PR = [view(T, 0, 1280), view(WIN, 1536, 1280)]
        PT = view(T, 1280, 2 * S)
        PT_AT = (0, S, P, S)
        qT = [view(T, 2304 + 512 * s, S) for s in range(2)]
        kT = [view(T, 3328 + 512 * s, S) for s in range(2)]
        wqh = [view(T, 4352 + 256 * s, KQ, P) for s in range(2)]
        wkh = [view(T, 4864 + 64 * s, 64) for s in range(2)]
        posf = view(T, 0, NT)
        freq = view(T, 8, HALF)
        ang = view(T, 64, NT, HALF)
        turns = view(T, 128, 2, NT * HALF)
        rang = view(T, 256, 2, NT * HALF)
        trig = view(T, 384, 2, NT * HALF)
        tbl_tok = view(T, 512, NT, P)
        kr_tok = view(T, 1024, NT, P)
        posi = T[:, 1536:1536 + NT].bitcast(I32)
        XP0, XPT0 = (view(T, 0, NT, M), view(WIN, S, NT, M)), view(T, NT * M, MT, S)
        w_pool = view(WIN, 0, KD, D)
        U = view(T, 0, NT, MW)
        QC = view(T, NT * MW, NT, XW)
        band = view(T, NT * D, len(WINDOWS), HALO)
        band0 = view(T, NT * D + len(WINDOWS) * HALO, len(WINDOWS), max(WINDOWS))
        ramp = view(T, NT * D + len(WINDOWS) * (HALO + 16), len(WINDOWS), max(WINDOWS))
        dT = view(HT, 0, 2 * len(WINDOWS), S)
        QCT1 = view(WEflat, RB, XW // P, S)
        XP1 = view(WEflat, RB + 1024, NT, M), view(WIN, 0, NT, M)
        XPT1 = view(WEflat, RB + 2048, MT, S)
        w_mix = view(WEflat, RB + 3072, 2 * len(WINDOWS), GW)
        scale_b = view(WEflat, RB + 3072 + 8 * GW, MW)
        XG = view(HT, 0, RING, D)
        XGT = over("T", 0, "rows_T", [P, 2, 2, KD * SLOTS], F32R)
        YS = view(T, 2 * D, 2, D)
        SG = view(T, 4 * D, 2, FE)
        AT = over("T", 4 * D + 2 * FE, "hidden_T", [P, 2, 2, KF * SLOTS], F32R)
        GU = 2 * KD * FE
        GU_HI = over("WIN", 0, "gate_up_hi", [P, 2, GU], F32R)
        DOWN_HI = over("XN", 0, "down_hi", [P, 2, KF * D], F32R)
        W_LO = [over("WE", u * RB, f"weights_lo_{u}", [P, RB], F32R) for u in range(RING)]
        CHUNK = 2 * KD * FE // 4
        YL = [view(HT, 0, 2, D), view(HT, 2 * D, 2, D), XN[:, 0:2, :], XN[:, 2:4, :]]
        gain = view(T, 4352, D)
        gfin = view(WIN, 0, D)
        LG = view(T, 0, NT, NR)
        LS = view(T, 256, NT, GROUPS)
        EG = view(T, 272, NT, GROUPS)
        SC = view(T, 288, NT, PER_GROUP)
        OG = view(T, 320, NT, GROUPS)
        LE = view(T, 384, NT, E)
        SEL = view(T, 512, NT, PER_GROUP)
        O1 = view(T, 544, NT, PER_GROUP)
        O2 = view(T, 576, NT, PER_GROUP)
        A1 = view(T, 640, NT, E)
        A2 = view(T, 768, NT, E)
        POS = view(T, 896, NT, E)
        PM = view(T, 1024, NT, E)
        AB = T[:, 1152:1152 + NT * E // 2].bitcast(BF16).rearrange("p (t e) -> p t e", t=NT)
        small = view(T, 1280, 64)
        CF = view(T, 1536, ROUNDS * E)

        banks = [ctx.enter_context(nc.psum_tensor(f"bank{i}", [P, 512], F32)) for i in range(8)]

        def bank(i, *shape):
            v = banks[i][:, :]
            if shape:
                v = v[:, 0:int(np.prod(shape))].rearrange("p (a b) -> p a b", a=shape[0])
            return v

        def wide(ap, *shape):
            return ap.to_broadcast(list(shape))

        def wait(eng, name, count):
            if not isinstance(count, int) or count > 0:
                eng.wait_ge(sem(name), count)

        def feat(w):
            return w.rearrange("(p k) n -> p (k n)", p=P)

        def row(v):
            return v.rearrange("(a n) -> a n", a=1)

        TILES = [0] + [MT + NT * n for n in range(5)]
        expert_counts = [f"{name}_{u}" for name in ("gu_in", "down_in") for u in range(RING)]
        expert_counts += ["gidx_set", "sidx_set", "xg_full", "x_hi", "x_lo", "gu_hi",
                          "gu_lo", "down_hi", "down_lo", "gu_full", "sg_ready", "a_ready", "at_full", "a_hi", "a_lo",
                          "y_full", "ys_act", "ys_dve"]
        block = ctx.enter_context(nc.Block())

        @block.sync
        def _(sp):
            sp.wait_ge(sem("inv_ready"), 1)
            for l in range(2):
                sp.dma_start(slot_dram[l].rearrange("(p n) a -> p (n a)", p=P), INV).then_inc(sem("slot_cleared"), 16)
            for t in range(MT):
                sp.dma_start(MEM[:, t, :], mem[0, t * P:(t + 1) * P, :]).then_inc(sem("mem_in"), 16)
            sp.dma_start(w_mkv.rearrange("p k n -> p (k n)"), feat(w_mem_kv)).then_inc(sem("w_mkv_in"), 16)
            for t in range(NT):
                sp.dma_start(X[:, t, :], x[0, t * P:(t + 1) * P, :]).then_inc(sem("x_in"), 16)
            sp.dma_start(w_mla.rearrange("p k n -> p (k n)"), feat(w_in_mla[0])).then_inc(sem("w_mla_in"), 16)
            sp.dma_start(w_kv, w_ukv[0]).then_inc(sem("w_qkv_in"), 16)
            sp.dma_start(w_q.rearrange("p k n -> p (k n)"), feat(w_uq[0])).then_inc(sem("w_qkv_in"), 16)
            sp.dma_start(w_out.rearrange("p k n -> p (k n)"), feat(w_o[0])).then_inc(sem("w_out_in"), 16)

            def load_gate_up(l, u, e):
                for j, w in enumerate((w_expert_gate, w_expert_up)):
                    src = w[l, bass.ds(e, 1)].rearrange("a (p k) n -> p (a k n)", p=P)
                    sp.dma_start(WE[:, u, j * KD * FE:(j + 1) * KD * FE], src).then_inc(sem(f"gu_in_{u}"), 16)

            def load_down(l, u, e):
                src = w_expert_down[l, bass.ds(e, 1)].rearrange("a (p k) n -> p (a k n)", p=P)
                sp.dma_start(WE[:, u, GU:], src).then_inc(sem(f"down_in_{u}"), 16)

            for l in range(2):
                if l == 1:
                    sp.wait_ge(sem("moe_done"), 1)
                load_gate_up(l, 0, 0)
                load_down(l, 0, 0)
                sp.dma_start(WR[:, :, 0:GROUPS], w_router_group[l].rearrange("(p k) n -> p k n", p=P))\
                    .then_inc(sem("wr_in"), 16)
                sp.dma_start(WR[:, :, GROUPS:], w_router_expert[l].rearrange("(p k) n -> p k n", p=P))\
                    .then_inc(sem("wr_in"), 16)
                if l == 0:
                    sp.wait_ge(sem("mixed"), H)
                else:
                    sp.wait_ge(sem("d_full"), 2 * len(WINDOWS))
                sp.dma_start(gain, row(g_ffn[l]).to_broadcast([P, D])).then_inc(sem("gain_in"), 16)
                for t in range(NT):
                    sp.wait_ge(sem("xn"), TILES[2 * l + 2] + t + 1)
                    if t == 0:
                        for u in range(1, RING):
                            load_gate_up(l, u, u)
                            if u + 1 < RING:
                                load_down(l, u, u)
                    sp.dma_start(xn_dram[l][t * P:(t + 1) * P, :], XN[:, t, :]).then_inc(sem("xn_out"), 16)
                sp.wait_ge(sem("slot_scattered"), 16 * 2 * NT * (l + 1))
                sp.dma_start(SIDX[0:SLOTS, :].rearrange("s (r e) -> s r e", r=ROUNDS),
                             slot_dram[l].rearrange("(r s e) a -> s r (e a)", r=ROUNDS, s=SLOTS))\
                    .then_inc(sem("sidx_in"), 16)

                def load_ahead(u, e):
                    sp.wait_ge(sem("gu_full"), e + 1 if isinstance(e, int) else sp.snap(e + 1))
                    load_gate_up(l, u, e + RING if isinstance(e, int) else sp.snap(e + RING))
                    if not isinstance(e, int) or e >= 1:
                        sp.wait_ge(sem("y_full"), e)
                    load_down(l, (u - 1) % RING, e + RING - 1 if isinstance(e, int) else sp.snap(e + (RING - 1)))

                for e in range(RING):
                    load_ahead(e, e)
                with sp.Fori(0, E // RING - 2) as i:
                    for u in range(RING):
                        load_ahead(u, sp.snap(RING * i + (RING + u)))
                sp.wait_ge(sem("y_full"), E - RING)
                load_down(l, RING - 1, E - 1)
                sp.wait_ge(sem("extra_ready"), l + 1)
                rounds = sp.value_load(extra[0:1, 0:1], min_val=0, max_val=ROUNDS - 1)
                with sp.If(rounds > 0):
                    with sp.Fori(0, rounds) as r:
                        with sp.Fori(0, E // RING) as q:
                            for u in range(RING):
                                e = sp.snap(RING * q + u)
                                sp.wait_ge(sem("y_full"), sp.snap(E * r + RING * q + (E + u - RING + 1)))
                                load_gate_up(l, u, e)
                                load_down(l, u, e)
                sp.wait_ge(sem("moe_done"), l + 1)
                for t in range(NT):
                    for j in range(2):
                        sp.dma_start(YL[t][:, j, :], y_dram[l][j * S + t * P:j * S + (t + 1) * P, :])\
                            .then_inc(sem(f"yl_in_{t}"), 16)
                    if l == 0 and t == NT - 1:
                        sp.dma_start(w_pool.rearrange("p k n -> p (k n)"), feat(w_in_pool[0]))\
                            .then_inc(sem("w_pool_in"), 16)
                        sp.dma_start(w_mix[0:HW].rearrange("p (g c) n -> p g c n", c=2),
                                     w_pool_mix[0].rearrange("g (c p) n -> p g c n", c=2)).then_inc(sem("w_mix_in"), 16)
                        sp.dma_start(scale_b, row(pool_scale[0]).to_broadcast([P, MW])).then_inc(sem("w_mix_in"), 16)
                        sp.dma_start(w_out.rearrange("p k n -> p (k n)"), feat(w_o[1])).then_inc(sem("w_out_in"), 16)
                if l == 1:
                    sp.dma_start(gfin, row(g_final).to_broadcast([P, D])).then_inc(sem("gfin_in"), 16)
            for t in range(NT):
                sp.wait_ge(sem("fin"), t + 1)
                sp.dma_start(out[0, t * P:(t + 1) * P, :], XN[:, t, :]).then_inc(sem("out_done"), 16)
            sp.wait_ge(sem("out_done"), 16 * NT)

        @block.gpsimd
        def _(pool):
            steps = [0]

            def link(ins):
                steps[0] += 1
                ins.then_inc(sem("pool_step"), 1)
                pool.wait_ge(sem("pool_step"), steps[0])

            def small_loads():
                for j, g in enumerate((g_mem, g_mix[0], g_mix[1])):
                    pool.dma_start(GN[:, j, :], g.rearrange("(p k) -> p k", p=P)).then_inc(sem("small_in"), 16)
                pool.dma_start(gq[:, :], g_q_lat[0].rearrange("(p k) -> p k", p=P)).then_inc(sem("small_in"), 16)
                pool.dma_start(gkv[:, :], g_kv_lat[0].rearrange("(p k) -> p k", p=P)).then_inc(sem("small_in"), 16)
                pool.dma_start(posi, positions[0].rearrange("(t p) -> p t", p=P)).then_inc(sem("small_in"), 16)
                for l in range(2):
                    pool.dma_start(bias_r[:, l, 0:GROUPS], row(b_router_group[l]).to_broadcast([P, GROUPS]))\
                        .then_inc(sem("small_in"), 16)
                    pool.dma_start(bias_r[:, l, GROUPS:], row(b_router_expert[l]).to_broadcast([P, E]))\
                        .then_inc(sem("small_in"), 16)

            pool.memset(INV, NO_TOKEN).then_inc(sem("inv_ready"), 1)
            with nc.allow_non_contiguous_dma(reason="a few small vectors, once"):
                small_loads()
            link(pool.memset(ident[:, :], 0.0))
            pool.affine_select(out=ident[:, :], in_=ident[:, :], compare_op=ALU.not_equal, fill=1.0, base=0,
                               pattern=[[-1, P]], channel_multiplier=1).then_inc(sem("constants"), 1)
            for i, f in enumerate(inv_freq):
                last = pool.memset(freq[:, i:i + 1], float(f))
            last.then_inc(sem("constants"), 1)
            link(pool.memset(tbl_tok, 0.0))
            link(pool.memset(kr_tok, 0.0))
            pool.memset(stat[:, 48:49], 0.0).then_inc(sem("constants"), 1)
            link(pool.memset(identb[:, :], 0.0))
            link(pool.affine_select(out=identb[:, :], in_=identb[:, :], compare_op=ALU.not_equal, fill=1.0, base=0,
                                    pattern=[[-1, P]], channel_multiplier=1))
            link(pool.memset(causal[:, :], 0.0))
            link(pool.affine_select(out=causal[:, :], in_=causal[:, :], compare_op=ALU.is_ge, fill=NEG_INF, base=0,
                                    pattern=[[-1, P]], channel_multiplier=1))
            link(pool.memset(onesb[:, :], 1.0))
            link(pool.affine_select(out=before[:, :], in_=onesb[:, :], compare_op=ALU.is_gt, fill=0.0, base=0,
                                    pattern=[[1, P]], channel_multiplier=-1))
            link(pool.iota(iota_e[:, :], pattern=[[1, E]], base=0, channel_multiplier=0,
                           allow_small_or_imprecise_dtypes=True))
            link(pool.iota(tie[:, :], pattern=[[-1, PER_GROUP]], base=PER_GROUP, channel_multiplier=0,
                           allow_small_or_imprecise_dtypes=True))
            link(pool.iota(thresh[:, :], pattern=[[SLOTS, ROUNDS - 1]], base=SLOTS, channel_multiplier=0,
                           allow_small_or_imprecise_dtypes=True))
            pool.iota(dest[:, :], pattern=[[S, 2], [P, NT]], base=0, channel_multiplier=1)\
                .then_inc(sem("constants"), 1)

            pool.wait_ge(sem("z_key"), NT)
            kr = ZS[:, :, QR + KVR:ZA]
            pool.tensor_copy(kr_tok[:, :, NOPE:QKD], kr).then_inc(sem("kr_ready"), 1)
            pool.tensor_copy(kr_tok[:, :, QKD:QKD + HALF], kr[:, :, HALF:]).then_inc(sem("kr_ready"), 1)
            pool.tensor_copy(kr_tok[:, :, QKD + HALF:], kr[:, :, 0:HALF]).then_inc(sem("kr_ready"), 1)

            def head_weights(s, h, used):
                if used is not None:
                    pool.wait_ge(sem("k_full"), used)
                src = w_q[:, :, bass.ds(h * QKD, QKD)]
                pool.tensor_copy(wqh[s][:, :, 0:QKD], src).then_inc(sem("wh_ready"), 1)
                a = w_q[:, :, bass.ds(h * QKD + (NOPE + HALF), HALF)]
                pool.tensor_copy(wqh[s][:, :, QKD:QKD + HALF], a).then_inc(sem("wh_ready"), 1)
                b = w_q[:, :, bass.ds(h * QKD + NOPE, HALF)]
                pool.tensor_copy(wqh[s][:, :, QKD + HALF:], b).then_inc(sem("wh_ready"), 1)
                c = w_kv[:, bass.ds(h * 2 * VD, NOPE)]
                pool.tensor_copy(wkh[s], c).then_inc(sem("wh_ready"), 1)

            pool.wait_ge(sem("w_qkv_in"), 32)
            for s in range(2):
                head_weights(s, s, None)
            with pool.Fori(0, H // 2 - 1) as i:
                for s in range(2):
                    head_weights(s, 2 * i + (2 + s), 2 * i + (s + 1))

            def band_matrices():
                for g, w in enumerate(WINDOWS):
                    link(pool.memset(band[:, g, :], 1.0))
                    link(pool.affine_select(out=band[:, g, :], in_=band[:, g, :], compare_op=ALU.is_ge, fill=0.0,
                                            base=0, pattern=[[1, HALO]], channel_multiplier=-1))
                    link(pool.affine_select(out=band[:, g, :], in_=band[:, g, :], compare_op=ALU.is_gt, fill=0.0,
                                            base=w, pattern=[[-1, HALO]], channel_multiplier=1))
                    link(pool.iota(ramp[:, g, :], pattern=[[1, 16]], base=1, channel_multiplier=0,
                                   allow_small_or_imprecise_dtypes=True))
                    link(pool.tensor_scalar(ramp[:, g, :], ramp[:, g, :], float(w), None, ALU.min))
                pool.tensor_copy(band0, band[:, :, 0:16]).then_inc(sem("band_sums"), 1)

            for l in range(2):
                pool.wait_ge(sem("slot_cleared"), 16 * 2)
                for c in range(2 * NT):
                    if c % NT == 0:
                        pool.wait_ge(sem("slot_pos_ready"), 2 * l + c // NT + 1)
                    pool.indirect_dma_start(
                        out=slot_dram[l], out_offset=bass.IndirectOffsetOnAxis(ap=slot_pos[:, c:c + 1], axis=0),
                        in_=dest[:, c:c + 1], in_offset=None, bounds_check=S * E - 1, oob_is_err=False)\
                        .then_inc(sem("slot_scattered"), 16)
                pool.wait_ge(sem("router_full"), l + 1)
                pool.wait_ge(sem("gidx_ready"), l + 1)
                pool.wait_ge(sem("xn_out"), 16 * NT * (l + 1))
                gather_bound = pool.to_reg(S - 1)
                scatter_bound = pool.to_reg(2 * S - 1)

                def settle():
                    pool.sem_inc(sem("pool_settled"), 1)

                def gather(u, e):
                    u %= RING
                    wait(pool, "xg_full", e - (RING - 1))
                    pool.tensor_copy(gidx[0:SLOTS, u:u + 1], GIDX[0:SLOTS, bass.ds(e, 1)])\
                        .then_inc(sem("gidx_set"), 1)
                    pool.wait_ge(sem("gidx_set"), e + 1)
                    settle()
                    pool.indirect_dma_start(
                        out=XG[0:SLOTS, u, :], out_offset=None, in_=xn_dram[l],
                        in_offset=bass.IndirectOffsetOnAxis(ap=gidx[0:SLOTS, u:u + 1], axis=0),
                        bounds_check=gather_bound, oob_is_err=False).then_inc(sem(f"xg_in{l}_{u}"), 16)

                def scatter(u, e, turn):
                    b = u % 2
                    wait(pool, f"scattered{l}_{b}", 16 * turn)
                    pool.tensor_copy(sidx[0:SLOTS, b:b + 1], SIDX[0:SLOTS, bass.ds(e, 1)])\
                        .then_inc(sem("sidx_set"), 1)
                    pool.wait_ge(sem("sidx_set"), e + 1)
                    pool.wait_ge(sem("ys_act"), e + 1)
                    pool.wait_ge(sem("ys_dve"), e + 1)
                    settle()
                    pool.indirect_dma_start(
                        out=y_dram[l], out_offset=bass.IndirectOffsetOnAxis(ap=sidx[0:SLOTS, b:b + 1], axis=0),
                        in_=YS[0:SLOTS, b, :], in_offset=None, bounds_check=scatter_bound, oob_is_err=False)\
                        .then_inc(sem(f"scattered{l}_{b}"), 16)

                for e in range(RING):
                    gather(e, e)
                for e in range(RING):
                    gather(e, e + RING)
                    scatter(e, e, e // 2)
                with pool.Fori(0, E // RING - 2) as i:
                    for u in range(RING):
                        gather(u, pool.snap(RING * i + (2 * RING + u)))
                        scatter(u, pool.snap(RING * i + (RING + u)), pool.snap(2 * i + (RING + u) // 2))
                for e in range(E - RING, E):
                    scatter(e, e, e // 2)
                pool.wait_ge(sem("extra_ready"), l + 1)
                rounds = pool.value_load(extra[0:1, 0:1], min_val=0, max_val=ROUNDS - 1)
                for b in range(2):
                    pool.wait_ge(sem(f"scattered{l}_{b}"), 16 * E // 2)
                with pool.If(rounds > 0):
                    with pool.Fori(0, rounds) as r:
                        with pool.Fori(0, E // RING) as q:
                            for u in range(RING):
                                e = pool.snap(E * r + RING * q + (E + u))
                                turn = pool.snap(E // 2 * r + 2 * q + (E + u) // 2)
                                gather(u, e)
                                scatter(u, e, turn)
                                pool.wait_ge(sem(f"scattered{l}_{u % 2}"), 16 * turn + 16)
                if l == 0:
                    for name in expert_counts:
                        pool.sem_clear(sem(name))
                pool.sem_inc(sem("moe_done"), 1)
                if l == 0:
                    pool.wait_ge(sem("moe_done"), 1)
                    band_matrices()

        NORM_TILES = [MT] + [NT] * 5

        def norm_source(n):
            return MEM if n == 0 else X

        def wait_tile(eng, n, t):
            if n == 0:
                eng.wait_ge(sem("mem_in"), 16 * MT)
            elif n == 1:
                eng.wait_ge(sem("x_in"), 16 * NT)
            elif n % 2 == 0:
                eng.wait_ge(sem("o_added"), 2 * NT * (n // 2 - 1) + 2 * t + 2)
            else:
                eng.wait_ge(sem("x_moe"), NT * (n // 2 - 1) + t + 1)

        def ht_of(n):
            return memhT if n == 0 else hT

        def chunk(w, c):
            return w.rearrange("p (j n) -> p j n", j=2)[:, :, c * CHUNK // 2:(c + 1) * CHUNK // 2]

        @block.scalar
        def _(act):
            def norm_squares(n):
                nt = NORM_TILES[n]
                src = norm_source(n)
                for t in range(nt):
                    wait_tile(act, n, t)
                    if n in (2, 4) and t == 0:
                        act.wait_ge(sem("mixT_full"), KD * (n // 2))
                    to = T[:, t * D:(t + 1) * D] if n in (3, 5) else XN[:, t, :]
                    act.activation(to, src[:, t, :], ACT.Square, accum_out=stat[:, t:t + 1])\
                        .then_inc(sem("squares"), 1)
                act.wait_ge(sem("var"), n + 1)
                act.activation(stat[:, 8:8 + nt], stat[:, 4:4 + nt], ACT.Sqrt).then_inc(sem("root"), 1)

            def norm_turned(n):
                width = NORM_TILES[n] * P
                for k in range(0, KD, 2):
                    act.wait_ge(sem("tok_T"), KD * n + k + 1)
                    if k == 0:
                        act.wait_ge(sem("small_in"), 16 * 10)
                    g = 1.0 if n in (2, 4) else GN[:, (n + 1) // 2, k:k + 1]
                    act.activation(ht_of(n)[:, k, :], bank(0)[:, 0:width], ACT.Copy, scale=g)\
                        .then_inc(sem("hT_act"), 1)

            def cross_attention(l):
                XP, XPT = (XP0, XPT0) if l == 0 else (XP1, XPT1)

                def exponentials(h):
                    p = h % 2
                    act.wait_ge(sem("x_max"), 2 * XHEADS * l + 2 * h + 2)
                    if h >= 2:
                        act.wait_ge(sem("xp_T"), MT * (XHEADS * l + h - 1))
                        act.wait_ge(sem("x_inv"), XHEADS * l + h - 1)
                    for t in range(NT):
                        s = bank(2 * p + t // 2)[:, (t % 2) * M:(t % 2 + 1) * M]
                        act.activation(XP[p][:, t, :], s, ACT.Exp, bias=stat[:, 24 + 4 * p + t:25 + 4 * p + t],
                                       accum_out=stat[:, 32 + 4 * p + t:33 + 4 * p + t]).then_inc(sem("x_exp"), 1)

                if l == 0:
                    act.wait_ge(sem("rope_done"), 1)
                exponentials(0)
                exponentials(1)
                for h in range(XHEADS):
                    act.wait_ge(sem("xp_T"), MT * (XHEADS * l + h) + 1)
                    if h >= 1:
                        act.wait_ge(sem("xo_full"), XHEADS * l + h)
                    act.activation(XPT[:, 0, :], bank(4), ACT.Copy).then_inc(sem("xpt_act"), 1)
                    if h + 2 < XHEADS:
                        exponentials(h + 2)

            def mix_turned(l):
                for k in range(0, KD, 2):
                    act.wait_ge(sem("mixT_full"), KD * l + k + 1)
                    act.activation(hT[:, k, :], bank(0), ACT.Copy).then_inc(sem("mixT_act"), 1)

            def head_nope(s, h):
                wait(act, "scores_full", 3 * h)
                act.wait_ge(sem("q_full"), h + 1)
                act.activation(qT[s][0:NOPE, :], bank(4)[0:NOPE, :], ACT.Copy).then_inc(sem("q_nope"), 1)
                act.wait_ge(sem("k_full"), h + 1)
                act.activation(kT[s][0:NOPE, :], bank(5)[0:NOPE, :], ACT.Copy).then_inc(sem("k_nope"), 1)

            SLOT_OF = [(1, 0, 0), (2, 0, 128), (1, 128, 384), (0, 0, 768)]

            def head_exp(p, h):
                if not isinstance(h, int) or h >= 2:
                    act.wait_ge(sem("p_T"), 4 * h - 4)
                    act.wait_ge(sem("inv_sum"), h - 1)
                for t in range(NT):
                    b, at, to = SLOT_OF[t]
                    n = (t + 1) * P
                    act.wait_ge(sem("row_max"), 4 * h + (2, 3, 2, 4)[t])
                    act.activation(PR[p][:, to:to + n], bank(b)[:, at:at + n], ACT.Exp, bias=stat[:, 16 + t:17 + t],
                                   accum_out=stat[:, 32 + 4 * p + t:33 + 4 * p + t]).then_inc(sem("probs"), 1)

            def head_pt(t, h):
                act.wait_ge(sem("p_T"), 4 * h + t + 1)
                wait(act, "o_done", 4 * h + t - 1)
                act.activation(PT[:, PT_AT[t]:PT_AT[t] + (t + 1) * P], bank(7)[:, 0:(t + 1) * P], ACT.Copy)\
                    .then_inc(sem("pt_act"), 1)

            norm_squares(0)
            norm_turned(0)
            act.wait_ge(sem("mk_full"), 1)
            act.activation(MK[:, 0, :], bank(2)[:, 0:M], ACT.Copy).then_inc(sem("mem_ready"), 1)
            act.wait_ge(sem("mk_full"), 2)
            act.activation(MK[:, 1, :], bank(3)[:, 0:M], ACT.Copy).then_inc(sem("mem_ready"), 1)
            act.wait_ge(sem("rang_ready"), 1)
            act.activation(trig, rang, ACT.Sin).then_inc(sem("trig_ready"), 1)
            norm_squares(1)
            norm_turned(1)
            for t in range(NT):
                act.wait_ge(sem("z_full"), 2 * t + 1)
                act.activation(ZS[:, t, 0:ZA], bank(2 + 2 * (t % 2))[:, 0:ZA], ACT.Copy).then_inc(sem("z_key"), 1)
            for t in range(NT):
                act.wait_ge(sem("z_key"), t + 1)
                act.activation(PR[0][:, 0:QR], ZS[:, t, 0:QR], ACT.Square, accum_out=stat[:, 24 + t:25 + t])\
                    .then_inc(sem("lat_squares"), 1)
                act.wait_ge(sem("lat_squares"), 2 * t + 1)
                act.activation(PR[0][:, 0:KVR], ZS[:, t, QR:QR + KVR], ACT.Square, accum_out=stat[:, 28 + t:29 + t])\
                    .then_inc(sem("lat_squares"), 1)
                act.wait_ge(sem("lat_squares"), 2 * t + 2)
            act.wait_ge(sem("lat_var"), 2)
            act.activation(stat[:, 32:40], stat[:, 24:32], ACT.Sqrt).then_inc(sem("lat_root"), 1)
            for k in range(KQ):
                act.wait_ge(sem("lat_T"), k + 1)
                act.activation(QLT[:, k, :], bank(k), ACT.Copy, scale=gq[:, k:k + 1]).then_inc(sem("lat_ready"), 1)
            act.wait_ge(sem("lat_T"), 3)
            act.activation(KVT, bank(2), ACT.Copy, scale=gkv[:, 0:1]).then_inc(sem("lat_ready"), 1)
            for t in range(NT):
                act.wait_ge(sem("v_full"), 2 * t + 1)
                act.activation(V[:, t, 0:MW // 2], bank(0)[:, 0:MW // 2], ACT.Copy).then_inc(sem("v_act"), 1)
            cross_attention(0)
            act.wait_ge(sem("xo_full"), XHEADS)
            def head_step(p, h, before):
                head_exp(p, h)
                if before is not None:
                    head_pt(1, before)
                if not isinstance(h, int):
                    head_nope(1 - p, act.snap(h + 1))
                elif h + 1 < H:
                    head_nope(1 - p, h + 1)
                if before is not None:
                    head_pt(3, before)

            head_nope(0, 0)
            head_step(0, 0, None)
            head_step(1, 1, 0)
            with act.Fori(0, H // 2 - 2) as i:
                for p in range(2):
                    head_step(p, act.snap(2 * i + (2 + p)), act.snap(2 * i + (1 + p)))
            head_step(0, H - 2, H - 3)
            head_step(1, H - 1, H - 2)
            head_pt(1, H - 1)
            head_pt(3, H - 1)
            mix_turned(0)

            def experts(l):

                def split_gate_up(u, e, lap):
                    u, b = u % RING, u % 2
                    act.wait_ge(sem(f"gu_in_{u}"), 32 * lap + 32)
                    wait(act, "gu_full", e - 1)
                    for c in range(4):
                        act.activation(chunk(GU_HI[:, b, :], c), chunk(WE[:, u, 0:GU], c), ACT.Copy)\
                            .then_inc(sem("gu_hi"), 1)

                def split_down(u, e, lap):
                    u, b = u % RING, u % 2
                    act.wait_ge(sem(f"down_in_{u}"), 16 * lap + 16)
                    wait(act, "y_full", e - 1)
                    for k in range(KF):
                        act.activation(DOWN_HI[:, b, k * D:(k + 1) * D], WE[:, u, GU + k * D:GU + (k + 1) * D],
                                       ACT.Copy).then_inc(sem("down_hi"), 1)

                def gate(u, e):
                    b = u % 2
                    act.wait_ge(sem("gu_full"), e + 1)
                    wait(act, "at_full", e - 1)
                    act.activation(SG[0:SLOTS, b, :], bank(2 + b)[0:SLOTS, 0:FE], ACT.Silu).then_inc(sem("sg_ready"), 1)

                def rows_hi(u, e):
                    b = u % 2
                    act.wait_ge(sem("xg_full"), e + 1)
                    wait(act, "gu_full", e - 1)
                    act.activation(XGT[:, b, 0, :], bank(b), ACT.Copy).then_inc(sem("x_hi"), 1)

                def hidden_hi(u, e):
                    b = u % 2
                    act.wait_ge(sem("at_full"), e + 1)
                    wait(act, "y_full", e - 1)
                    act.activation(AT[:, b, 0, :], bank(4 + b)[:, 0:KF * SLOTS], ACT.Copy).then_inc(sem("a_hi"), 1)

                def rows_out(u, e, turn):
                    b = u % 2
                    act.wait_ge(sem("y_full"), e + 1)
                    wait(act, f"scattered{l}_{b}", 16 * turn)
                    act.activation(YS[0:SLOTS, b, 0:D // 2], bank(6)[0:SLOTS, :], ACT.Copy).then_inc(sem("ys_act"), 1)

                def step(u, e, lap, turn, before, after, after_lap):
                    if after is not None:
                        split_gate_up(u + 1, after, after_lap)
                    gate(u, e)
                    if after is not None:
                        rows_hi(u + 1, after)
                    split_down(u, e, lap)
                    if before is not None:
                        rows_out(u - 1, before, turn)
                    hidden_hi(u, e)

                split_gate_up(0, 0, 0)
                rows_hi(0, 0)
                act.wait_ge(sem("xn_out"), 16 * NT * (l + 1))
                for e in range(RING):
                    step(e, e, 0, (e - 1) // 2, e - 1 if e else None, e + 1, (e + 1) // RING)
                with act.Fori(0, E // RING - 2) as i:
                    for u in range(RING):
                        step(u + RING, act.snap(RING * i + (RING + u)), act.snap(i + 1),
                             act.snap(2 * i + (RING + u - 1) // 2), act.snap(RING * i + (RING + u - 1)),
                             act.snap(RING * i + (RING + u + 1)), act.snap(i + (RING + u + 1) // RING))
                for e in range(E - RING, E):
                    step(e, e, e // RING, (e - 1) // 2, e - 1, e + 1 if e + 1 < E else None, (e + 1) // RING)
                rows_out(E - 1, E - 1, (E - 1) // 2)
                act.wait_ge(sem("extra_ready"), l + 1)
                rounds = act.value_load(extra[0:1, 0:1], min_val=0, max_val=ROUNDS - 1)
                with act.If(rounds > 0):
                    with act.Fori(0, rounds) as r:
                        with act.Fori(0, E // RING) as q:
                            for u in range(RING):
                                e = act.snap(E * r + RING * q + (E + u))
                                lap = act.snap(E // RING * r + q + E // RING)
                                split_gate_up(u, e, lap)
                                rows_hi(u, e)
                                gate(u, e)
                                split_down(u, e, lap)
                                hidden_hi(u, e)
                                rows_out(u, e, act.snap(E // 2 * r + 2 * q + (E + u) // 2))

            def router(l):
                act.wait_ge(sem("group_logits"), l + 1)
                act.activation(EG, LS, ACT.Exp).then_inc(sem("group_exp"), 1)
                act.wait_ge(sem("second"), l + 1)
                act.activation(small[:, 4:8], small[:, 0:4], ACT.Exp).then_inc(sem("second_exp"), 1)

            norm_squares(2)
            norm_turned(2)
            router(0)
            experts(0)
            norm_squares(3)
            norm_turned(3)
            for t in range(NT):
                act.wait_ge(sem("zp_full"), 2 * t + 1)
                act.activation(U[:, t, 0:512], bank(2 + 2 * (t % 2)), ACT.Copy).then_inc(sem("u_act"), 1)
            act.wait_ge(sem("qcT_full1"), 1)
            act.activation(QCT1[:, 0, :], bank(0), ACT.Copy).then_inc(sem("qct_act"), 1)
            for j in range(0, 2 * len(WINDOWS), 2):
                act.wait_ge(sem("d_full"), j + 1)
                act.activation(dT[0:HW, j, :], bank(6)[0:HW, :], ACT.Copy, scale=1.0 / WINDOWS[j // 2])\
                    .then_inc(sem("d_act"), 1)
            cross_attention(1)
            mix_turned(1)
            norm_squares(4)
            norm_turned(4)
            router(1)
            experts(1)
            norm_squares(5)

        @block.vector
        def _(dve):
            steps = [0]

            def link(ins):
                steps[0] += 1
                ins.then_inc(sem("dve_step"), 1)
                dve.wait_ge(sem("dve_step"), steps[0])

            def norm_scale(n):
                nt = NORM_TILES[n]
                src = norm_source(n)
                dve.wait_ge(sem("squares"), TILES[n] + nt)
                dve.tensor_scalar(stat[:, 4:4 + nt], stat[:, 0:nt], 1.0 / D, EPS, ALU.mult, ALU.add)\
                    .then_inc(sem("var"), 1)
                dve.wait_ge(sem("root"), n + 1)
                link(dve.reciprocal(stat[:, 12:12 + nt], stat[:, 8:8 + nt]))
                if n == 5:
                    dve.wait_ge(sem("gfin_in"), 16)
                if n in (2, 4):
                    dve.wait_ge(sem("gain_in"), 16 * (n // 2))
                for t in range(nt):
                    if n == 5:
                        dve.scalar_tensor_tensor(out=XN[:, t, :], in0=X[:, t, :], scalar=stat[:, 12 + t:13 + t],
                                                 in1=gfin, op0=ALU.mult, op1=ALU.mult).then_inc(sem("fin"), 1)
                    elif n in (2, 4):
                        dve.scalar_tensor_tensor(out=XN[:, t, :], in0=X[:, t, :], scalar=stat[:, 12 + t:13 + t],
                                                 in1=gain, op0=ALU.mult, op1=ALU.mult).then_inc(sem("xn"), 1)
                    else:
                        dve.tensor_scalar(XN[:, t, :], src[:, t, :], stat[:, 12 + t:13 + t], None, ALU.mult)\
                            .then_inc(sem("xn"), 1)

            def norm_turned(n):
                width = NORM_TILES[n] * P
                for k in range(1, KD, 2):
                    dve.wait_ge(sem("tok_T"), KD * n + k + 1)
                    if k == 1:
                        dve.wait_ge(sem("small_in"), 16 * 10)
                    g = 1.0 if n in (2, 4) else GN[:, (n + 1) // 2, k:k + 1]
                    dve.tensor_scalar(ht_of(n)[:, k, :], bank(1)[:, 0:width], g, None, ALU.mult)\
                        .then_inc(sem("hT_dve"), 1)

            def cross_attention(l):
                XPT = XPT0 if l == 0 else XPT1

                def maxima(h):
                    p = h % 2
                    if h >= 2:
                        dve.wait_ge(sem("x_exp"), NT * (XHEADS * l + h - 1))
                    for j in range(2):
                        dve.wait_ge(sem("xs_full"), 2 * XHEADS * l + 2 * h + j + 1)
                        at = 24 + 4 * p + 2 * j
                        dve.tensor_reduce(stat[:, at:at + 2], bank(2 * p + j, 2, M), AX.X, ALU.max, negate=True)\
                            .then_inc(sem("x_max"), 1)

                maxima(0)
                maxima(1)
                for h in range(XHEADS):
                    p = h % 2
                    dve.wait_ge(sem("x_exp"), NT * (XHEADS * l + h + 1))
                    dve.reciprocal(stat[:, 40 + 4 * p:44 + 4 * p], stat[:, 32 + 4 * p:36 + 4 * p])\
                        .then_inc(sem("x_inv"), 1)
                    if h + 2 < XHEADS:
                        maxima(h + 2)
                    dve.wait_ge(sem("xp_T"), MT * (XHEADS * l + h) + 2)
                    if h >= 1:
                        dve.wait_ge(sem("xo_full"), XHEADS * l + h)
                    dve.tensor_copy(XPT[:, 1, :], bank(5)).then_inc(sem("xpt_dve"), 1)
                    dve.wait_ge(sem("x_inv"), XHEADS * l + h + 1)
                    dve.wait_ge(sem("xo_full"), XHEADS * l + h + 1)
                    r = stat[:, 40 + 4 * p:44 + 4 * p].rearrange("p (t a) -> p t a", a=1)
                    dve.tensor_tensor(XN[:, :, MW + h * XD:MW + (h + 1) * XD], bank(6 + p, NT, XD),
                                      wide(r, P, NT, XD), ALU.mult).then_inc(sem("xmix"), 1)

            def mix_turned(l):
                for k in range(1, KD, 2):
                    dve.wait_ge(sem("mixT_full"), KD * l + k + 1)
                    dve.tensor_copy(hT[:, k, :], bank(1)).then_inc(sem("mixT_dve"), 1)

            def residual(l):
                for t in range(NT):
                    for j in range(2):
                        dve.wait_ge(sem("o_full"), 2 * NT * l + 2 * t + j + 1)
                        part = X[:, t, j * 512:(j + 1) * 512]
                        dve.tensor_tensor(part, bank(2 + (2 * t + j) % 4), part, ALU.add).then_inc(sem("o_added"), 1)

            def router(l):
                dve.wait_ge(sem("router_full"), l + 1)
                if l == 0:
                    dve.wait_ge(sem("constants"), 4)
                logits = bank(6, NT, NR)
                b = bias_r[:, l, :].rearrange("p (a n) -> p a n", a=1)
                link(dve.tensor_tensor(LG, logits, wide(b, P, NT, NR), ALU.add))

                def col(at, n=1):
                    return small[:, at:at + NT].rearrange("p (t a) -> p t a", a=1)

                def first_of(best_of, n, out_):
                    w = tie[:, 0:n].rearrange("p (a n) -> p a n", a=1)
                    link(dve.scalar_tensor_tensor(out=SC[:, :, 0:n], in0=best_of, scalar=0.0, in1=wide(w, P, NT, n),
                                                  op0=ALU.is_equal, op1=ALU.mult))
                    link(dve.tensor_reduce(small[:, 16:20], SC[:, :, 0:n], AX.X, ALU.max))
                    link(dve.tensor_tensor(out_, SC[:, :, 0:n], wide(col(16), P, NT, n), ALU.is_equal))

                link(dve.tensor_reduce(small[:, 8:12], LG[:, :, 0:GROUPS], AX.X, ALU.max))
                dve.tensor_tensor(LS, LG[:, :, 0:GROUPS], wide(col(8), P, NT, GROUPS), ALU.subtract)\
                    .then_inc(sem("group_logits"), 1)
                dve.wait_ge(sem("group_logits"), l + 1)
                first_of(LS, GROUPS, OG)

                def by_group(ap):
                    return ap.rearrange("p t (g j) -> p (t g) j", g=GROUPS)

                def og():
                    return OG.rearrange("p t (g a) -> p (t g) a", a=1)

                link(dve.tensor_copy(LE, LG[:, :, GROUPS:]))
                link(dve.tensor_tensor(by_group(LE), by_group(LE), wide(og(), P, NT * GROUPS, PER_GROUP), ALU.mult))
                link(dve.tensor_reduce(SEL, LE.rearrange("p t (g j) -> p t j g", g=GROUPS), AX.X, ALU.add))
                link(dve.tensor_reduce(small[:, 8:12], SEL, AX.X, ALU.max))
                link(dve.tensor_tensor(SEL, SEL, wide(col(8), P, NT, PER_GROUP), ALU.subtract))
                first_of(SEL, PER_GROUP, O1)
                link(dve.scalar_tensor_tensor(out=SEL, in0=O1, scalar=NEG_INF, in1=SEL, op0=ALU.mult, op1=ALU.add))
                dve.tensor_reduce(small[:, 0:4], SEL, AX.X, ALU.max).then_inc(sem("second"), 1)
                dve.wait_ge(sem("second"), l + 1)
                link(dve.tensor_tensor(SEL, SEL, wide(col(0), P, NT, PER_GROUP), ALU.subtract))
                first_of(SEL, PER_GROUP, O2)
                for o, a in ((O1, A1), (O2, A2)):
                    for t in range(NT):
                        g = OG[:, t, :].rearrange("p (g a) -> p g a", a=1)
                        j = o[:, t, :].rearrange("p (a j) -> p a j", a=1)
                        ins = dve.tensor_tensor(a[:, t, :].rearrange("p (g j) -> p g j", g=GROUPS),
                                                wide(g, P, GROUPS, PER_GROUP), wide(j, P, GROUPS, PER_GROUP), ALU.mult)
                link(ins)
                dve.tensor_tensor(AB, A1, A2, ALU.add).then_inc(sem("assigned"), 1)
                dve.wait_ge(sem("group_exp"), l + 1)
                link(dve.tensor_reduce(small[:, 12:16], EG, AX.X, ALU.add))
                dve.wait_ge(sem("second_exp"), l + 1)
                link(dve.scalar_tensor_tensor(out=small[:, 20:24], in0=small[:, 4:8], scalar=1.0, in1=small[:, 12:16],
                                              op0=ALU.add, op1=ALU.mult))
                link(dve.reciprocal(wtok[:, 0, :], small[:, 20:24]))
                link(dve.tensor_tensor(wtok[:, 1, :], wtok[:, 0, :], small[:, 4:8], ALU.mult))
                dve.wait_ge(sem("ranks_full"), l + 1)
                ie = iota_e[:, :].rearrange("p (a e) -> p a e", a=1)
                link(dve.scalar_tensor_tensor(out=POS, in0=bank(7, NT, E), scalar=float(E), in1=wide(ie, P, NT, E),
                                              op0=ALU.mult, op1=ALU.add))
                for j, a in enumerate((A1, A2)):
                    link(dve.tensor_tensor(PM, POS, a, ALU.mult))
                    with nc.allow_low_precision(reason="small whole numbers"):
                        dve.tensor_reduce(slot_pos[:, j * NT:(j + 1) * NT], PM, AX.X, ALU.add)\
                            .then_inc(sem("slot_pos_ready"), 1)
                    dve.wait_ge(sem("slot_pos_ready"), 2 * l + j + 1)
                link(dve.tensor_reduce(small[:, 24:25], banks[7][:, NT * E:(NT + 1) * E], AX.X, ALU.max))
                link(dve.tensor_scalar(small[:, 32:32 + ROUNDS - 1], thresh[:, :], small[:, 24:25], None, ALU.is_lt))
                with nc.allow_low_precision(reason="small whole numbers"):
                    dve.tensor_reduce(extra[:, 0:1], small[:, 32:32 + ROUNDS - 1], AX.X, ALU.add)\
                        .then_inc(sem("extra_ready"), 1)
                split_gate_up(0, 0)
                dve.wait_ge(sem("sidx_in"), 16 * (l + 1))
                link(dve.tensor_scalar(CF[0:SLOTS, :], SIDX[0:SLOTS, :], float(S), -float(S), ALU.is_ge, ALU.mult))
                dve.tensor_tensor(GIDX[0:SLOTS, :], SIDX[0:SLOTS, :], CF[0:SLOTS, :], ALU.add)\
                    .then_inc(sem("gidx_ready"), 1)

            def split_gate_up(u, e):
                u, b = u % RING, u % 2
                for c in range(4):
                    dve.wait_ge(sem("gu_hi"), 4 * e + c + 1)
                    w = chunk(WE[:, u, 0:GU], c)
                    dve.tensor_tensor(chunk(W_LO[u][:, 0:GU], c), w, chunk(GU_HI[:, b, :].bitcast(F32), c), ALU.subtract)\
                        .then_inc(sem("gu_lo"), 1)

            def experts(l):

                def split_down(u, e):
                    u, b = u % RING, u % 2
                    for k in range(KF):
                        dve.wait_ge(sem("down_hi"), KF * e + k + 1)
                        at = slice(GU + k * D, GU + (k + 1) * D)
                        dve.tensor_tensor(W_LO[u][:, at], WE[:, u, at], DOWN_HI[:, b, k * D:(k + 1) * D].bitcast(F32),
                                          ALU.subtract).then_inc(sem("down_lo"), 1)

                def rows_lo(u, e):
                    b = u % 2
                    dve.wait_ge(sem("x_hi"), e + 1)
                    dve.tensor_tensor(XGT[:, b, 1, :], bank(b), XGT[:, b, 0, :].bitcast(F32), ALU.subtract)\
                        .then_inc(sem("x_lo"), 1)

                def hidden(u, e):
                    b = u % 2
                    dve.wait_ge(sem("sg_ready"), e + 1)
                    dve.tensor_tensor(SG[0:SLOTS, b, :], bank(2 + b)[0:SLOTS, FE:2 * FE], SG[0:SLOTS, b, :], ALU.mult)\
                        .then_inc(sem("a_ready"), 1)

                def hidden_lo(u, e):
                    b = u % 2
                    dve.wait_ge(sem("a_hi"), e + 1)
                    dve.tensor_tensor(AT[:, b, 1, :], bank(4 + b)[:, 0:KF * SLOTS], AT[:, b, 0, :].bitcast(F32),
                                      ALU.subtract).then_inc(sem("a_lo"), 1)

                def rows_out(u, e, turn):
                    b = u % 2
                    dve.wait_ge(sem("y_full"), e + 1)
                    wait(dve, f"scattered{l}_{b}", 16 * turn)
                    dve.tensor_copy(YS[0:SLOTS, b, D // 2:], bank(7)[0:SLOTS, :]).then_inc(sem("ys_dve"), 1)

                def step(u, e, turn, before, after):
                    if after is not None:
                        split_gate_up(u + 1, after)
                    hidden(u, e)
                    if after is not None:
                        rows_lo(u + 1, after)
                    split_down(u, e)
                    if before is not None:
                        rows_out(u - 1, before, turn)
                    hidden_lo(u, e)

                rows_lo(0, 0)
                for e in range(RING):
                    step(e, e, (e - 1) // 2, e - 1 if e else None, e + 1)
                with dve.Fori(0, E // RING - 2) as i:
                    for u in range(RING):
                        step(u + RING, dve.snap(RING * i + (RING + u)), dve.snap(2 * i + (RING + u - 1) // 2),
                             dve.snap(RING * i + (RING + u - 1)), dve.snap(RING * i + (RING + u + 1)))
                for e in range(E - RING, E):
                    step(e, e, (e - 1) // 2, e - 1, e + 1 if e + 1 < E else None)
                rows_out(E - 1, E - 1, (E - 1) // 2)
                dve.wait_ge(sem("extra_ready"), l + 1)
                rounds = dve.value_load(extra[0:1, 0:1], min_val=0, max_val=ROUNDS - 1)
                with dve.If(rounds > 0):
                    with dve.Fori(0, rounds) as r:
                        with dve.Fori(0, E // RING) as q:
                            for u in range(RING):
                                e = dve.snap(E * r + RING * q + (E + u))
                                split_gate_up(u, e)
                                rows_lo(u, e)
                                hidden(u, e)
                                split_down(u, e)
                                hidden_lo(u, e)
                                rows_out(u, e, dve.snap(E // 2 * r + 2 * q + (E + u) // 2))
                for t in range(NT):
                    dve.wait_ge(sem(f"yl_in_{t}"), 32 * (l + 1))
                    for j in range(2):
                        ins = dve.scalar_tensor_tensor(
                            out=X[:, t, :], in0=YL[t][:, j, :], scalar=wtok[:, j, t:t + 1],
                            in1=X[:, t, :], op0=ALU.mult, op1=ALU.add)
                        if j == 0:
                            link(ins)
                    ins.then_inc(sem("x_moe"), 1)

            def rope(src, dst, scratch):
                lo, hi = slice(NOPE, QKD), slice(QKD, P)
                a = scratch
                return (dve.tensor_tensor(a[lo, :], src[hi, :], TBL[hi, :], ALU.mult),
                        dve.tensor_tensor(dst[lo, :], src[lo, :], TBL[lo, :], ALU.mult))

            norm_scale(0)
            norm_turned(0)
            for c in range(MT):
                dve.wait_ge(sem("mv_full"), c + 1)
                dve.tensor_copy(MV[:, c, :], bank(4 + c)[:, 0:XW]).then_inc(sem("mv_ready"), 1)
            two_pi = 2 * np.pi
            c1 = 6.28125
            c2 = float(np.float32(np.round((two_pi - c1) * 2 ** 21) / 2 ** 21))
            c3 = float(np.float32(two_pi - c1 - c2))
            MAGIC = 1.5 * 2 ** 23
            dve.wait_ge(sem("small_in"), 16 * 10)
            dve.wait_ge(sem("constants"), 2)
            link(dve.tensor_copy(posf, posi))
            p3 = posf.rearrange("p (t a) -> p t a", a=1)
            f3 = freq.rearrange("p (a i) -> p a i", a=1)
            link(dve.tensor_tensor(ang, wide(p3, P, NT, HALF), wide(f3, P, NT, HALF), ALU.mult))
            flat = ang.rearrange("p t i -> p (t i)")
            for j, shift in ((0, 0.25), (1, 0.0)):
                link(dve.tensor_scalar(turns[:, j, :], flat, float(np.float32(1 / two_pi)), shift, ALU.mult, ALU.add))
                link(dve.tensor_scalar(turns[:, j, :], turns[:, j, :], MAGIC, None, ALU.add))
                link(dve.tensor_scalar(turns[:, j, :], turns[:, j, :], MAGIC, None, ALU.subtract))
                link(dve.scalar_tensor_tensor(out=rang[:, j, :], in0=turns[:, j, :], scalar=-c1, in1=flat,
                                              op0=ALU.mult, op1=ALU.add))
                link(dve.scalar_tensor_tensor(out=rang[:, j, :], in0=turns[:, j, :], scalar=-c2, in1=rang[:, j, :],
                                              op0=ALU.mult, op1=ALU.add))
                link(dve.scalar_tensor_tensor(out=rang[:, j, :], in0=turns[:, j, :], scalar=-c3, in1=rang[:, j, :],
                                              op0=ALU.mult, op1=ALU.add))
                if j == 0:
                    link(dve.tensor_scalar(rang[:, j, :], rang[:, j, :], float(np.float32(np.pi / 2)), None, ALU.add))
            lim = float(np.nextafter(np.float32(np.pi), np.float32(0)))
            dve.tensor_scalar(rang, rang, lim, -lim, ALU.min, ALU.max).then_inc(sem("rang_ready"), 1)
            dve.wait_ge(sem("trig_ready"), 1)
            dve.wait_ge(sem("constants"), 3)
            cos = trig[:, 0, :].rearrange("p (t i) -> p t i", t=NT)
            sin = trig[:, 1, :].rearrange("p (t i) -> p t i", t=NT)
            for at, src, s in ((NOPE, cos, 1.0), (NOPE + HALF, cos, 1.0), (QKD, sin, -1.0), (QKD + HALF, sin, 1.0)):
                dve.tensor_scalar(tbl_tok[:, :, at:at + HALF], src, s, None, ALU.mult).then_inc(sem("tbl_ready"), 1)
            norm_scale(1)
            norm_turned(1)
            for t in range(NT):
                dve.wait_ge(sem("z_full"), 2 * t + 2)
                dve.tensor_scalar(ZS[:, t, ZA:ZW], bank(3 + 2 * (t % 2))[:, 0:XW], XSCALE, None, ALU.mult)\
                    .then_inc(sem("z_xq"), 1)
            dve.wait_ge(sem("tblT_full"), 1)
            link(dve.tensor_copy(TBL[NOPE:P, :], bank(7)[NOPE:P, :]))
            dve.wait_ge(sem("lat_squares"), 2 * NT)
            dve.tensor_scalar(stat[:, 24:28], stat[:, 24:28], 1.0 / QR, EPS, ALU.mult, ALU.add).then_inc(sem("lat_var"), 1)
            dve.tensor_scalar(stat[:, 28:32], stat[:, 28:32], 1.0 / KVR, EPS, ALU.mult, ALU.add).then_inc(sem("lat_var"), 1)
            dve.wait_ge(sem("lat_root"), 1)
            link(dve.reciprocal(stat[:, 40:48], stat[:, 32:40]))
            link(dve.tensor_scalar(stat[:, 40:44], stat[:, 40:44], QSCALE, None, ALU.mult))
            for t in range(NT):
                for a, b, c in ((0, QR, 40), (QR, QR + KVR, 44)):
                    dve.tensor_scalar(ZS[:, t, a:b], ZS[:, t, a:b], stat[:, c + t:c + t + 1], None, ALU.mult)\
                        .then_inc(sem("lat_normed"), 1)
            for m in range(2):
                dve.wait_ge(sem("lat_T"), 4 + m)
                dve.tensor_copy(QCT0[:, m, :], bank(3 + m)).then_inc(sem("qct0"), 1)
            dve.wait_ge(sem("lat_T"), 6)
            for s in range(2):
                for ins in rope(bank(5), kT[s], qT[s]):
                    link(ins)
                ins = dve.tensor_tensor(kT[s][NOPE:QKD, :], kT[s][NOPE:QKD, :], qT[s][NOPE:QKD, :], ALU.add)
                if s == 0:
                    link(ins)
                else:
                    ins.then_inc(sem("rope_done"), 1)
            for t in range(NT):
                dve.wait_ge(sem("v_full"), 2 * t + 2)
                dve.tensor_copy(V[:, t, MW // 2:], bank(1)[:, 0:MW // 2]).then_inc(sem("v_dve"), 1)
            cross_attention(0)

            def head_rope(s, h):
                dve.wait_ge(sem("q_full"), h + 1)
                wait(dve, "scores_full", 3 * h)
                for ins in rope(bank(4), qT[s], rope_scratch):
                    ins.then_inc(sem("q_rot"), 1)
                dve.wait_ge(sem("q_rot"), 2 * h + 2)
                dve.tensor_tensor(qT[s][NOPE:QKD, :], qT[s][NOPE:QKD, :], rope_scratch[NOPE:QKD, :], ALU.add)\
                    .then_inc(sem("q_rope"), 1)

            SLOT_OF = [(1, 0, 1), (2, 0, 2), (1, 128, 1), (0, 0, 3)]

            def head_max(h):
                wait(dve, "probs", 4 * h)
                for t in (0, 2, 1, 3):
                    b, at, n_full = SLOT_OF[t]
                    dve.wait_ge(sem("scores_full"), 3 * h + n_full)
                    dve.tensor_reduce(stat[:, 16 + t:17 + t], bank(b)[:, at:at + (t + 1) * P], AX.X, ALU.max,
                                      negate=True).then_inc(sem("row_max"), 1)

            def head_pt(t, h):
                dve.wait_ge(sem("p_T"), 4 * h + t + 1)
                wait(dve, "o_done", 4 * h + t - 3)
                dve.tensor_copy(PT[:, PT_AT[t]:PT_AT[t] + (t + 1) * P], bank(6)[:, 0:(t + 1) * P])\
                    .then_inc(sem("pt_dve"), 1)

            def head_out(p, h, col):
                dve.wait_ge(sem("probs"), 4 * h + 4)
                dve.reciprocal(stat[:, 40:44], stat[:, 32 + 4 * p:36 + 4 * p]).then_inc(sem("inv_sum"), 1)
                dve.wait_ge(sem("inv_sum"), h + 1)
                dve.wait_ge(sem("o_done"), 4 * h + 4)
                r = stat[:, 40:44].rearrange("p (t a) -> p t a", a=1)
                dve.tensor_tensor(XN[:, :, bass.ds(col, VD)], bank(3, NT, VD), wide(r, P, NT, VD), ALU.mult)\
                    .then_inc(sem("mixed"), 1)

            def head_step(p, h, before, col):
                head_max(h)
                if before is not None:
                    head_pt(0, before)
                    head_pt(2, before)
                if not isinstance(h, int):
                    head_rope(1 - p, dve.snap(h + 1))
                elif h + 1 < H:
                    head_rope(1 - p, h + 1)
                if before is not None:
                    head_out(1 - p, before, col)

            head_rope(0, 0)
            head_step(0, 0, None, None)
            head_step(1, 1, 0, 0)
            with dve.Fori(0, H // 2 - 2) as i:
                for p in range(2):
                    head_step(p, dve.snap(2 * i + (2 + p)), dve.snap(2 * i + (1 + p)),
                              dve.snap(2 * VD * i + (1 + p) * VD))
            head_step(0, H - 2, H - 3, (H - 3) * VD)
            head_step(1, H - 1, H - 2, (H - 2) * VD)
            head_pt(0, H - 1)
            head_pt(2, H - 1)
            head_out(1, H - 1, (H - 1) * VD)
            mix_turned(0)
            residual(0)
            norm_scale(2)
            norm_turned(2)
            router(0)
            experts(0)
            norm_scale(3)
            norm_turned(3)
            for t in range(NT):
                b = bank(3 + 2 * (t % 2))
                dve.wait_ge(sem("zp_full"), 2 * t + 2)
                dve.tensor_copy(U[:, t, 512:MW], b[:, 0:MW - 512]).then_inc(sem("u_dve"), 1)
                dve.tensor_scalar(QC[:, t, :], b[:, MW - 512:512], XSCALE, None, ALU.mult).then_inc(sem("u_dve"), 1)
            dve.wait_ge(sem("qcT_full1"), 2)
            dve.tensor_copy(QCT1[:, 1, :], bank(1)).then_inc(sem("qct_dve"), 1)
            dve.wait_ge(sem("band_sums"), 1)
            link(dve.reciprocal(ramp, ramp))
            for g, w in enumerate(WINDOWS):
                dve.scalar_tensor_tensor(out=band0[:, g, :], in0=ramp[:, g, :], scalar=float(w), in1=band0[:, g, :],
                                         op0=ALU.mult, op1=ALU.mult).then_inc(sem("band_scaled"), 1)
            dve.wait_ge(sem("band_scaled"), len(WINDOWS))
            for g, w in enumerate(WINDOWS):
                for m, n in ((band, P), (band0, 16)):
                    dve.scalar_tensor_tensor(out=m[:, g, 0:n], in0=ident[:, 0:n], scalar=-float(w), in1=m[:, g, 0:n],
                                             op0=ALU.mult, op1=ALU.add).then_inc(sem("bands_ready"), 1)
            for j in range(1, 2 * len(WINDOWS), 2):
                dve.wait_ge(sem("d_full"), j + 1)
                dve.tensor_scalar(dT[0:HW, j, :], bank(7)[0:HW, :], 1.0 / WINDOWS[j // 2], None, ALU.mult)\
                    .then_inc(sem("d_dve"), 1)
            dve.wait_ge(sem("w_mix_in"), 32)
            for t in range(NT):
                for j in range(2):
                    dve.wait_ge(sem("y_pool"), 2 * t + j + 1)
                    c = slice(j * MW // 2, (j + 1) * MW // 2)
                    dve.tensor_tensor(XN[:, t, c], bank(2 + 2 * (t % 2) + j)[:, 0:MW // 2], scale_b[:, c], ALU.mult)\
                        .then_inc(sem("pool_mixed"), 1)
            cross_attention(1)
            mix_turned(1)
            residual(1)
            norm_scale(4)
            norm_turned(4)
            router(1)
            experts(1)
            norm_scale(5)

        @block.tensor
        def _(pe):
            def norm_turned(n):
                for k in range(KD):
                    if k >= 2:
                        pe.wait_ge(sem("hT_act" if k % 2 == 0 else "hT_dve"), KD // 2 * n + k // 2)
                    for t in range(NORM_TILES[n]):
                        if k == 0:
                            pe.wait_ge(sem("xn"), TILES[n] + t + 1)
                        ins = pe.transpose(bank(k % 2)[:, t * P:(t + 1) * P], XN[:, t, k:D:KD], ident[:, :])
                    ins.then_inc(sem("tok_T"), 1)

            def wait_turned(n, k):
                pe.wait_ge(sem("hT_act" if k % 2 == 0 else "hT_dve"), KD // 2 * n + k // 2 + 1)

            def project(n, w, splits, banks_of, full, free):
                for t in range(NT):
                    for j, (a, b) in enumerate(splits):
                        free(t, j)
                        for k in range(KD):
                            if t == 0 and j == 0:
                                wait_turned(n, k)
                            ins = pe.matmul(bank(banks_of(t, j))[:, 0:b - a], hT[:, k, t * P:(t + 1) * P],
                                            w[:, k, a:b], start=(k == 0), stop=(k == KD - 1))
                        ins.then_inc(sem(full), 1)

            def cross_attention(l):
                QCT = QCT0 if l == 0 else QCT1
                XP, XPT = (XP0, XPT0) if l == 0 else (XP1, XPT1)

                def scores(h):
                    at = slice((h % 2) * XD, (h % 2 + 1) * XD)
                    if h >= 2:
                        pe.wait_ge(sem("x_exp"), NT * XHEADS * l + NT * (h - 1))
                    for t in range(NT):
                        ins = pe.matmul(bank(2 * (h % 2) + t // 2)[:, (t % 2) * M:(t % 2 + 1) * M],
                                        QCT[at, h // 2, t * P:(t + 1) * P], MK[at, h // 2, :], start=True, stop=True)
                        if t % 2:
                            ins.then_inc(sem("xs_full"), 1)

                scores(0)
                scores(1)
                for h in range(XHEADS):
                    p = h % 2
                    pe.wait_ge(sem("x_exp"), NT * XHEADS * l + NT * (h + 1))
                    for c in range(MT):
                        if h >= 1:
                            pe.wait_ge(sem("xpt_act" if c == 0 else "xpt_dve"), XHEADS * l + h)
                        for t in range(NT):
                            ins = pe.transpose(bank(4 + c)[:, t * P:(t + 1) * P], XP[p][:, t, c * P:(c + 1) * P],
                                               ident[:, :])
                        ins.then_inc(sem("xp_T"), 1)
                    if h + 2 < XHEADS:
                        scores(h + 2)
                    pe.wait_ge(sem("xpt_act"), XHEADS * l + h + 1)
                    pe.wait_ge(sem("xpt_dve"), XHEADS * l + h + 1)
                    if h >= 2:
                        pe.wait_ge(sem("xmix"), XHEADS * l + h - 1)
                    for t in range(NT):
                        for c in range(MT):
                            ins = pe.matmul(bank(6 + p)[:, t * XD:(t + 1) * XD], XPT[:, c, t * P:(t + 1) * P],
                                            MV[:, c, h * XD:(h + 1) * XD], start=(c == 0), stop=(c == MT - 1))
                    ins.then_inc(sem("xo_full"), 1)

            def output_projection(l):
                pe.wait_ge(sem("xmix"), XHEADS * l + XHEADS)
                for k in range(KD):
                    if k >= 2:
                        pe.wait_ge(sem("mixT_act" if k % 2 == 0 else "mixT_dve"), KD // 2 * l + k // 2)
                    for t in range(NT):
                        ins = pe.transpose(bank(k % 2)[:, t * P:(t + 1) * P], XN[:, t, k:D:KD], ident[:, :])
                    ins.then_inc(sem("mixT_full"), 1)
                pe.wait_ge(sem("w_out_in"), 16 * (l + 1))
                for t in range(NT):
                    for j in range(2):
                        n = 2 * t + j
                        if n >= 4:
                            pe.wait_ge(sem("o_added"), 2 * NT * l + n - 3)
                        for k in range(KD):
                            if n == 0:
                                pe.wait_ge(sem("mixT_act" if k % 2 == 0 else "mixT_dve"), KD // 2 * l + k // 2 + 1)
                            ins = pe.matmul(bank(2 + n % 4), hT[:, k, t * P:(t + 1) * P],
                                            w_out[:, k, j * 512:(j + 1) * 512], start=(k == 0), stop=(k == KD - 1))
                        ins.then_inc(sem("o_full"), 1)

            def router(l):
                pe.wait_ge(sem("wr_in"), 32 * (l + 1))
                for t in range(NT):
                    for k in range(KD):
                        if t == 0:
                            wait_turned(2 * l + 2, k)
                        ins = pe.matmul(bank(6)[:, t * NR:(t + 1) * NR], hT[:, k, t * P:(t + 1) * P], WR[:, k, :],
                                        start=(k == 0), stop=(k == KD - 1))
                ins.then_inc(sem("router_full"), 1)
                pe.wait_ge(sem("assigned"), l + 1)
                for t in range(NT + 1):
                    for s in range(min(t + 1, NT)):
                        ins = pe.matmul(banks[7][:, t * E:(t + 1) * E], (before if s == t else onesb)[:, :], AB[:, s, :],
                                        start=(s == 0), stop=(s == min(t, NT - 1)))
                ins.then_inc(sem("ranks_full"), 1)

            def experts(l):

                def settle():
                    pe.sem_inc(sem("pe_settled"), 1)

                def rows_T(u, e, lap):
                    u, b = u % RING, u % 2
                    pe.wait_ge(sem(f"xg_in{l}_{u}"), 16 * lap + 16)
                    wait(pe, "x_lo", e - 1)
                    settle()
                    for k in range(KD):
                        ins = pe.transpose(bank(b)[:, k * SLOTS:(k + 1) * SLOTS], XG[0:SLOTS, u, k:D:KD],
                                           ident[0:SLOTS, 0:SLOTS])
                    ins.then_inc(sem("xg_full"), 1)

                def gate_up(u, e):
                    u, b = u % RING, u % 2
                    pe.wait_ge(sem("x_lo"), e + 1)
                    wait(pe, "a_ready", e - 1)
                    hi = GU_HI[:, b, :].rearrange("p (j k n) -> p j k n", j=2, k=KD)
                    lo = W_LO[u][:, 0:GU].rearrange("p (j k n) -> p j k n", j=2, k=KD)
                    for k in range(KD):
                        if k % 2 == 0:
                            pe.wait_ge(sem("gu_lo"), 4 * e + k // 2 + 1)
                        rows = slice(k * SLOTS, (k + 1) * SLOTS)
                        for n, (part, w) in enumerate(((0, hi), (0, lo), (1, hi))):
                            ins = pe.matmul(bank(2 + b, 2, FE)[0:SLOTS], XGT[:, b, part, rows], w[:, :, k, :],
                                            start=(k == 0 and n == 0), stop=(k == KD - 1 and n == 2))
                    ins.then_inc(sem("gu_full"), 1)

                def hidden_T(u, e):
                    b = u % 2
                    pe.wait_ge(sem("a_ready"), e + 1)
                    wait(pe, "a_lo", e - 1)
                    settle()
                    for k in range(KF):
                        ins = pe.transpose(bank(4 + b)[:, k * SLOTS:(k + 1) * SLOTS], SG[0:SLOTS, b, k:FE:KF],
                                           ident[0:SLOTS, 0:SLOTS])
                    ins.then_inc(sem("at_full"), 1)

                def down(u, e):
                    u, b = u % RING, u % 2
                    pe.wait_ge(sem("a_lo"), e + 1)
                    pe.wait_ge(sem("down_lo"), KF * e + KF)
                    wait(pe, "ys_act", e)
                    wait(pe, "ys_dve", e)
                    hi = DOWN_HI[:, b, :].rearrange("p (k n) -> p k n", k=KF)
                    lo = W_LO[u][:, GU:].rearrange("p (k n) -> p k n", k=KF)
                    for j in range(2):
                        for k in range(KF):
                            rows = slice(k * SLOTS, (k + 1) * SLOTS)
                            for n, (part, w) in enumerate(((0, hi), (0, lo), (1, hi))):
                                ins = pe.matmul(bank(6 + j)[0:SLOTS, :], AT[:, b, part, rows],
                                                w[:, k, j * 512:(j + 1) * 512], start=(k == 0 and n == 0),
                                                stop=(k == KF - 1 and n == 2))
                    ins.then_inc(sem("y_full"), 1)

                def step(u, e, before, after, after_lap):
                    gate_up(u, e)
                    if after is not None:
                        rows_T(u + 1, after, after_lap)
                    if before is not None:
                        down(u - 1, before)
                    hidden_T(u, e)

                rows_T(0, 0, 0)
                for e in range(RING):
                    step(e, e, e - 1 if e else None, e + 1, (e + 1) // RING)
                with pe.Fori(0, E // RING - 2) as i:
                    for u in range(RING):
                        step(u + RING, pe.snap(RING * i + (RING + u)), pe.snap(RING * i + (RING + u - 1)),
                             pe.snap(RING * i + (RING + u + 1)), pe.snap(i + (RING + u + 1) // RING))
                for e in range(E - RING, E):
                    step(e, e, e - 1, e + 1 if e + 1 < E else None, (e + 1) // RING)
                down(E - 1, E - 1)
                pe.wait_ge(sem("extra_ready"), l + 1)
                rounds = pe.value_load(extra[0:1, 0:1], min_val=0, max_val=ROUNDS - 1)
                with pe.If(rounds > 0):
                    with pe.Fori(0, rounds) as r:
                        with pe.Fori(0, E // RING) as q:
                            for u in range(RING):
                                e = pe.snap(E * r + RING * q + (E + u))
                                lap = pe.snap(E // RING * r + q + E // RING)
                                rows_T(u, e, lap)
                                gate_up(u, e)
                                hidden_T(u, e)
                                down(u, e)

            pe.wait_ge(sem("constants"), 1)
            norm_turned(0)
            for k in range(KD):
                wait_turned(0, k)
            pe.wait_ge(sem("w_mkv_in"), 16)
            for m in range(XW // P):
                for k in range(KD):
                    ins = pe.matmul(bank(2 + m)[:, 0:M], w_mkv[:, k, m * P:(m + 1) * P], memhT[:, k, :],
                                    start=(k == 0), stop=(k == KD - 1))
                ins.then_inc(sem("mk_full"), 1)
            for c in range(MT):
                for k in range(KD):
                    ins = pe.matmul(bank(4 + c)[:, 0:XW], memhT[:, k, c * P:(c + 1) * P], w_mkv[:, k, XW:],
                                    start=(k == 0), stop=(k == KD - 1))
                ins.then_inc(sem("mv_full"), 1)
            pe.wait_ge(sem("tbl_ready"), 4)
            for t in range(NT):
                ins = pe.transpose(bank(7)[:, t * P:(t + 1) * P], tbl_tok[:, t, :], ident[:, :])
            ins.then_inc(sem("tblT_full"), 1)
            norm_turned(1)
            pe.wait_ge(sem("w_mla_in"), 16)

            def z_free(t, j):
                if t == 0:
                    pe.wait_ge(sem("mem_ready"), 2)
                    pe.wait_ge(sem("mv_ready"), 2)
                if t >= 2:
                    pe.wait_ge(sem("z_key" if j == 0 else "z_xq"), t - 1)

            project(1, w_mla, ((0, ZA), (ZA, ZW)), lambda t, j: 2 + 2 * (t % 2) + j, "z_full", z_free)
            pe.wait_ge(sem("z_key"), NT)
            pe.wait_ge(sem("z_xq"), NT)
            pe.wait_ge(sem("lat_normed"), 2 * NT)
            for k in range(KQ):
                for t in range(NT):
                    ins = pe.transpose(bank(k)[:, t * P:(t + 1) * P], ZS[:, t, k:QR:KQ], ident[:, :])
                ins.then_inc(sem("lat_T"), 1)
            for b, at in ((2, QR), (3, ZA), (4, ZA + P)):
                for t in range(NT):
                    ins = pe.transpose(bank(b)[:, t * P:(t + 1) * P], ZS[:, t, at:at + P], ident[:, :])
                ins.then_inc(sem("lat_T"), 1)
            pe.wait_ge(sem("kr_ready"), 3)
            for t in range(NT):
                ins = pe.transpose(bank(5)[:, t * P:(t + 1) * P], kr_tok[:, t, :], ident[:, :])
            ins.then_inc(sem("lat_T"), 1)
            pe.wait_ge(sem("lat_ready"), 3)
            pe.wait_ge(sem("w_qkv_in"), 32)
            wv = w_kv.rearrange("p (h n) -> p h n", h=H)
            for t in range(NT):
                for j in range(2):
                    if t >= 1:
                        pe.wait_ge(sem("v_act" if j == 0 else "v_dve"), t)
                    ins = pe.matmul(bank(j, H // 2, VD), KVT[:, t * P:(t + 1) * P],
                                    wv[:, j * H // 2:(j + 1) * H // 2, NOPE:], start=True, stop=True)
                    ins.then_inc(sem("v_full"), 1)
            pe.wait_ge(sem("v_act"), NT)
            pe.wait_ge(sem("v_dve"), NT)
            pe.wait_ge(sem("qct0"), 2)
            pe.wait_ge(sem("rope_done"), 1)
            cross_attention(0)
            pe.wait_ge(sem("xmix"), XHEADS)

            def head_query(s, h):
                pe.wait_ge(sem("wh_ready"), 4 * h + 4)
                wait(pe, "q_nope", h)
                wait(pe, "q_rope", h)
                for k in range(KQ):
                    ins = pe.matmul(bank(4), wqh[s][:, k, :], QLT[:, k, :], start=(k == 0), stop=(k == KQ - 1))
                ins.then_inc(sem("q_full"), 1)

            def head_key(s, h):
                wait(pe, "k_nope", h)
                pe.matmul(bank(5)[0:NOPE, :], wkh[s], KVT, start=True, stop=True).then_inc(sem("k_full"), 1)

            def head_scores(s, h):
                pe.wait_ge(sem("q_nope"), h + 1)
                pe.wait_ge(sem("k_nope"), h + 1)
                pe.wait_ge(sem("q_rope"), h + 1)
                wait(pe, "probs", 4 * h)
                for b, at, t, done in ((1, 0, 0, 0), (1, 128, 2, 1), (2, 0, 1, 1), (0, 0, 3, 1)):
                    n = (t + 1) * P
                    pe.matmul(bank(b)[:, at:at + n], qT[s][0:QKD, t * P:(t + 1) * P], kT[s][0:QKD, 0:n],
                              start=True, stop=False)
                    ins = pe.matmul(bank(b)[:, at + t * P:at + n], identb[:, :], causal[:, :], start=False, stop=True)
                    if done:
                        ins.then_inc(sem("scores_full"), 1)

            AT_OF = (0, 128, 384, 768)

            def turn(t, p, h):
                pe.wait_ge(sem("probs"), 4 * h + t + 1)
                wait(pe, "pt_dve" if t % 2 == 0 else "pt_act", 2 * h + t // 2)
                for c in range(t + 1):
                    a = AT_OF[t] + c * P
                    ins = pe.transpose(bank(6 + t % 2)[:, c * P:(c + 1) * P], PR[p][:, a:a + P], ident[:, :])
                ins.then_inc(sem("p_T"), 1)

            def product(t, h, col):
                pe.wait_ge(sem("pt_dve" if t % 2 == 0 else "pt_act"), 2 * h + t // 2 + 1)
                if t == 0:
                    wait(pe, "mixed", h)
                for c in range(t + 1):
                    part = PT[:, PT_AT[t] + c * P:PT_AT[t] + (c + 1) * P]
                    ins = pe.matmul(bank(3)[:, t * VD:(t + 1) * VD], part, V[:, c, bass.ds(col, VD)],
                                    start=(c == 0), stop=(c == t))
                ins.then_inc(sem("o_done"), 1)

            def head_step(p, h, after, before, col):
                if h is not None:
                    head_scores(p, h)
                if before is not None:
                    turn(0, 1 - p, before)
                    turn(1, 1 - p, before)
                if after is not None:
                    head_query(1 - p, after)
                if before is not None:
                    turn(2, 1 - p, before)
                if after is not None:
                    head_key(1 - p, after)
                if before is not None:
                    product(0, before, col)
                    product(1, before, col)
                    turn(3, 1 - p, before)
                    product(2, before, col)
                    product(3, before, col)

            head_query(0, 0)
            head_key(0, 0)
            head_step(0, 0, 1, None, None)
            head_step(1, 1, 2, 0, 0)
            with pe.Fori(0, H // 2 - 2) as i:
                for p in range(2):
                    head_step(p, pe.snap(2 * i + (2 + p)), pe.snap(2 * i + (3 + p)), pe.snap(2 * i + (1 + p)),
                              pe.snap(2 * VD * i + (1 + p) * VD))
            head_step(0, H - 2, H - 1, H - 3, (H - 3) * VD)
            head_step(1, H - 1, None, H - 2, (H - 2) * VD)
            head_step(0, None, None, H - 1, (H - 1) * VD)
            pe.wait_ge(sem("mixed"), H)
            output_projection(0)
            norm_turned(2)
            router(0)
            experts(0)
            norm_turned(3)
            pe.wait_ge(sem("w_pool_in"), 16)

            def zp_free(t, j):
                if t >= 2:
                    pe.wait_ge(sem("u_act" if j == 0 else "u_dve"), t - 1 if j == 0 else 2 * (t - 1))

            project(3, w_pool, ((0, 512), (512, D)), lambda t, j: 2 + 2 * (t % 2) + j, "zp_full", zp_free)
            pe.wait_ge(sem("u_act"), NT)
            pe.wait_ge(sem("u_dve"), 2 * NT)
            for m in range(XW // P):
                for t in range(NT):
                    ins = pe.transpose(bank(m)[:, t * P:(t + 1) * P], QC[:, t, m * P:(m + 1) * P], ident[:, :])
                ins.then_inc(sem("qcT_full1"), 1)
            pe.wait_ge(sem("bands_ready"), 2 * len(WINDOWS))
            for j in range(2 * len(WINDOWS)):
                g, b = j // 2, bank(6 + j % 2)[0:HW, :]
                if j >= 2:
                    pe.wait_ge(sem("d_act" if j % 2 == 0 else "d_dve"), j // 2)
                for t in range(NT):
                    lhs = U[:, t, j * HW:(j + 1) * HW]
                    if t == 0:
                        pe.matmul(b[:, 0:16], lhs, band0[:, g, :], start=True, stop=False, skip_group_check=True)
                        pe.matmul(b[:, 16:HALO], lhs, band[:, g, 16:HALO], start=False, stop=False,
                                  skip_group_check=True)
                    else:
                        end = min(S, t * P + HALO)
                        ins = pe.matmul(b[:, t * P:end], lhs, band[:, g, 0:end - t * P], start=False,
                                        stop=(t == NT - 1), skip_group_check=True)
                ins.then_inc(sem("d_full"), 1)
            pe.wait_ge(sem("w_mix_in"), 32)
            pe.wait_ge(sem("d_act"), len(WINDOWS))
            pe.wait_ge(sem("d_dve"), len(WINDOWS))
            for t in range(NT):
                for j in range(2):
                    if t >= 2:
                        pe.wait_ge(sem("pool_mixed"), 2 * (t - 2) + j + 1)
                    for g in range(2):
                        for c in range(2):
                            jj = 2 * (2 * j + g) + c
                            ins = pe.matmul(bank(2 + 2 * (t % 2) + j)[:, g * GW:(g + 1) * GW],
                                            dT[0:HW, jj, t * P:(t + 1) * P], w_mix[0:HW, jj, :],
                                            start=(c == 0), stop=(c == 1))
                    ins.then_inc(sem("y_pool"), 1)
            pe.wait_ge(sem("qct_act"), 1)
            pe.wait_ge(sem("qct_dve"), 1)
            pe.wait_ge(sem("pool_mixed"), 2 * NT)
            cross_attention(1)
            output_projection(1)
            norm_turned(4)
            router(1)
            experts(1)


_INS = ['x', 'mem', 'positions', 'g_mix', 'w_in_mla', 'g_q_lat', 'w_uq', 'g_kv_lat', 'w_ukv', 'w_in_pool',
        'w_pool_mix', 'pool_scale', 'g_mem', 'w_mem_kv', 'w_o', 'g_ffn', 'w_router_group', 'b_router_group',
        'w_router_expert', 'b_router_expert', 'w_expert_gate', 'w_expert_up', 'w_expert_down', 'g_final']


def kernel(**inputs):
    import numpy as _np
    import concourse.bacc as _bacc
    from concourse import mybir as _mybir
    from concourse.bass_utils import run_bass_kernel_spmd as _run

    nc = _bacc.Bacc("TRN2", target_bir_lowering=False, num_devices=1)
    arrays, args = {}, []
    for name in _INS:
        a = _np.ascontiguousarray(inputs[name])
        arrays[f"in_{name}_dram"] = a
        args.append(nc.dram_tensor(f"in_{name}_dram", a.shape, _mybir.dt.from_np(a.dtype), kind="ExternalInput").ap())
    shape = inputs['x'].shape
    out = nc.dram_tensor("out_0_dram", shape, _mybir.dt.float32, kind="ExternalOutput").ap()
    program(nc, *args, out)
    r = _run(nc, [arrays], core_ids=[0])
    return r.results[0]["out_0_dram"]
```

```python
from contextlib import ExitStack

import numpy as np

import concourse.bass as bass
from concourse import mybir

F32 = mybir.dt.float32
F32R = mybir.dt.float32r
BF16 = mybir.dt.bfloat16
I32 = mybir.dt.int32
ALU = mybir.AluOpType
ACT = mybir.ActivationFunctionType
AX = mybir.AxisListType

P = 128
EPS = 1e-6
NEG_INF = -1e30
THETA = 10000.0
WINDOWS = (2, 4, 8, 16)
XHEADS = 4
GROUPS = 4
PER_GROUP = 8
SLOTS = 64
RING = 4
NO_TOKEN = 1 << 20


def program(nc, x, mem, positions, g_mix, w_in_mla, g_q_lat, w_uq, g_kv_lat, w_ukv, w_in_pool, w_pool_mix,
            pool_scale, g_mem, w_mem_kv, w_o, g_ffn, w_router_group, b_router_group, w_router_expert,
            b_router_expert, w_expert_gate, w_expert_up, w_expert_down, g_final, out):
    S, D = x.shape[1:]
    M = mem.shape[1]
    NT, MT, KD = S // P, M // P, D // P
    QR, KVR = g_q_lat.shape[1], g_kv_lat.shape[1]
    XW = w_mem_kv.shape[1] // 2
    XD = XW // XHEADS
    MW = D - XW
    ROPE = w_in_mla.shape[2] - QR - KVR - XW
    HALF = ROPE // 2
    VD = 64
    NOPE = 64
    H = MW // VD
    QKD = NOPE + ROPE
    ZW = w_in_mla.shape[2]
    ZA = QR + KVR + ROPE
    KQ = QR // P
    E = w_expert_gate.shape[1]
    FE = w_expert_gate.shape[3]
    KF = FE // P
    NR = GROUPS + E
    GW = MW // len(WINDOWS)
    HW = GW // 2
    ROUNDS = S // SLOTS
    HALO = P + max(WINDOWS) - 1
    QSCALE = QKD ** -0.5
    XSCALE = XD ** -0.5
    assert (S, D, M, QR, KVR, XD, ROPE, H, E, FE) == (512, 1024, 256, 256, 128, 64, 32, 12, 32, 256)
    inv_freq = (THETA ** (-np.arange(0, ROPE, 2, dtype=np.float64) / ROPE)).astype(np.float32)

    with ExitStack() as ctx:
        place = {}

        def sb(name, shape, dt=F32):
            place[name] = nc.sbuf_base
            return ctx.enter_context(nc.sbuf_tensor(name, shape, dt))

        def over(base, at, name, shape, dt):
            return nc.alloc_sbuf_tensor_at(name, shape, dt, offset=place[base] + 4 * at)

        sems = {}

        def sem(name):
            if name not in sems:
                sems[name] = ctx.enter_context(nc.semaphore(name))
            return sems[name]

        xn_dram = [nc.dram_tensor(f"xn_rows_{l}", (S, D), F32, kind="Internal").ap() for l in range(2)]
        slot_dram = [nc.dram_tensor(f"slot_table_{l}", (S * E, 1), I32, kind="Internal").ap() for l in range(2)]
        y_dram = [nc.dram_tensor(f"expert_rows_{l}", (2 * S, D), F32, kind="Internal").ap() for l in range(2)]

        X = sb("X", [P, NT, D])
        XN = sb("XN", [P, NT, D])
        HT = sb("HT", [P, KD * S])
        WIN = sb("WIN", [P, KD * D])
        WE = sb("WE", [P, RING, 3 * KD * FE])
        T = sb("T", [P, 5376])
        MK = sb("MK", [P, XW // P, M])
        MV = sb("MV", [P, MT, XW])
        WR = sb("WR", [P, KD, NR])
        ident = sb("ident", [P, P])
        identb = sb("identb", [P, P], BF16)
        causal = sb("causal", [P, P], BF16)
        before = sb("before", [P, P], BF16)
        onesb = sb("onesb", [P, P], BF16)
        iota_e = sb("iota_e", [P, E])
        iota_s = sb("iota_s", [P, SLOTS])
        destf = sb("destf", [P, 2 * NT])
        tie = sb("tie", [P, PER_GROUP])
        thresh = sb("thresh", [P, ROUNDS - 1])
        dest = sb("dest", [P, 2 * NT], I32)
        slot_pos = sb("slot_pos", [P, 2 * NT], I32)
        SIDX = sb("SIDX", [P, ROUNDS * E], I32)
        INV = SIDX[:, 0:S * E // P]
        GIDX = sb("GIDX", [P, ROUNDS * E], I32)
        gidx = sb("gidx", [P, RING], I32)
        sidx = sb("sidx", [P, 2], I32)
        extra = sb("extra", [P, 1], I32)
        GN = sb("GN", [P, 3, KD])
        gq = sb("gq", [P, KQ])
        gkv = sb("gkv", [P, 1])
        bias_r = sb("bias_r", [P, 2, NR])
        stat = sb("stat", [P, 64])
        wtok = sb("wtok", [P, 2, NT])

        def view(base, at, *shape):
            n = int(np.prod(shape))
            v = base[:, at:at + n]
            if len(shape) == 2:
                v = v.rearrange("p (a b) -> p a b", a=shape[0])
            if len(shape) == 3:
                v = v.rearrange("p (a b c) -> p a b c", a=shape[0], b=shape[1])
            return v

        hT = view(HT, 0, KD, S)
        WEflat = WE[:, :, :].rearrange("p r n -> p (r n)")
        RB = 3 * KD * FE
        MEM = view(WEflat, 0, MT, D)
        memhT = view(WEflat, MT * D, KD, M)
        w_mkv = view(WEflat, 2 * RB, KD, 2 * XW)
        w_out = view(WEflat, 2 * RB + KD * 2 * XW, KD, D)
        W_HI = over("WIN", 0, "weights_hi", [P, KD, D], F32R)
        POOL_LO = over("WE", 0, "w_pool_lo", [P, KD, D], F32R)
        OUT_LO = over("WE", 2 * RB + KD * 2 * XW, "w_out_lo", [P, KD, D], F32R)
        TOK_HI = over("HT", 0, "tokens_hi", [P, KD, S], F32R)
        TOK_LO = over("T", 0, "tokens_lo", [P, KD, S], F32R)
        w_mla = view(WIN, 0, KD, ZW)
        ZS = view(WIN, KD * ZW, NT, ZW)
        w_q = view(WEflat, RB, KQ, H * QKD)
        w_kv = view(WEflat, RB + 2304, H * 2 * VD)
        QLT = view(WEflat, RB + 3840, KQ, S)
        KVT = view(WEflat, RB + 4864, S)
        TBL = view(WEflat, RB + 5376, S)
        V = view(HT, 0, NT, MW)
        QCT0 = view(HT, NT * MW, XW // P, S)
        rope_scratch = view(WEflat, 0, S)
        PR = [view(T, 0, 1280), view(WEflat, 1536, 1280)]
        PT = view(T, 1280, 2 * S)
        PT_AT = (0, S, P, S)
        qT = [view(T, 2304 + 512 * s, S) for s in range(2)]
        kT = [view(T, 3328 + 512 * s, S) for s in range(2)]
        wqh = [view(T, 4352 + 256 * s, KQ, P) for s in range(2)]
        wkh = [view(T, 4864 + 64 * s, 64) for s in range(2)]
        posf = view(T, 0, NT)
        freq = view(T, 8, HALF)
        ang = view(T, 64, NT, HALF)
        turns = view(T, 128, 2, NT * HALF)
        rang = view(T, 256, 2, NT * HALF)
        trig = view(T, 384, 2, NT * HALF)
        tbl_tok = view(T, 512, NT, P)
        kr_tok = view(T, 1024, NT, P)
        posi = T[:, 1536:1536 + NT].bitcast(I32)
        XP0, XPT0 = (view(T, 0, NT, M), view(WEflat, S, NT, M)), view(T, NT * M, MT, S)
        w_pool = view(WEflat, 0, KD, D)
        U = XN[:, :, 0:MW]
        QC = XN[:, :, MW:]
        band = view(T, NT * D, len(WINDOWS), HALO)
        band0 = view(T, NT * D + len(WINDOWS) * HALO, len(WINDOWS), max(WINDOWS))
        ramp = view(T, NT * D + len(WINDOWS) * (HALO + 16), len(WINDOWS), max(WINDOWS))
        dT = view(HT, 0, 2 * len(WINDOWS), S)
        QCT1 = view(WEflat, RB, XW // P, S)
        XP1 = view(WEflat, RB + 1024, NT, M), view(WEflat, 0, NT, M)
        XPT1 = view(WEflat, RB + 2048, MT, S)
        w_mix = view(WEflat, RB + 3072, 2 * len(WINDOWS), GW)
        scale_b = view(WEflat, RB + 3072 + 8 * GW, MW)
        XG = view(HT, 0, RING, D)
        XGT = over("T", 0, "rows_T", [P, 2, 2, KD * SLOTS], F32R)
        YS = view(T, 2 * D, 2, D)
        SG = view(T, 4 * D, 2, FE)
        AT = over("T", 4 * D + 2 * FE, "hidden_T", [P, 2, 2, KF * SLOTS], F32R)
        GU = 2 * KD * FE
        GU_HI = over("WIN", 0, "gate_up_hi", [P, 2, GU], F32R)
        DOWN_HI = over("XN", 0, "down_hi", [P, 2, KF * D], F32R)
        W_LO = [over("WE", u * RB, f"weights_lo_{u}", [P, RB], F32R) for u in range(RING)]
        CHUNK = 2 * KD * FE // 4
        YL = [view(HT, 0, 2, D), view(HT, 2 * D, 2, D), view(T, 0, 2, D), view(T, 2 * D, 2, D)]
        gain = view(T, 4352, D)
        gfin = view(WIN, 0, D)
        LG = view(T, 0, NT, NR)
        LT = view(T, 2816, S)
        LS = view(T, 256, NT, GROUPS)
        EG = view(T, 272, NT, GROUPS)
        SC = view(T, 288, NT, PER_GROUP)
        OG = view(T, 320, NT, GROUPS)
        LE = view(T, 384, NT, E)
        SEL = view(T, 512, NT, PER_GROUP)
        O1 = view(T, 544, NT, PER_GROUP)
        O2 = view(T, 576, NT, PER_GROUP)
        RH = view(T, 1792, 2, NT * 2, E).rearrange("p j (t v) e -> p j t v e", v=2)
        A1, A2 = (RH[:, j, :, 1, :] for j in range(2))
        RO = view(T, 2304, 2, NT * SLOTS).rearrange("p j (t s) -> p j t s", t=NT)
        POS = view(T, 896, NT, E)
        PM = view(T, 1024, NT, E)
        AB = T[:, 1152:1152 + NT * E // 2].bitcast(BF16).rearrange("p (t e) -> p t e", t=NT)
        small = view(T, 1280, 64)
        CF = view(T, 1536, ROUNDS * E)

        banks = [ctx.enter_context(nc.psum_tensor(f"bank{i}", [P, 512], F32)) for i in range(8)]

        def bank(i, *shape):
            v = banks[i][:, :]
            if shape:
                v = v[:, 0:int(np.prod(shape))].rearrange("p (a b) -> p a b", a=shape[0])
            return v

        def wide(ap, *shape):
            return ap.to_broadcast(list(shape))

        def wait(eng, name, count):
            if not isinstance(count, int) or count > 0:
                eng.wait_ge(sem(name), count)

        def feat(w):
            return w.rearrange("(p k) n -> p (k n)", p=P)

        def row(v):
            return v.rearrange("(a n) -> a n", a=1)

        HALVED = (0, 1, 2, 3, 3)
        TILES = [0, NT] + [MT + NT * n for n in range(1, 5)]
        expert_counts = [f"{name}_{u}" for name in ("gu_in", "down_in") for u in range(RING)]
        expert_counts += ["sidx_in", "gidx_rest", "gidx_set", "sidx_set", "xg_full", "x_hi", "x_lo", "gu_hi",
                          "gu_lo", "down_hi", "down_lo", "gu_full", "sg_ready", "a_ready", "at_full", "a_hi", "a_lo",
                          "y_full", "ys_act", "ys_dve"]
        block = ctx.enter_context(nc.Block())

        @block.sync
        def _(sp):
            for t in range(NT):
                sp.dma_start(X[:, t, :], x[0, t * P:(t + 1) * P, :]).then_inc(sem(f"x_in_{t}"), 16)
            for j, g in enumerate((g_mix[0], g_mem, g_mix[1])):
                sp.dma_start(GN[:, j, :], g.rearrange("(p k) -> p k", p=P)).then_inc(sem("gains_in"), 16)
            sp.dma_start(w_mla.rearrange("p k n -> p (k n)"), feat(w_in_mla[0])).then_inc(sem("w_mla_in"), 16)
            for t in range(MT):
                sp.dma_start(MEM[:, t, :], mem[0, t * P:(t + 1) * P, :]).then_inc(sem("mem_in"), 16)
            sp.dma_start(w_mkv.rearrange("p k n -> p (k n)"), feat(w_mem_kv)).then_inc(sem("w_mkv_in"), 16)
            sp.dma_start(w_kv, w_ukv[0]).then_inc(sem("w_qkv_in"), 16)
            sp.dma_start(w_q.rearrange("p k n -> p (k n)"), feat(w_uq[0])).then_inc(sem("w_qkv_in"), 16)
            sp.dma_start(w_out.rearrange("p k n -> p (k n)"), feat(w_o[0])).then_inc(sem("w_out_in"), 16)
            sp.wait_ge(sem("inv_ready"), 1)
            for l in range(2):
                sp.dma_start(slot_dram[l].rearrange("(p n) a -> p (n a)", p=P), INV).then_inc(sem("slot_cleared"), 16)

            def load_gate_up(l, u, e):
                for j, w in enumerate((w_expert_gate, w_expert_up)):
                    src = w[l, bass.ds(e, 1)].rearrange("a (p k) n -> p (a k n)", p=P)
                    sp.dma_start(WE[:, u, j * KD * FE:(j + 1) * KD * FE], src).then_inc(sem(f"gu_in_{u}"), 16)

            def load_down(l, u, e):
                src = w_expert_down[l, bass.ds(e, 1)].rearrange("a (p k) n -> p (a k n)", p=P)
                sp.dma_start(WE[:, u, GU:], src).then_inc(sem(f"down_in_{u}"), 16)

            for l in range(2):
                if l == 1:
                    sp.wait_ge(sem("moe_done"), 1)
                sp.dma_start(WR[:, :, 0:GROUPS], w_router_group[l].rearrange("(p k) n -> p k n", p=P))\
                    .then_inc(sem("wr_in"), 16)
                sp.dma_start(WR[:, :, GROUPS:], w_router_expert[l].rearrange("(p k) n -> p k n", p=P))\
                    .then_inc(sem("wr_in"), 16)
                if l == 0:
                    sp.wait_ge(sem("mixed"), H)
                else:
                    sp.wait_ge(sem("d_full"), 2 * len(WINDOWS))
                sp.dma_start(gain, row(g_ffn[l]).to_broadcast([P, D])).then_inc(sem("gain_in"), 16)
                sp.wait_ge(sem("xmix"), XHEADS * (l + 1))
                for u in range(2):
                    load_gate_up(l, u, u)
                    load_down(l, u, u)
                for t in range(NT):
                    sp.wait_ge(sem("xn"), TILES[2 * l + 2] + t + 1)
                    sp.dma_start(xn_dram[l][t * P:(t + 1) * P, :], XN[:, t, :]).then_inc(sem("xn_out"), 16)
                for u in range(2, RING):
                    load_gate_up(l, u, u)
                    if u + 1 < RING:
                        load_down(l, u, u)

                def load_ahead(u, e):
                    sp.wait_ge(sem("gu_full"), e + 1 if isinstance(e, int) else sp.snap(e + 1))
                    load_gate_up(l, u, e + RING if isinstance(e, int) else sp.snap(e + RING))
                    if not isinstance(e, int) or e >= 1:
                        sp.wait_ge(sem("y_full"), e)
                    load_down(l, (u - 1) % RING, e + RING - 1 if isinstance(e, int) else sp.snap(e + (RING - 1)))

                for e in range(RING):
                    load_ahead(e, e)
                with sp.Fori(0, E // RING - 2) as i:
                    for u in range(RING):
                        load_ahead(u, sp.snap(RING * i + (RING + u)))
                sp.wait_ge(sem("y_full"), E - RING)
                load_down(l, RING - 1, E - 1)
                sp.wait_ge(sem("extra_ready"), l + 1)
                rounds = sp.value_load(extra[0:1, 0:1], min_val=0, max_val=ROUNDS - 1)
                with sp.If(rounds > 0):
                    sp.wait_ge(sem("slot_scattered"), 16 * 2 * NT * (l + 1))
                    sp.dma_start(SIDX[0:SLOTS, E:].rearrange("s (r e) -> s r e", r=ROUNDS - 1),
                                 slot_dram[l].rearrange("(r s e) a -> s r (e a)", r=ROUNDS, s=SLOTS)[:, 1:, :])\
                        .then_inc(sem("sidx_in"), 16)
                    with sp.Fori(0, rounds) as r:
                        with sp.Fori(0, E // RING) as q:
                            for u in range(RING):
                                e = sp.snap(RING * q + u)
                                sp.wait_ge(sem("y_full"), sp.snap(E * r + RING * q + (E + u - RING + 1)))
                                load_gate_up(l, u, e)
                                load_down(l, u, e)
                if l == 0:
                    used = sp.snap(E * rounds + (E - 2))
                    sp.wait_ge(sem("y_full"), used)
                    sp.dma_start(w_pool.rearrange("p k n -> p (k n)"), feat(w_in_pool[0]))\
                        .then_inc(sem("w_pool_in"), 16)
                sp.wait_ge(sem("moe_done"), l + 1)
                for t in range(NT):
                    for j in range(2):
                        sp.dma_start(YL[t][:, j, :], y_dram[l][j * S + t * P:j * S + (t + 1) * P, :])\
                            .then_inc(sem(f"yl_in_{t}"), 16)
                    if l == 0 and t == NT - 1:
                        sp.dma_start(w_mix[0:HW].rearrange("p (g c) n -> p g c n", c=2),
                                     w_pool_mix[0].rearrange("g (c p) n -> p g c n", c=2)).then_inc(sem("w_mix_in"), 16)
                        sp.dma_start(scale_b, row(pool_scale[0]).to_broadcast([P, MW])).then_inc(sem("w_mix_in"), 16)
                        sp.dma_start(w_out.rearrange("p k n -> p (k n)"), feat(w_o[1])).then_inc(sem("w_out_in"), 16)
                if l == 1:
                    sp.dma_start(gfin, row(g_final).to_broadcast([P, D])).then_inc(sem("gain_in"), 16)
            for t in range(NT):
                sp.wait_ge(sem("fin"), t + 1)
                sp.dma_start(out[0, t * P:(t + 1) * P, :], XN[:, t, :]).then_inc(sem("out_done"), 16)
            sp.wait_ge(sem("out_done"), 16 * NT)

        @block.gpsimd
        def _(pool):
            steps = [0]

            def link(ins):
                steps[0] += 1
                ins.then_inc(sem("pool_step"), 1)
                pool.wait_ge(sem("pool_step"), steps[0])

            def small_loads():
                pool.dma_start(posi, positions[0].rearrange("(t p) -> p t", p=P)).then_inc(sem("positions_in"), 16)
                pool.dma_start(gq[:, :], g_q_lat[0].rearrange("(p k) -> p k", p=P)).then_inc(sem("small_in"), 16)
                pool.dma_start(gkv[:, :], g_kv_lat[0].rearrange("(p k) -> p k", p=P)).then_inc(sem("small_in"), 16)
                for l in range(2):
                    pool.dma_start(bias_r[:, l, 0:GROUPS], row(b_router_group[l]).to_broadcast([P, GROUPS]))\
                        .then_inc(sem("small_in"), 16)
                    pool.dma_start(bias_r[:, l, GROUPS:], row(b_router_expert[l]).to_broadcast([P, E]))\
                        .then_inc(sem("small_in"), 16)

            pool.memset(INV, NO_TOKEN).then_inc(sem("inv_ready"), 1)
            with nc.allow_non_contiguous_dma(reason="a few small vectors, once"):
                small_loads()
            link(pool.memset(ident[:, :], 0.0))
            pool.affine_select(out=ident[:, :], in_=ident[:, :], compare_op=ALU.not_equal, fill=1.0, base=0,
                               pattern=[[-1, P]], channel_multiplier=1).then_inc(sem("constants"), 1)
            for i, f in enumerate(inv_freq):
                last = pool.memset(freq[:, i:i + 1], float(f))
            last.then_inc(sem("constants"), 1)
            link(pool.memset(tbl_tok, 0.0))
            link(pool.memset(kr_tok, 0.0))
            pool.memset(stat[:, 48:49], 0.0).then_inc(sem("constants"), 1)
            link(pool.memset(identb[:, :], 0.0))
            link(pool.affine_select(out=identb[:, :], in_=identb[:, :], compare_op=ALU.not_equal, fill=1.0, base=0,
                                    pattern=[[-1, P]], channel_multiplier=1))
            link(pool.memset(causal[:, :], 0.0))
            link(pool.affine_select(out=causal[:, :], in_=causal[:, :], compare_op=ALU.is_ge, fill=NEG_INF, base=0,
                                    pattern=[[-1, P]], channel_multiplier=1))
            link(pool.memset(onesb[:, :], 1.0))
            link(pool.affine_select(out=before[:, :], in_=onesb[:, :], compare_op=ALU.is_gt, fill=0.0, base=0,
                                    pattern=[[1, P]], channel_multiplier=-1))
            link(pool.iota(iota_e[:, :], pattern=[[1, E]], base=0, channel_multiplier=0,
                           allow_small_or_imprecise_dtypes=True))
            link(pool.iota(iota_s[:, :], pattern=[[1, SLOTS]], base=0, channel_multiplier=0,
                           allow_small_or_imprecise_dtypes=True))
            link(pool.iota(destf[:, :], pattern=[[S, 2], [P, NT]], base=0, channel_multiplier=1,
                           allow_small_or_imprecise_dtypes=True))
            link(pool.iota(tie[:, :], pattern=[[-1, PER_GROUP]], base=PER_GROUP, channel_multiplier=0,
                           allow_small_or_imprecise_dtypes=True))
            link(pool.iota(thresh[:, :], pattern=[[SLOTS, ROUNDS - 1]], base=SLOTS, channel_multiplier=0,
                           allow_small_or_imprecise_dtypes=True))
            pool.iota(dest[:, :], pattern=[[S, 2], [P, NT]], base=0, channel_multiplier=1)\
                .then_inc(sem("constants"), 1)

            pool.wait_ge(sem("z_key"), NT)
            kr = ZS[:, :, QR + KVR:ZA]
            pool.tensor_copy(kr_tok[:, :, NOPE:QKD], kr).then_inc(sem("kr_ready"), 1)
            pool.tensor_copy(kr_tok[:, :, QKD:QKD + HALF], kr[:, :, HALF:]).then_inc(sem("kr_ready"), 1)
            pool.tensor_copy(kr_tok[:, :, QKD + HALF:], kr[:, :, 0:HALF]).then_inc(sem("kr_ready"), 1)

            def head_weights(s, h, used):
                if used is not None:
                    pool.wait_ge(sem("k_full"), used)
                src = w_q[:, :, bass.ds(h * QKD, QKD)]
                pool.tensor_copy(wqh[s][:, :, 0:QKD], src).then_inc(sem("wh_ready"), 1)
                a = w_q[:, :, bass.ds(h * QKD + (NOPE + HALF), HALF)]
                pool.tensor_copy(wqh[s][:, :, QKD:QKD + HALF], a).then_inc(sem("wh_ready"), 1)
                b = w_q[:, :, bass.ds(h * QKD + NOPE, HALF)]
                pool.tensor_copy(wqh[s][:, :, QKD + HALF:], b).then_inc(sem("wh_ready"), 1)
                c = w_kv[:, bass.ds(h * 2 * VD, NOPE)]
                pool.tensor_copy(wkh[s], c).then_inc(sem("wh_ready"), 1)

            pool.wait_ge(sem("w_qkv_in"), 32)
            for s in range(2):
                head_weights(s, s, None)
            with pool.Fori(0, H // 2 - 1) as i:
                for s in range(2):
                    head_weights(s, 2 * i + (2 + s), 2 * i + (s + 1))

            def band_matrices():
                for g, w in enumerate(WINDOWS):
                    link(pool.memset(band[:, g, :], 1.0))
                    link(pool.affine_select(out=band[:, g, :], in_=band[:, g, :], compare_op=ALU.is_ge, fill=0.0,
                                            base=0, pattern=[[1, HALO]], channel_multiplier=-1))
                    link(pool.affine_select(out=band[:, g, :], in_=band[:, g, :], compare_op=ALU.is_gt, fill=0.0,
                                            base=w, pattern=[[-1, HALO]], channel_multiplier=1))
                    link(pool.iota(ramp[:, g, :], pattern=[[1, 16]], base=1, channel_multiplier=0,
                                   allow_small_or_imprecise_dtypes=True))
                    link(pool.tensor_scalar(ramp[:, g, :], ramp[:, g, :], float(w), None, ALU.min))
                pool.tensor_copy(band0, band[:, :, 0:16]).then_inc(sem("band_sums"), 1)

            for l in range(2):
                pool.wait_ge(sem("router_full"), 2 * l + 1)
                pool.wait_ge(sem("gidx_ready"), 2 * l + 2)
                pool.wait_ge(sem("xn_out"), 16 * NT * (l + 1))
                gather_bound = pool.to_reg(S - 1)
                scatter_bound = pool.to_reg(2 * S - 1)

                def settle():
                    pool.sem_inc(sem("pool_settled"), 1)

                def gather(u, e):
                    u %= RING
                    wait(pool, "xg_full", e - (RING - 1))
                    pool.tensor_copy(gidx[0:SLOTS, u:u + 1], GIDX[0:SLOTS, bass.ds(e, 1)])\
                        .then_inc(sem("gidx_set"), 1)
                    pool.wait_ge(sem("gidx_set"), e + 1)
                    settle()
                    pool.indirect_dma_start(
                        out=XG[0:SLOTS, u, :], out_offset=None, in_=xn_dram[l],
                        in_offset=bass.IndirectOffsetOnAxis(ap=gidx[0:SLOTS, u:u + 1], axis=0),
                        bounds_check=gather_bound, oob_is_err=False).then_inc(sem(f"xg_in{l}_{u}"), 16)

                def scatter(u, e, turn):
                    b = u % 2
                    wait(pool, f"scattered{l}_{b}", 16 * turn)
                    pool.tensor_copy(sidx[0:SLOTS, b:b + 1], SIDX[0:SLOTS, bass.ds(e, 1)])\
                        .then_inc(sem("sidx_set"), 1)
                    pool.wait_ge(sem("sidx_set"), e + 1)
                    pool.wait_ge(sem("ys_act"), e + 1)
                    pool.wait_ge(sem("ys_dve"), e + 1)
                    settle()
                    pool.indirect_dma_start(
                        out=y_dram[l], out_offset=bass.IndirectOffsetOnAxis(ap=sidx[0:SLOTS, b:b + 1], axis=0),
                        in_=YS[0:SLOTS, b, :], in_offset=None, bounds_check=scatter_bound, oob_is_err=False)\
                        .then_inc(sem(f"scattered{l}_{b}"), 16)

                for e in range(RING):
                    gather(e, e)
                pool.wait_ge(sem("slot_cleared"), 16 * 2)
                pool.wait_ge(sem("slot_pos_ready"), 2 * (l + 1))
                for c in range(2 * NT):
                    pool.indirect_dma_start(
                        out=slot_dram[l], out_offset=bass.IndirectOffsetOnAxis(ap=slot_pos[:, c:c + 1], axis=0),
                        in_=dest[:, c:c + 1], in_offset=None, bounds_check=S * E - 1, oob_is_err=False)\
                        .then_inc(sem("slot_scattered"), 16)
                for e in range(RING):
                    gather(e, e + RING)
                    scatter(e, e, e // 2)
                with pool.Fori(0, E // RING - 2) as i:
                    for u in range(RING):
                        gather(u, pool.snap(RING * i + (2 * RING + u)))
                        scatter(u, pool.snap(RING * i + (RING + u)), pool.snap(2 * i + (RING + u) // 2))
                for e in range(E - RING, E):
                    scatter(e, e, e // 2)
                pool.wait_ge(sem("extra_ready"), l + 1)
                rounds = pool.value_load(extra[0:1, 0:1], min_val=0, max_val=ROUNDS - 1)
                for b in range(2):
                    pool.wait_ge(sem(f"scattered{l}_{b}"), 16 * E // 2)
                pool.wait_ge(sem("slot_scattered"), 16 * 2 * NT * (l + 1))
                with pool.If(rounds > 0):
                    pool.wait_ge(sem("gidx_rest"), 2)
                    with pool.Fori(0, rounds) as r:
                        with pool.Fori(0, E // RING) as q:
                            for u in range(RING):
                                e = pool.snap(E * r + RING * q + (E + u))
                                turn = pool.snap(E // 2 * r + 2 * q + (E + u) // 2)
                                gather(u, e)
                                scatter(u, e, turn)
                                pool.wait_ge(sem(f"scattered{l}_{u % 2}"), 16 * turn + 16)
                if l == 0:
                    pool.wait_ge(sem("w_pool_in"), 16)
                    for name in expert_counts:
                        pool.sem_clear(sem(name))
                pool.sem_inc(sem("moe_done"), 1)
                if l == 0:
                    pool.wait_ge(sem("moe_done"), 1)
                    band_matrices()

        NORM_TILES = [NT, MT] + [NT] * 4

        def norm_source(n):
            return MEM if n == 1 else X

        def wait_tile(eng, n, t):
            if n == 0:
                eng.wait_ge(sem(f"x_in_{t}"), 16)
            elif n == 1:
                eng.wait_ge(sem("mem_in"), 16 * MT)
            elif n % 2 == 0:
                eng.wait_ge(sem("o_added"), 2 * NT * (n // 2 - 1) + 2 * t + 2)
            else:
                eng.wait_ge(sem("x_moe"), NT * (n // 2 - 1) + t + 1)

        def ht_of(n):
            return memhT if n == 1 else hT

        def chunk(w, c):
            return w.rearrange("p (j n) -> p j n", j=2)[:, :, c * CHUNK // 2:(c + 1) * CHUNK // 2]

        @block.scalar
        def _(act):
            def norm_squares(n):
                src = norm_source(n)
                for t in range(NORM_TILES[n]):
                    wait_tile(act, n, t)
                    if t == 0 and n == 1:
                        act.wait_ge(sem("tok_T"), KD)
                    if t == 0 and n in (2, 4):
                        act.wait_ge(sem("mixT_full"), KD * (n // 2))
                    act.activation(XN[:, t, :], src[:, t, :], ACT.Square, accum_out=stat[:, t:t + 1])\
                        .then_inc(sem("squares"), 1)
                    act.wait_ge(sem("var"), TILES[n] + t + 1)
                    act.activation(stat[:, 8 + t:9 + t], stat[:, 4 + t:5 + t], ACT.Sqrt).then_inc(sem("root"), 1)

            def norm_turned(n):
                if n == 3:
                    act.wait_ge(sem("gains_in"), 16 * 3)
                    turned(1, 2)
                    return
                width = NORM_TILES[n] * P
                for k in range(0, KD, 2):
                    act.wait_ge(sem("tok_T"), KD * n + k + 1)
                    if k == 0:
                        act.wait_ge(sem("gains_in"), 16 * 3)
                    g = 1.0 if n in (2, 4) else GN[:, n if n < 2 else 2, k:k + 1]
                    act.activation(ht_of(n)[:, k, :], bank(0)[:, 0:width], ACT.Copy, scale=g)\
                        .then_inc(sem("hT_act"), 1)
                    if n in (2, 4):
                        split_gate_up(0, 0, 0, (k // 2,))

            def cross_attention(l):
                XP, XPT = (XP0, XPT0) if l == 0 else (XP1, XPT1)

                def exponentials(h):
                    p = h % 2
                    act.wait_ge(sem("x_max"), 2 * XHEADS * l + 2 * h + 2)
                    if h >= 2:
                        act.wait_ge(sem("xp_T"), MT * (XHEADS * l + h - 1))
                        act.wait_ge(sem("x_inv"), XHEADS * l + h - 1)
                    for t in range(NT):
                        s = bank(2 * p + t // 2)[:, (t % 2) * M:(t % 2 + 1) * M]
                        act.activation(XP[p][:, t, :], s, ACT.Exp, bias=stat[:, 24 + 4 * p + t:25 + 4 * p + t],
                                       accum_out=stat[:, 32 + 4 * p + t:33 + 4 * p + t]).then_inc(sem("x_exp"), 1)

                if l == 0:
                    act.wait_ge(sem("rope_done"), 1)
                exponentials(0)
                exponentials(1)
                for h in range(XHEADS):
                    act.wait_ge(sem("xp_T"), MT * (XHEADS * l + h) + 1)
                    if h >= 1:
                        act.wait_ge(sem("xo_full"), XHEADS * l + h)
                    act.activation(XPT[:, 0, :], bank(4), ACT.Copy).then_inc(sem("xpt_act"), 1)
                    if h + 2 < XHEADS:
                        exponentials(h + 2)

            def turned(m, gain_of=None):
                for k in range(KD):
                    act.wait_ge(sem("tok_T" if m == 1 else "mixT_full"), KD * (3, m // 2)[m != 1] + k + 1)
                    g = 1.0 if gain_of is None else GN[:, gain_of, k:k + 1]
                    act.activation(TOK_HI[:, k, :], bank(k % 2), ACT.Copy, scale=g).then_inc(sem("tok_hi"), 1)

            def split(m, k, w):
                if m == 1:
                    act.wait_ge(sem("w_pool_in"), 16)
                else:
                    act.wait_ge(sem("w_out_in"), 16 * (m // 2 + 1))
                c = bass.ds(k, 1)
                act.activation(W_HI[:, c, :], w[:, c, :], ACT.Copy).then_inc(sem("w_hi"), 1)

            def head_nope(s, h):
                wait(act, "scores_full", 3 * h)
                act.wait_ge(sem("q_full"), h + 1)
                act.activation(qT[s][0:NOPE, :], bank(4)[0:NOPE, :], ACT.Copy).then_inc(sem("q_nope"), 1)
                act.wait_ge(sem("k_full"), h + 1)
                act.activation(kT[s][0:NOPE, :], bank(5)[0:NOPE, :], ACT.Copy).then_inc(sem("k_nope"), 1)

            SLOT_OF = [(1, 0, 0), (2, 0, 128), (1, 128, 384), (0, 0, 768)]

            def head_exp(p, h):
                if not isinstance(h, int) or h >= 2:
                    act.wait_ge(sem("p_T"), 4 * h - 4)
                    act.wait_ge(sem("inv_sum"), h - 1)
                for t in range(NT):
                    b, at, to = SLOT_OF[t]
                    n = (t + 1) * P
                    act.wait_ge(sem("row_max"), 4 * h + (2, 3, 2, 4)[t])
                    act.activation(PR[p][:, to:to + n], bank(b)[:, at:at + n], ACT.Exp, bias=stat[:, 16 + t:17 + t],
                                   accum_out=stat[:, 32 + 4 * p + t:33 + 4 * p + t]).then_inc(sem("probs"), 1)

            def head_pt(t, h):
                act.wait_ge(sem("p_T"), 4 * h + t + 1)
                wait(act, "o_done", 4 * h + t - 1)
                act.activation(PT[:, PT_AT[t]:PT_AT[t] + (t + 1) * P], bank(7)[:, 0:(t + 1) * P], ACT.Copy)\
                    .then_inc(sem("pt_act"), 1)

            norm_squares(0)
            norm_turned(0)
            act.wait_ge(sem("rang_ready"), 1)
            act.activation(trig, rang, ACT.Sin).then_inc(sem("trig_ready"), 1)
            norm_squares(1)
            for t in range(NT):
                act.wait_ge(sem("z_full"), 2 * t + 1)
                act.activation(ZS[:, t, 0:ZA], bank(2 + 2 * (t % 2))[:, 0:ZA], ACT.Copy).then_inc(sem("z_key"), 1)
            norm_turned(1)
            for t in range(NT):
                act.wait_ge(sem("z_key"), t + 1)
                act.activation(PR[0][:, 0:QR], ZS[:, t, 0:QR], ACT.Square, accum_out=stat[:, 24 + t:25 + t])\
                    .then_inc(sem("lat_squares"), 1)
                act.wait_ge(sem("lat_squares"), 2 * t + 1)
                act.activation(PR[0][:, 0:KVR], ZS[:, t, QR:QR + KVR], ACT.Square, accum_out=stat[:, 28 + t:29 + t])\
                    .then_inc(sem("lat_squares"), 1)
                act.wait_ge(sem("lat_squares"), 2 * t + 2)
            act.wait_ge(sem("lat_var"), 2)
            act.activation(stat[:, 32:40], stat[:, 24:32], ACT.Sqrt).then_inc(sem("lat_root"), 1)
            for m in range(XW // P):
                act.wait_ge(sem("mk_full"), m + 1)
                act.activation(MK[:, m, :], bank(2 + m)[:, 0:M], ACT.Copy).then_inc(sem("mem_ready"), 1)
            act.wait_ge(sem("small_in"), 16 * 6)
            for k in range(KQ):
                act.wait_ge(sem("lat_T"), k + 1)
                act.activation(QLT[:, k, :], bank(k), ACT.Copy, scale=gq[:, k:k + 1]).then_inc(sem("lat_ready"), 1)
            act.wait_ge(sem("lat_T"), 3)
            act.activation(KVT, bank(2), ACT.Copy, scale=gkv[:, 0:1]).then_inc(sem("lat_ready"), 1)
            for t in range(NT):
                act.wait_ge(sem("v_full"), 2 * t + 1)
                act.activation(V[:, t, 0:MW // 2], bank(0)[:, 0:MW // 2], ACT.Copy).then_inc(sem("v_act"), 1)
            cross_attention(0)
            act.wait_ge(sem("xo_full"), XHEADS)
            def head_step(p, h, before):
                head_exp(p, h)
                if before is not None:
                    head_pt(1, before)
                if not isinstance(h, int):
                    head_nope(1 - p, act.snap(h + 1))
                elif h + 1 < H:
                    head_nope(1 - p, h + 1)
                if before is not None:
                    head_pt(3, before)

            head_nope(0, 0)
            head_step(0, 0, None)
            head_step(1, 1, 0)
            with act.Fori(0, H // 2 - 2) as i:
                for p in range(2):
                    head_step(p, act.snap(2 * i + (2 + p)), act.snap(2 * i + (1 + p)))
                    split(0, act.snap(2 * i + p), w_out)
            head_step(0, H - 2, H - 3)
            head_step(1, H - 1, H - 2)
            head_pt(1, H - 1)
            head_pt(3, H - 1)
            turned(0)

            def split_gate_up(u, e, lap, quarters=range(4)):
                u, b = u % RING, u % 2
                act.wait_ge(sem(f"gu_in_{u}"), 32 * lap + 32)
                wait(act, "gu_full", e - 1)
                for c in quarters:
                    act.activation(chunk(GU_HI[:, b, :], c), chunk(WE[:, u, 0:GU], c), ACT.Copy)\
                        .then_inc(sem("gu_hi"), 1)

            def experts(l):

                def split_down(u, e, lap):
                    u, b = u % RING, u % 2
                    act.wait_ge(sem(f"down_in_{u}"), 16 * lap + 16)
                    wait(act, "y_full", e - 1)
                    for k in range(KF):
                        act.activation(DOWN_HI[:, b, k * D:(k + 1) * D], WE[:, u, GU + k * D:GU + (k + 1) * D],
                                       ACT.Copy).then_inc(sem("down_hi"), 1)

                def gate(u, e):
                    b = u % 2
                    act.wait_ge(sem("gu_full"), e + 1)
                    wait(act, "at_full", e - 1)
                    act.activation(SG[0:SLOTS, b, :], bank(2 + b)[0:SLOTS, 0:FE], ACT.Silu).then_inc(sem("sg_ready"), 1)

                def rows_hi(u, e):
                    b = u % 2
                    act.wait_ge(sem("xg_full"), e + 1)
                    wait(act, "gu_full", e - 1)
                    act.activation(XGT[:, b, 0, :], bank(b), ACT.Copy).then_inc(sem("x_hi"), 1)

                def hidden_hi(u, e):
                    b = u % 2
                    act.wait_ge(sem("at_full"), e + 1)
                    wait(act, "y_full", e - 1)
                    act.activation(AT[:, b, 0, :], bank(4 + b)[:, 0:KF * SLOTS], ACT.Copy).then_inc(sem("a_hi"), 1)

                def rows_out(u, e, turn):
                    b = u % 2
                    act.wait_ge(sem("y_full"), e + 1)
                    wait(act, f"scattered{l}_{b}", 16 * turn)
                    act.activation(YS[0:SLOTS, b, 0:D // 2], bank(6)[0:SLOTS, :], ACT.Copy).then_inc(sem("ys_act"), 1)

                def step(u, e, lap, turn, before, after, after_lap):
                    if after is not None:
                        split_gate_up(u + 1, after, after_lap)
                    gate(u, e)
                    if after is not None:
                        rows_hi(u + 1, after)
                    split_down(u, e, lap)
                    if before is not None:
                        rows_out(u - 1, before, turn)
                    hidden_hi(u, e)

                rows_hi(0, 0)
                act.wait_ge(sem("xn_out"), 16 * NT * (l + 1))
                for e in range(RING):
                    step(e, e, 0, (e - 1) // 2, e - 1 if e else None, e + 1, (e + 1) // RING)
                with act.Fori(0, E // RING - 2) as i:
                    for u in range(RING):
                        step(u + RING, act.snap(RING * i + (RING + u)), act.snap(i + 1),
                             act.snap(2 * i + (RING + u - 1) // 2), act.snap(RING * i + (RING + u - 1)),
                             act.snap(RING * i + (RING + u + 1)), act.snap(i + (RING + u + 1) // RING))
                for e in range(E - RING, E):
                    step(e, e, e // RING, (e - 1) // 2, e - 1, e + 1 if e + 1 < E else None, (e + 1) // RING)
                rows_out(E - 1, E - 1, (E - 1) // 2)
                act.wait_ge(sem("extra_ready"), l + 1)
                rounds = act.value_load(extra[0:1, 0:1], min_val=0, max_val=ROUNDS - 1)
                with act.If(rounds > 0):
                    with act.Fori(0, rounds) as r:
                        with act.Fori(0, E // RING) as q:
                            for u in range(RING):
                                e = act.snap(E * r + RING * q + (E + u))
                                lap = act.snap(E // RING * r + q + E // RING)
                                split_gate_up(u, e, lap)
                                rows_hi(u, e)
                                gate(u, e)
                                split_down(u, e, lap)
                                hidden_hi(u, e)
                                rows_out(u, e, act.snap(E // 2 * r + 2 * q + (E + u) // 2))

            def router(l):
                act.wait_ge(sem("router_full"), 2 * l + 1)
                act.activation(LT[0:NR, :], bank(6)[0:NR, :], ACT.Copy).then_inc(sem("router_act"), 1)
                act.wait_ge(sem("to_exponentiate"), 2 * l + 1)
                act.activation(EG, LS, ACT.Exp).then_inc(sem("router_act"), 1)
                act.wait_ge(sem("to_exponentiate"), 2 * l + 2)
                act.activation(small[:, 4:8], small[:, 0:4], ACT.Exp).then_inc(sem("router_act"), 1)

            norm_squares(2)
            norm_turned(2)
            router(0)
            experts(0)
            for k in range(KD):
                split(1, k, w_pool)
            norm_squares(3)
            norm_turned(3)
            for t in range(NT):
                act.wait_ge(sem("zp_full"), 2 * t + 1)
                act.activation(U[:, t, 0:512], bank(2 + 2 * (t % 2)), ACT.Copy).then_inc(sem("u_act"), 1)
            act.wait_ge(sem("qcT_full1"), 1)
            act.activation(QCT1[:, 0, :], bank(0), ACT.Copy).then_inc(sem("u_act"), 1)
            for j in range(0, 2 * len(WINDOWS), 2):
                act.wait_ge(sem("d_full"), j + 1)
                act.activation(dT[0:HW, j, :], bank(6)[0:HW, :], ACT.Copy, scale=1.0 / WINDOWS[j // 2])\
                    .then_inc(sem("d_act"), 1)
                split(2, j // 2, w_out)
            for k in range(len(WINDOWS), KD):
                split(2, k, w_out)
            cross_attention(1)
            turned(2)
            norm_squares(4)
            norm_turned(4)
            router(1)
            experts(1)
            norm_squares(5)

        @block.vector
        def _(dve):
            steps = [0]

            def link(ins):
                steps[0] += 1
                ins.then_inc(sem("dve_step"), 1)
                dve.wait_ge(sem("dve_step"), steps[0])

            def norm_tile(n, t):
                dve.wait_ge(sem("squares"), TILES[n] + t + 1)
                dve.tensor_scalar(stat[:, 4 + t:5 + t], stat[:, t:t + 1], 1.0 / D, EPS, ALU.mult, ALU.add)\
                    .then_inc(sem("var"), 1)
                dve.wait_ge(sem("root"), TILES[n] + t + 1)
                r = stat[:, 12 + t:13 + t]
                link(dve.reciprocal(r, stat[:, 8 + t:9 + t]))
                if n in (2, 4, 5):
                    if t == 0:
                        dve.wait_ge(sem("gain_in"), 16 * ((n + 1) // 2))
                    g, done = (gfin, "fin") if n == 5 else (gain, "xn")
                    dve.scalar_tensor_tensor(out=XN[:, t, :], in0=X[:, t, :], scalar=r, in1=g, op0=ALU.mult,
                                             op1=ALU.mult).then_inc(sem(done), 1)
                else:
                    dve.tensor_scalar(XN[:, t, :], norm_source(n)[:, t, :], r, None, ALU.mult).then_inc(sem("xn"), 1)

            def norm_scale(n):
                for t in range(NORM_TILES[n]):
                    norm_tile(n, t)

            def norm_turned(n):
                width = NORM_TILES[n] * P
                for k in range(1, KD, 2):
                    dve.wait_ge(sem("tok_T"), KD * n + k + 1)
                    if k == 1:
                        dve.wait_ge(sem("gains_in"), 16 * 3)
                    g = 1.0 if n in (2, 4) else GN[:, n if n < 2 else 2, k:k + 1]
                    dve.tensor_scalar(ht_of(n)[:, k, :], bank(1)[:, 0:width], g, None, ALU.mult)\
                        .then_inc(sem("hT_dve"), 1)
                    if n in (2, 4):
                        split_gate_up(0, 0, (k // 2,))

            def x_maxima(l, h):
                p = h % 2
                if h >= 2:
                    dve.wait_ge(sem("x_exp"), NT * (XHEADS * l + h - 1))
                for j in range(2):
                    dve.wait_ge(sem("xs_full"), 2 * XHEADS * l + 2 * h + j + 1)
                    at = 24 + 4 * p + 2 * j
                    dve.tensor_reduce(stat[:, at:at + 2], bank(2 * p + j, 2, M), AX.X, ALU.max, negate=True)\
                        .then_inc(sem("x_max"), 1)

            def cross_attention(l):
                XPT = XPT0 if l == 0 else XPT1

                if l == 0:
                    x_maxima(l, 0)
                x_maxima(l, 1)
                for h in range(XHEADS):
                    p = h % 2
                    dve.wait_ge(sem("x_exp"), NT * (XHEADS * l + h + 1))
                    dve.reciprocal(stat[:, 40 + 4 * p:44 + 4 * p], stat[:, 32 + 4 * p:36 + 4 * p])\
                        .then_inc(sem("x_inv"), 1)
                    if h + 2 < XHEADS:
                        x_maxima(l, h + 2)
                    dve.wait_ge(sem("xp_T"), MT * (XHEADS * l + h) + 2)
                    if h >= 1:
                        dve.wait_ge(sem("xo_full"), XHEADS * l + h)
                    dve.tensor_copy(XPT[:, 1, :], bank(5)).then_inc(sem("xpt_dve"), 1)
                    dve.wait_ge(sem("x_inv"), XHEADS * l + h + 1)
                    dve.wait_ge(sem("xo_full"), XHEADS * l + h + 1)
                    r = stat[:, 40 + 4 * p:44 + 4 * p].rearrange("p (t a) -> p t a", a=1)
                    dve.tensor_tensor(XN[:, :, MW + h * XD:MW + (h + 1) * XD], bank(6 + p, NT, XD),
                                      wide(r, P, NT, XD), ALU.mult).then_inc(sem("xmix"), 1)

            def turned(m, gain_of=None):
                for k in range(KD):
                    dve.wait_ge(sem("tok_hi"), KD * m + k + 1)
                    hi = TOK_HI[:, k, :].bitcast(F32)
                    if gain_of is None:
                        ins = dve.tensor_tensor(TOK_LO[:, k, :], bank(k % 2), hi, ALU.subtract)
                    else:
                        ins = dve.scalar_tensor_tensor(out=TOK_LO[:, k, :], in0=bank(k % 2),
                                                       scalar=GN[:, gain_of, k:k + 1], in1=hi, op0=ALU.mult,
                                                       op1=ALU.subtract)
                    ins.then_inc(sem("tok_lo"), 1)

            def split(k, count, w, lo):
                dve.wait_ge(sem("w_hi"), count)
                c = bass.ds(k, 1)
                dve.tensor_tensor(lo[:, c, :], w[:, c, :], W_HI[:, c, :].bitcast(F32), ALU.subtract)\
                    .then_inc(sem("w_lo"), 1)

            def residual(l):
                for t in range(NT):
                    for j in range(2):
                        dve.wait_ge(sem("o_full"), 2 * NT * l + 2 * t + j + 1)
                        part = X[:, t, j * 512:(j + 1) * 512]
                        dve.tensor_tensor(part, bank(2 + (2 * t + j) % 4), part, ALU.add).then_inc(sem("o_added"), 1)
                    norm_tile(2 * l + 2, t)

            def router(l):
                dve.wait_ge(sem("router_full"), 2 * l + 2)
                if l == 0:
                    dve.wait_ge(sem("constants"), 4)
                    dve.wait_ge(sem("small_in"), 16 * 6)
                logits = bank(3, NT, NR)
                b = bias_r[:, l, :].rearrange("p (a n) -> p a n", a=1)
                link(dve.tensor_tensor(LG, logits, wide(b, P, NT, NR), ALU.add))

                def col(at, n=1):
                    return small[:, at:at + NT].rearrange("p (t a) -> p t a", a=1)

                def first_of(best_of, n, out_):
                    w = tie[:, 0:n].rearrange("p (a n) -> p a n", a=1)
                    link(dve.scalar_tensor_tensor(out=SC[:, :, 0:n], in0=best_of, scalar=0.0, in1=wide(w, P, NT, n),
                                                  op0=ALU.is_equal, op1=ALU.mult))
                    link(dve.tensor_reduce(small[:, 16:20], SC[:, :, 0:n], AX.X, ALU.max))
                    link(dve.tensor_tensor(out_, SC[:, :, 0:n], wide(col(16), P, NT, n), ALU.is_equal))

                link(dve.tensor_reduce(small[:, 8:12], LG[:, :, 0:GROUPS], AX.X, ALU.max))
                dve.tensor_tensor(LS, LG[:, :, 0:GROUPS], wide(col(8), P, NT, GROUPS), ALU.subtract)\
                    .then_inc(sem("to_exponentiate"), 1)
                dve.wait_ge(sem("to_exponentiate"), 2 * l + 1)
                first_of(LS, GROUPS, OG)

                def by_group(ap):
                    return ap.rearrange("p t (g j) -> p (t g) j", g=GROUPS)

                def og():
                    return OG.rearrange("p t (g a) -> p (t g) a", a=1)

                link(dve.tensor_copy(LE, LG[:, :, GROUPS:]))
                link(dve.tensor_tensor(by_group(LE), by_group(LE), wide(og(), P, NT * GROUPS, PER_GROUP), ALU.mult))
                link(dve.tensor_reduce(SEL, LE.rearrange("p t (g j) -> p t j g", g=GROUPS), AX.X, ALU.add))
                link(dve.tensor_reduce(small[:, 8:12], SEL, AX.X, ALU.max))
                link(dve.tensor_tensor(SEL, SEL, wide(col(8), P, NT, PER_GROUP), ALU.subtract))
                first_of(SEL, PER_GROUP, O1)
                link(dve.scalar_tensor_tensor(out=SEL, in0=O1, scalar=NEG_INF, in1=SEL, op0=ALU.mult, op1=ALU.add))
                dve.tensor_reduce(small[:, 0:4], SEL, AX.X, ALU.max).then_inc(sem("to_exponentiate"), 1)
                dve.wait_ge(sem("to_exponentiate"), 2 * l + 2)
                link(dve.tensor_tensor(SEL, SEL, wide(col(0), P, NT, PER_GROUP), ALU.subtract))
                first_of(SEL, PER_GROUP, O2)
                for o, a in ((O1, A1), (O2, A2)):
                    for t in range(NT):
                        g = OG[:, t, :].rearrange("p (g a) -> p g a", a=1)
                        j = o[:, t, :].rearrange("p (a j) -> p a j", a=1)
                        ins = dve.tensor_tensor(a[:, t, :].rearrange("p (g j) -> p g j", g=GROUPS),
                                                wide(g, P, GROUPS, PER_GROUP), wide(j, P, GROUPS, PER_GROUP), ALU.mult)
                link(ins)
                dve.tensor_tensor(AB, A1, A2, ALU.add).then_inc(sem("assigned"), 1)
                dve.wait_ge(sem("router_act"), 3 * l + 2)
                link(dve.tensor_reduce(small[:, 12:16], EG, AX.X, ALU.add))
                dve.wait_ge(sem("router_act"), 3 * l + 3)
                link(dve.scalar_tensor_tensor(out=small[:, 20:24], in0=small[:, 4:8], scalar=1.0, in1=small[:, 12:16],
                                              op0=ALU.add, op1=ALU.mult))
                link(dve.reciprocal(wtok[:, 0, :], small[:, 20:24]))
                link(dve.tensor_tensor(wtok[:, 1, :], wtok[:, 0, :], small[:, 4:8], ALU.mult))
                for j, a in enumerate((A1, A2)):
                    d = destf[:, j * NT:(j + 1) * NT].rearrange("p (t a) -> p t a", a=1)
                    link(dve.tensor_tensor(RH[:, j, :, 0, :], a, wide(d, P, NT, E), ALU.mult))
                dve.wait_ge(sem("ranks_full"), l + 1)
                for j, a in enumerate((A1, A2)):
                    link(dve.tensor_tensor(PM, bank(7, NT, E), a, ALU.mult))
                    link(dve.tensor_reduce(small[:, 40 + 4 * j:44 + 4 * j], PM, AX.X, ALU.add))
                    i = iota_s[:, :].rearrange("p (a s) -> p a s", a=1)
                    dve.tensor_tensor(RO[:, j, :, :], wide(i, P, NT, SLOTS), wide(col(40 + 4 * j), P, NT, SLOTS),
                                      ALU.is_equal).then_inc(sem("slot_onehots"), 1)
                link(dve.tensor_reduce(small[:, 24:25], banks[7][:, NT * E:(NT + 1) * E], AX.X, ALU.max))
                link(dve.tensor_scalar(small[:, 32:32 + ROUNDS - 1], thresh[:, :], small[:, 24:25], None, ALU.is_lt))
                with nc.allow_low_precision(reason="small whole numbers"):
                    dve.tensor_reduce(extra[:, 0:1], small[:, 32:32 + ROUNDS - 1], AX.X, ALU.add)\
                        .then_inc(sem("extra_ready"), 1)
                dve.wait_ge(sem("table_full"), l + 1)
                if l == 0:
                    dve.wait_ge(sem("slot_cleared"), 16 * 2)
                table = bank(5, 2, E)[0:SLOTS]
                link(dve.tensor_copy(CF[0:SLOTS, 0:E], table[:, 0, :]))
                link(dve.scalar_tensor_tensor(out=CF[0:SLOTS, 0:E], in0=table[:, 1, :], scalar=-float(NO_TOKEN),
                                              in1=CF[0:SLOTS, 0:E], op0=ALU.mult, op1=ALU.add))
                link(dve.tensor_scalar(SIDX[0:SLOTS, 0:E], CF[0:SLOTS, 0:E], float(NO_TOKEN), None, ALU.add))
                tokens_of(0, E, "gidx_ready", 2 * l)
                ie = iota_e[:, :].rearrange("p (a e) -> p a e", a=1)
                link(dve.scalar_tensor_tensor(out=POS, in0=bank(7, NT, E), scalar=float(E), in1=wide(ie, P, NT, E),
                                              op0=ALU.mult, op1=ALU.add))
                for j, a in enumerate((A1, A2)):
                    link(dve.tensor_tensor(PM, POS, a, ALU.mult))
                    with nc.allow_low_precision(reason="small whole numbers"):
                        dve.tensor_reduce(slot_pos[:, j * NT:(j + 1) * NT], PM, AX.X, ALU.add)\
                            .then_inc(sem("slot_pos_ready"), 1)
                    dve.wait_ge(sem("slot_pos_ready"), 2 * l + j + 1)

            def tokens_of(a, b, done, count):
                c = slice(a, b)
                dve.tensor_scalar(CF[0:SLOTS, c], SIDX[0:SLOTS, c], float(S), -float(S), ALU.is_ge, ALU.mult)\
                    .then_inc(sem(done), 1)
                dve.wait_ge(sem(done), count + 1)
                dve.tensor_tensor(GIDX[0:SLOTS, c], SIDX[0:SLOTS, c], CF[0:SLOTS, c], ALU.add).then_inc(sem(done), 1)

            def split_gate_up(u, e, quarters=range(4)):
                u, b = u % RING, u % 2
                for c in quarters:
                    dve.wait_ge(sem("gu_hi"), 4 * e + c + 1)
                    w = chunk(WE[:, u, 0:GU], c)
                    dve.tensor_tensor(chunk(W_LO[u][:, 0:GU], c), w, chunk(GU_HI[:, b, :].bitcast(F32), c), ALU.subtract)\
                        .then_inc(sem("gu_lo"), 1)

            def experts(l):

                def split_down(u, e):
                    u, b = u % RING, u % 2
                    for k in range(KF):
                        dve.wait_ge(sem("down_hi"), KF * e + k + 1)
                        at = slice(GU + k * D, GU + (k + 1) * D)
                        dve.tensor_tensor(W_LO[u][:, at], WE[:, u, at], DOWN_HI[:, b, k * D:(k + 1) * D].bitcast(F32),
                                          ALU.subtract).then_inc(sem("down_lo"), 1)

                def rows_lo(u, e):
                    b = u % 2
                    dve.wait_ge(sem("x_hi"), e + 1)
                    dve.tensor_tensor(XGT[:, b, 1, :], bank(b), XGT[:, b, 0, :].bitcast(F32), ALU.subtract)\
                        .then_inc(sem("x_lo"), 1)

                def hidden(u, e):
                    b = u % 2
                    dve.wait_ge(sem("sg_ready"), e + 1)
                    dve.tensor_tensor(SG[0:SLOTS, b, :], bank(2 + b)[0:SLOTS, FE:2 * FE], SG[0:SLOTS, b, :], ALU.mult)\
                        .then_inc(sem("a_ready"), 1)

                def hidden_lo(u, e):
                    b = u % 2
                    dve.wait_ge(sem("a_hi"), e + 1)
                    dve.tensor_tensor(AT[:, b, 1, :], bank(4 + b)[:, 0:KF * SLOTS], AT[:, b, 0, :].bitcast(F32),
                                      ALU.subtract).then_inc(sem("a_lo"), 1)

                def rows_out(u, e, turn):
                    b = u % 2
                    dve.wait_ge(sem("y_full"), e + 1)
                    wait(dve, f"scattered{l}_{b}", 16 * turn)
                    dve.tensor_copy(YS[0:SLOTS, b, D // 2:], bank(7)[0:SLOTS, :]).then_inc(sem("ys_dve"), 1)

                def step(u, e, turn, before, after):
                    if after is not None:
                        split_gate_up(u + 1, after)
                    hidden(u, e)
                    if after is not None:
                        rows_lo(u + 1, after)
                    split_down(u, e)
                    if before is not None:
                        rows_out(u - 1, before, turn)
                    hidden_lo(u, e)

                rows_lo(0, 0)
                for e in range(RING):
                    step(e, e, (e - 1) // 2, e - 1 if e else None, e + 1)
                with dve.Fori(0, E // RING - 2) as i:
                    for u in range(RING):
                        step(u + RING, dve.snap(RING * i + (RING + u)), dve.snap(2 * i + (RING + u - 1) // 2),
                             dve.snap(RING * i + (RING + u - 1)), dve.snap(RING * i + (RING + u + 1)))
                for e in range(E - RING, E):
                    step(e, e, (e - 1) // 2, e - 1, e + 1 if e + 1 < E else None)
                rows_out(E - 1, E - 1, (E - 1) // 2)
                dve.wait_ge(sem("extra_ready"), l + 1)
                rounds = dve.value_load(extra[0:1, 0:1], min_val=0, max_val=ROUNDS - 1)
                with dve.If(rounds > 0):
                    dve.wait_ge(sem("sidx_in"), 16)
                    tokens_of(E, ROUNDS * E, "gidx_rest", 0)
                    with dve.Fori(0, rounds) as r:
                        with dve.Fori(0, E // RING) as q:
                            for u in range(RING):
                                e = dve.snap(E * r + RING * q + (E + u))
                                split_gate_up(u, e)
                                rows_lo(u, e)
                                hidden(u, e)
                                split_down(u, e)
                                hidden_lo(u, e)
                                rows_out(u, e, dve.snap(E // 2 * r + 2 * q + (E + u) // 2))
                if l == 0:
                    for k in range(KD - 2):
                        split(k, KD + k + 1, w_pool, POOL_LO)
                for t in range(NT):
                    dve.wait_ge(sem(f"yl_in_{t}"), 32 * (l + 1))
                    for j in range(2):
                        ins = dve.scalar_tensor_tensor(
                            out=X[:, t, :], in0=YL[t][:, j, :], scalar=wtok[:, j, t:t + 1],
                            in1=X[:, t, :], op0=ALU.mult, op1=ALU.add)
                        if j == 0:
                            link(ins)
                    ins.then_inc(sem("x_moe"), 1)
                    if t >= 1:
                        norm_tile(2 * l + 3, t - 1)
                norm_tile(2 * l + 3, NT - 1)

            def rope(src, dst, scratch):
                lo, hi = slice(NOPE, QKD), slice(QKD, P)
                a = scratch
                return (dve.tensor_tensor(a[lo, :], src[hi, :], TBL[hi, :], ALU.mult),
                        dve.tensor_tensor(dst[lo, :], src[lo, :], TBL[lo, :], ALU.mult))

            norm_scale(0)
            norm_turned(0)
            two_pi = 2 * np.pi
            c1 = 6.28125
            c2 = float(np.float32(np.round((two_pi - c1) * 2 ** 21) / 2 ** 21))
            c3 = float(np.float32(two_pi - c1 - c2))
            MAGIC = 1.5 * 2 ** 23
            dve.wait_ge(sem("positions_in"), 16)
            dve.wait_ge(sem("constants"), 2)
            link(dve.tensor_copy(posf, posi))
            p3 = posf.rearrange("p (t a) -> p t a", a=1)
            f3 = freq.rearrange("p (a i) -> p a i", a=1)
            link(dve.tensor_tensor(ang, wide(p3, P, NT, HALF), wide(f3, P, NT, HALF), ALU.mult))
            flat = ang.rearrange("p t i -> p (t i)")
            for j, shift in ((0, 0.25), (1, 0.0)):
                link(dve.tensor_scalar(turns[:, j, :], flat, float(np.float32(1 / two_pi)), shift, ALU.mult, ALU.add))
                link(dve.tensor_scalar(turns[:, j, :], turns[:, j, :], MAGIC, None, ALU.add))
                link(dve.tensor_scalar(turns[:, j, :], turns[:, j, :], MAGIC, None, ALU.subtract))
                link(dve.scalar_tensor_tensor(out=rang[:, j, :], in0=turns[:, j, :], scalar=-c1, in1=flat,
                                              op0=ALU.mult, op1=ALU.add))
                link(dve.scalar_tensor_tensor(out=rang[:, j, :], in0=turns[:, j, :], scalar=-c2, in1=rang[:, j, :],
                                              op0=ALU.mult, op1=ALU.add))
                link(dve.scalar_tensor_tensor(out=rang[:, j, :], in0=turns[:, j, :], scalar=-c3, in1=rang[:, j, :],
                                              op0=ALU.mult, op1=ALU.add))
                if j == 0:
                    link(dve.tensor_scalar(rang[:, j, :], rang[:, j, :], float(np.float32(np.pi / 2)), None, ALU.add))
            lim = float(np.nextafter(np.float32(np.pi), np.float32(0)))
            dve.tensor_scalar(rang, rang, lim, -lim, ALU.min, ALU.max).then_inc(sem("rang_ready"), 1)
            dve.wait_ge(sem("trig_ready"), 1)
            dve.wait_ge(sem("constants"), 3)
            cos = trig[:, 0, :].rearrange("p (t i) -> p t i", t=NT)
            sin = trig[:, 1, :].rearrange("p (t i) -> p t i", t=NT)
            for at, src, s in ((NOPE, cos, 1.0), (NOPE + HALF, cos, 1.0), (QKD, sin, -1.0), (QKD + HALF, sin, 1.0)):
                dve.tensor_scalar(tbl_tok[:, :, at:at + HALF], src, s, None, ALU.mult).then_inc(sem("tbl_ready"), 1)
            norm_scale(1)
            for t in range(NT):
                dve.wait_ge(sem("z_full"), 2 * t + 2)
                dve.tensor_scalar(ZS[:, t, ZA:ZW], bank(3 + 2 * (t % 2))[:, 0:XW], XSCALE, None, ALU.mult)\
                    .then_inc(sem("z_xq"), 1)
            norm_turned(1)
            dve.wait_ge(sem("tblT_full"), 1)
            link(dve.tensor_copy(TBL[NOPE:P, :], bank(7)[NOPE:P, :]))
            dve.wait_ge(sem("lat_squares"), 2 * NT)
            dve.tensor_scalar(stat[:, 24:28], stat[:, 24:28], 1.0 / QR, EPS, ALU.mult, ALU.add).then_inc(sem("lat_var"), 1)
            dve.tensor_scalar(stat[:, 28:32], stat[:, 28:32], 1.0 / KVR, EPS, ALU.mult, ALU.add).then_inc(sem("lat_var"), 1)
            dve.wait_ge(sem("lat_root"), 1)
            link(dve.reciprocal(stat[:, 40:48], stat[:, 32:40]))
            link(dve.tensor_scalar(stat[:, 40:44], stat[:, 40:44], QSCALE, None, ALU.mult))
            for t in range(NT):
                for a, b, c in ((0, QR, 40), (QR, QR + KVR, 44)):
                    dve.tensor_scalar(ZS[:, t, a:b], ZS[:, t, a:b], stat[:, c + t:c + t + 1], None, ALU.mult)\
                        .then_inc(sem("lat_normed"), 1)
            for c in range(MT):
                dve.wait_ge(sem("mv_full"), c + 1)
                dve.tensor_copy(MV[:, c, :], bank(4 + c)[:, 0:XW]).then_inc(sem("mv_ready"), 1)
            for m in range(2):
                dve.wait_ge(sem("lat_T"), 4 + m)
                dve.tensor_copy(QCT0[:, m, :], bank(3 + m)).then_inc(sem("qct0"), 1)
            dve.wait_ge(sem("lat_T"), 6)
            for s in range(2):
                for ins in rope(bank(5), kT[s], qT[s]):
                    link(ins)
                ins = dve.tensor_tensor(kT[s][NOPE:QKD, :], kT[s][NOPE:QKD, :], qT[s][NOPE:QKD, :], ALU.add)
                if s == 0:
                    link(ins)
                else:
                    ins.then_inc(sem("rope_done"), 1)
            for t in range(NT):
                dve.wait_ge(sem("v_full"), 2 * t + 2)
                dve.tensor_copy(V[:, t, MW // 2:], bank(1)[:, 0:MW // 2]).then_inc(sem("v_dve"), 1)
            cross_attention(0)

            def head_rope(s, h):
                dve.wait_ge(sem("q_full"), h + 1)
                wait(dve, "scores_full", 3 * h)
                for ins in rope(bank(4), qT[s], rope_scratch):
                    ins.then_inc(sem("q_rot"), 1)
                dve.wait_ge(sem("q_rot"), 2 * h + 2)
                dve.tensor_tensor(qT[s][NOPE:QKD, :], qT[s][NOPE:QKD, :], rope_scratch[NOPE:QKD, :], ALU.add)\
                    .then_inc(sem("q_rope"), 1)

            SLOT_OF = [(1, 0, 1), (2, 0, 2), (1, 128, 1), (0, 0, 3)]

            def head_max(h):
                wait(dve, "probs", 4 * h)
                for t in (0, 2, 1, 3):
                    b, at, n_full = SLOT_OF[t]
                    dve.wait_ge(sem("scores_full"), 3 * h + n_full)
                    dve.tensor_reduce(stat[:, 16 + t:17 + t], bank(b)[:, at:at + (t + 1) * P], AX.X, ALU.max,
                                      negate=True).then_inc(sem("row_max"), 1)

            def head_pt(t, h):
                dve.wait_ge(sem("p_T"), 4 * h + t + 1)
                wait(dve, "o_done", 4 * h + t - 3)
                dve.tensor_copy(PT[:, PT_AT[t]:PT_AT[t] + (t + 1) * P], bank(6)[:, 0:(t + 1) * P])\
                    .then_inc(sem("pt_dve"), 1)

            def head_out(p, h, col):
                dve.wait_ge(sem("probs"), 4 * h + 4)
                dve.reciprocal(stat[:, 40:44], stat[:, 32 + 4 * p:36 + 4 * p]).then_inc(sem("inv_sum"), 1)
                dve.wait_ge(sem("inv_sum"), h + 1)
                dve.wait_ge(sem("o_done"), 4 * h + 4)
                r = stat[:, 40:44].rearrange("p (t a) -> p t a", a=1)
                dve.tensor_tensor(XN[:, :, bass.ds(col, VD)], bank(3, NT, VD), wide(r, P, NT, VD), ALU.mult)\
                    .then_inc(sem("mixed"), 1)

            def head_step(p, h, before, col):
                head_max(h)
                if before is not None:
                    head_pt(0, before)
                    head_pt(2, before)
                if not isinstance(h, int):
                    head_rope(1 - p, dve.snap(h + 1))
                elif h + 1 < H:
                    head_rope(1 - p, h + 1)
                if before is not None:
                    head_out(1 - p, before, col)

            head_rope(0, 0)
            head_step(0, 0, None, None)
            head_step(1, 1, 0, 0)
            with dve.Fori(0, H // 2 - 2) as i:
                for p in range(2):
                    head_step(p, dve.snap(2 * i + (2 + p)), dve.snap(2 * i + (1 + p)),
                              dve.snap(2 * VD * i + (1 + p) * VD))
                    split(dve.snap(2 * i + p), dve.snap(2 * i + (p + 1)), w_out, OUT_LO)
            head_step(0, H - 2, H - 3, (H - 3) * VD)
            head_step(1, H - 1, H - 2, (H - 2) * VD)
            head_pt(0, H - 1)
            head_pt(2, H - 1)
            head_out(1, H - 1, (H - 1) * VD)
            turned(0)
            residual(0)
            norm_turned(2)
            router(0)
            experts(0)
            turned(1, 2)
            for k in range(KD - 2, KD):
                split(k, KD + k + 1, w_pool, POOL_LO)
            for t in range(NT):
                b = bank(3 + 2 * (t % 2))
                dve.wait_ge(sem("zp_full"), 2 * t + 2)
                dve.tensor_copy(U[:, t, 512:MW], b[:, 0:MW - 512]).then_inc(sem("u_dve"), 1)
                dve.tensor_scalar(QC[:, t, :], b[:, MW - 512:512], XSCALE, None, ALU.mult).then_inc(sem("u_dve"), 1)
            dve.wait_ge(sem("qcT_full1"), 2)
            dve.tensor_copy(QCT1[:, 1, :], bank(1)).then_inc(sem("u_dve"), 1)
            dve.wait_ge(sem("band_sums"), 1)
            link(dve.reciprocal(ramp, ramp))
            for g, w in enumerate(WINDOWS):
                dve.scalar_tensor_tensor(out=band0[:, g, :], in0=ramp[:, g, :], scalar=float(w), in1=band0[:, g, :],
                                         op0=ALU.mult, op1=ALU.mult).then_inc(sem("bands_ready"), 1)
            dve.wait_ge(sem("bands_ready"), len(WINDOWS))
            for g, w in enumerate(WINDOWS):
                for m, n in ((band, P), (band0, 16)):
                    dve.scalar_tensor_tensor(out=m[:, g, 0:n], in0=ident[:, 0:n], scalar=-float(w), in1=m[:, g, 0:n],
                                             op0=ALU.mult, op1=ALU.add).then_inc(sem("bands_ready"), 1)
            for j in range(1, 2 * len(WINDOWS), 2):
                dve.wait_ge(sem("d_full"), j + 1)
                dve.tensor_scalar(dT[0:HW, j, :], bank(7)[0:HW, :], 1.0 / WINDOWS[j // 2], None, ALU.mult)\
                    .then_inc(sem("d_dve"), 1)
                split(j // 2, 2 * KD + j // 2 + 1, w_out, OUT_LO)
            x_maxima(1, 0)
            dve.wait_ge(sem("w_mix_in"), 32)
            for t in range(NT):
                for j in range(2):
                    dve.wait_ge(sem("y_pool"), 2 * t + j + 1)
                    c = slice(j * MW // 2, (j + 1) * MW // 2)
                    dve.tensor_tensor(XN[:, t, c], bank(2 + 2 * (t % 2) + j)[:, 0:MW // 2], scale_b[:, c], ALU.mult)\
                        .then_inc(sem("pool_mixed"), 1)
                split(NT + t, 2 * KD + NT + t + 1, w_out, OUT_LO)
            cross_attention(1)
            turned(2)
            residual(1)
            norm_turned(4)
            router(1)
            experts(1)

        @block.tensor
        def _(pe):
            def norm_turned(n, between=None):
                if between is not None:
                    pe.wait_ge(sem("wr_in"), 16 * n)
                for k in range(KD):
                    if k >= 2:
                        if n == 3:
                            pe.wait_ge(sem("tok_lo"), KD + k - 1)
                        else:
                            pe.wait_ge(sem("hT_act" if k % 2 == 0 else "hT_dve"), KD // 2 * HALVED[n] + k // 2)
                    for t in range(NORM_TILES[n]):
                        if k == 0:
                            pe.wait_ge(sem("xn"), TILES[n] + t + 1)
                        ins = pe.transpose(bank(k % 2)[:, t * P:(t + 1) * P], XN[:, t, k:D:KD], ident[:, :])
                    ins.then_inc(sem("tok_T"), 1)
                    if between is not None and k >= 1:
                        between(k - 1)

            def wait_turned(n, k):
                pe.wait_ge(sem("hT_act" if k % 2 == 0 else "hT_dve"), KD // 2 * HALVED[n] + k // 2 + 1)

            def wait_parts(m, k):
                pe.wait_ge(sem("tok_lo"), KD * m + k + 1)
                pe.wait_ge(sem("w_lo"), KD * m + k + 1)

            def project(parts, splits, banks_of, full, free, first):
                for t in range(NT):
                    for j, (a, b) in enumerate(splits):
                        free(t, j)
                        for k in range(KD):
                            if t == 0 and j == 0:
                                first(k)
                            for m, (tokens, w) in enumerate(parts):
                                ins = pe.matmul(bank(banks_of(t, j))[:, 0:b - a], tokens[:, k, t * P:(t + 1) * P],
                                                w[:, k, a:b], start=(k == 0 and m == 0),
                                                stop=(k == KD - 1 and m + 1 == len(parts)))
                        ins.then_inc(sem(full), 1)

            def x_scores(l, h):
                QCT = QCT0 if l == 0 else QCT1
                at = slice((h % 2) * XD, (h % 2 + 1) * XD)
                if h >= 2:
                    pe.wait_ge(sem("x_exp"), NT * XHEADS * l + NT * (h - 1))
                for t in range(NT):
                    ins = pe.matmul(bank(2 * (h % 2) + t // 2)[:, (t % 2) * M:(t % 2 + 1) * M],
                                    QCT[at, h // 2, t * P:(t + 1) * P], MK[at, h // 2, :], start=True, stop=True)
                    if t % 2:
                        ins.then_inc(sem("xs_full"), 1)

            def cross_attention(l):
                XP, XPT = (XP0, XPT0) if l == 0 else (XP1, XPT1)

                if l == 0:
                    x_scores(l, 0)
                x_scores(l, 1)
                for h in range(XHEADS):
                    p = h % 2
                    pe.wait_ge(sem("x_exp"), NT * XHEADS * l + NT * (h + 1))
                    for c in range(MT):
                        if h >= 1:
                            pe.wait_ge(sem("xpt_act" if c == 0 else "xpt_dve"), XHEADS * l + h)
                        for t in range(NT):
                            ins = pe.transpose(bank(4 + c)[:, t * P:(t + 1) * P], XP[p][:, t, c * P:(c + 1) * P],
                                               ident[:, :])
                        ins.then_inc(sem("xp_T"), 1)
                    if h + 2 < XHEADS:
                        x_scores(l, h + 2)
                    pe.wait_ge(sem("xpt_act"), XHEADS * l + h + 1)
                    pe.wait_ge(sem("xpt_dve"), XHEADS * l + h + 1)
                    if h >= 2:
                        pe.wait_ge(sem("xmix"), XHEADS * l + h - 1)
                    for t in range(NT):
                        for c in range(MT):
                            ins = pe.matmul(bank(6 + p)[:, t * XD:(t + 1) * XD], XPT[:, c, t * P:(t + 1) * P],
                                            MV[:, c, h * XD:(h + 1) * XD], start=(c == 0), stop=(c == MT - 1))
                    ins.then_inc(sem("xo_full"), 1)

            def output_projection(l):
                pe.wait_ge(sem("xmix"), XHEADS * l + XHEADS)
                for k in range(KD):
                    if k >= 2:
                        pe.wait_ge(sem("tok_lo"), KD * 2 * l + k - 1)
                    for t in range(NT):
                        ins = pe.transpose(bank(k % 2)[:, t * P:(t + 1) * P], XN[:, t, k:D:KD], ident[:, :])
                    ins.then_inc(sem("mixT_full"), 1)
                for t in range(NT):
                    for j in range(2):
                        n = 2 * t + j
                        if n >= 4:
                            pe.wait_ge(sem("o_added"), 2 * NT * l + n - 3)
                        for k in range(KD):
                            if n == 0:
                                wait_parts(2 * l, k)
                            for m, (a, w) in enumerate(((TOK_HI, W_HI), (TOK_HI, OUT_LO), (TOK_LO, W_HI))):
                                ins = pe.matmul(bank(2 + n % 4), a[:, k, t * P:(t + 1) * P],
                                                w[:, k, j * 512:(j + 1) * 512], start=(k == 0 and m == 0),
                                                stop=(k == KD - 1 and m == 2))
                        ins.then_inc(sem("o_full"), 1)

            def router(l):
                n = 2 * l + 2

                def logits(k):
                    wait_turned(n, k)
                    return pe.matmul(bank(6)[0:NR, :], WR[:, k, :], hT[:, k, :], start=(k == 0), stop=(k == KD - 1))

                norm_turned(n, logits)
                logits(KD - 1).then_inc(sem("router_full"), 1)
                pe.wait_ge(sem("router_act"), 3 * l + 1)
                for t in range(NT):
                    ins = pe.transpose(bank(3)[:, t * NR:(t + 1) * NR], LT[0:NR, t * P:(t + 1) * P], ident[0:NR, 0:NR])
                ins.then_inc(sem("router_full"), 1)
                pe.wait_ge(sem("assigned"), l + 1)
                for t in range(NT + 1):
                    for s in range(min(t + 1, NT)):
                        ins = pe.matmul(banks[7][:, t * E:(t + 1) * E], (before if s == t else onesb)[:, :], AB[:, s, :],
                                        start=(s == 0), stop=(s == min(t, NT - 1)))
                ins.then_inc(sem("ranks_full"), 1)
                for j in range(2):
                    pe.wait_ge(sem("slot_onehots"), 2 * l + j + 1)
                    for t in range(NT):
                        ins = pe.matmul(bank(5)[0:SLOTS, 0:2 * E], RO[:, j, t, :],
                                        RH[:, j, t, :, :].rearrange("p v e -> p (v e)"),
                                        start=(j == 0 and t == 0), stop=(j == 1 and t == NT - 1))
                ins.then_inc(sem("table_full"), 1)

            def experts(l):

                def settle():
                    pe.sem_inc(sem("pe_settled"), 1)

                def rows_T(u, e, lap):
                    u, b = u % RING, u % 2
                    pe.wait_ge(sem(f"xg_in{l}_{u}"), 16 * lap + 16)
                    wait(pe, "x_lo", e - 1)
                    settle()
                    for k in range(KD):
                        ins = pe.transpose(bank(b)[:, k * SLOTS:(k + 1) * SLOTS], XG[0:SLOTS, u, k:D:KD],
                                           ident[0:SLOTS, 0:SLOTS])
                    ins.then_inc(sem("xg_full"), 1)

                def gate_up(u, e):
                    u, b = u % RING, u % 2
                    pe.wait_ge(sem("x_lo"), e + 1)
                    wait(pe, "a_ready", e - 1)
                    hi = GU_HI[:, b, :].rearrange("p (j k n) -> p j k n", j=2, k=KD)
                    lo = W_LO[u][:, 0:GU].rearrange("p (j k n) -> p j k n", j=2, k=KD)
                    for k in range(KD):
                        if k % 2 == 0:
                            pe.wait_ge(sem("gu_lo"), 4 * e + k // 2 + 1)
                        rows = slice(k * SLOTS, (k + 1) * SLOTS)
                        for n, (part, w) in enumerate(((0, hi), (0, lo), (1, hi))):
                            ins = pe.matmul(bank(2 + b, 2, FE)[0:SLOTS], XGT[:, b, part, rows], w[:, :, k, :],
                                            start=(k == 0 and n == 0), stop=(k == KD - 1 and n == 2))
                    ins.then_inc(sem("gu_full"), 1)

                def hidden_T(u, e):
                    b = u % 2
                    pe.wait_ge(sem("a_ready"), e + 1)
                    wait(pe, "a_lo", e - 1)
                    settle()
                    for k in range(KF):
                        ins = pe.transpose(bank(4 + b)[:, k * SLOTS:(k + 1) * SLOTS], SG[0:SLOTS, b, k:FE:KF],
                                           ident[0:SLOTS, 0:SLOTS])
                    ins.then_inc(sem("at_full"), 1)

                def down(u, e):
                    u, b = u % RING, u % 2
                    pe.wait_ge(sem("a_lo"), e + 1)
                    pe.wait_ge(sem("down_lo"), KF * e + KF)
                    wait(pe, "ys_act", e)
                    wait(pe, "ys_dve", e)
                    hi = DOWN_HI[:, b, :].rearrange("p (k n) -> p k n", k=KF)
                    lo = W_LO[u][:, GU:].rearrange("p (k n) -> p k n", k=KF)
                    for j in range(2):
                        for k in range(KF):
                            rows = slice(k * SLOTS, (k + 1) * SLOTS)
                            for n, (part, w) in enumerate(((0, hi), (0, lo), (1, hi))):
                                ins = pe.matmul(bank(6 + j)[0:SLOTS, :], AT[:, b, part, rows],
                                                w[:, k, j * 512:(j + 1) * 512], start=(k == 0 and n == 0),
                                                stop=(k == KF - 1 and n == 2))
                    ins.then_inc(sem("y_full"), 1)

                def step(u, e, before, after, after_lap):
                    gate_up(u, e)
                    if after is not None:
                        rows_T(u + 1, after, after_lap)
                    if before is not None:
                        down(u - 1, before)
                    hidden_T(u, e)

                rows_T(0, 0, 0)
                for e in range(RING):
                    step(e, e, e - 1 if e else None, e + 1, (e + 1) // RING)
                with pe.Fori(0, E // RING - 2) as i:
                    for u in range(RING):
                        step(u + RING, pe.snap(RING * i + (RING + u)), pe.snap(RING * i + (RING + u - 1)),
                             pe.snap(RING * i + (RING + u + 1)), pe.snap(i + (RING + u + 1) // RING))
                for e in range(E - RING, E):
                    step(e, e, e - 1, e + 1 if e + 1 < E else None, (e + 1) // RING)
                down(E - 1, E - 1)
                pe.wait_ge(sem("extra_ready"), l + 1)
                rounds = pe.value_load(extra[0:1, 0:1], min_val=0, max_val=ROUNDS - 1)
                with pe.If(rounds > 0):
                    with pe.Fori(0, rounds) as r:
                        with pe.Fori(0, E // RING) as q:
                            for u in range(RING):
                                e = pe.snap(E * r + RING * q + (E + u))
                                lap = pe.snap(E // RING * r + q + E // RING)
                                rows_T(u, e, lap)
                                gate_up(u, e)
                                hidden_T(u, e)
                                down(u, e)

            pe.wait_ge(sem("constants"), 1)
            norm_turned(0)
            pe.wait_ge(sem("w_mla_in"), 16)

            def z_free(t, j):
                if t >= 2:
                    pe.wait_ge(sem("z_key" if j == 0 else "z_xq"), t - 1)

            project([(hT, w_mla)], ((0, ZA), (ZA, ZW)), lambda t, j: 2 + 2 * (t % 2) + j, "z_full", z_free,
                    lambda k: wait_turned(0, k))
            norm_turned(1)
            pe.wait_ge(sem("tbl_ready"), 4)
            for t in range(NT):
                ins = pe.transpose(bank(7)[:, t * P:(t + 1) * P], tbl_tok[:, t, :], ident[:, :])
            ins.then_inc(sem("tblT_full"), 1)
            for k in range(KD):
                wait_turned(1, k)
            pe.wait_ge(sem("w_mkv_in"), 16)
            pe.wait_ge(sem("z_key"), NT)
            pe.wait_ge(sem("z_xq"), NT)
            for m in range(XW // P):
                for k in range(KD):
                    ins = pe.matmul(bank(2 + m)[:, 0:M], w_mkv[:, k, m * P:(m + 1) * P], memhT[:, k, :],
                                    start=(k == 0), stop=(k == KD - 1))
                ins.then_inc(sem("mk_full"), 1)
            for c in range(MT):
                for k in range(KD):
                    ins = pe.matmul(bank(4 + c)[:, 0:XW], memhT[:, k, c * P:(c + 1) * P], w_mkv[:, k, XW:],
                                    start=(k == 0), stop=(k == KD - 1))
                ins.then_inc(sem("mv_full"), 1)
            pe.wait_ge(sem("lat_normed"), 2 * NT)
            pe.wait_ge(sem("mem_ready"), 2)
            pe.wait_ge(sem("mv_ready"), 2)
            for k in range(KQ):
                for t in range(NT):
                    ins = pe.transpose(bank(k)[:, t * P:(t + 1) * P], ZS[:, t, k:QR:KQ], ident[:, :])
                ins.then_inc(sem("lat_T"), 1)
            for b, at in ((2, QR), (3, ZA), (4, ZA + P)):
                for t in range(NT):
                    ins = pe.transpose(bank(b)[:, t * P:(t + 1) * P], ZS[:, t, at:at + P], ident[:, :])
                ins.then_inc(sem("lat_T"), 1)
            pe.wait_ge(sem("kr_ready"), 3)
            for t in range(NT):
                ins = pe.transpose(bank(5)[:, t * P:(t + 1) * P], kr_tok[:, t, :], ident[:, :])
            ins.then_inc(sem("lat_T"), 1)
            pe.wait_ge(sem("lat_ready"), 3)
            pe.wait_ge(sem("w_qkv_in"), 32)
            wv = w_kv.rearrange("p (h n) -> p h n", h=H)
            for t in range(NT):
                for j in range(2):
                    if t >= 1:
                        pe.wait_ge(sem("v_act" if j == 0 else "v_dve"), t)
                    ins = pe.matmul(bank(j, H // 2, VD), KVT[:, t * P:(t + 1) * P],
                                    wv[:, j * H // 2:(j + 1) * H // 2, NOPE:], start=True, stop=True)
                    ins.then_inc(sem("v_full"), 1)
            pe.wait_ge(sem("v_act"), NT)
            pe.wait_ge(sem("v_dve"), NT)
            pe.wait_ge(sem("qct0"), 2)
            pe.wait_ge(sem("rope_done"), 1)
            cross_attention(0)
            pe.wait_ge(sem("xmix"), XHEADS)

            def head_query(s, h):
                pe.wait_ge(sem("wh_ready"), 4 * h + 4)
                wait(pe, "q_nope", h)
                wait(pe, "q_rope", h)
                for k in range(KQ):
                    ins = pe.matmul(bank(4), wqh[s][:, k, :], QLT[:, k, :], start=(k == 0), stop=(k == KQ - 1))
                ins.then_inc(sem("q_full"), 1)

            def head_key(s, h):
                wait(pe, "k_nope", h)
                pe.matmul(bank(5)[0:NOPE, :], wkh[s], KVT, start=True, stop=True).then_inc(sem("k_full"), 1)

            def head_scores(s, h):
                pe.wait_ge(sem("q_nope"), h + 1)
                pe.wait_ge(sem("k_nope"), h + 1)
                pe.wait_ge(sem("q_rope"), h + 1)
                wait(pe, "probs", 4 * h)
                for b, at, t, done in ((1, 0, 0, 0), (1, 128, 2, 1), (2, 0, 1, 1), (0, 0, 3, 1)):
                    n = (t + 1) * P
                    pe.matmul(bank(b)[:, at:at + n], qT[s][0:QKD, t * P:(t + 1) * P], kT[s][0:QKD, 0:n],
                              start=True, stop=False)
                    ins = pe.matmul(bank(b)[:, at + t * P:at + n], identb[:, :], causal[:, :], start=False, stop=True)
                    if done:
                        ins.then_inc(sem("scores_full"), 1)

            AT_OF = (0, 128, 384, 768)

            def turn(t, p, h):
                pe.wait_ge(sem("probs"), 4 * h + t + 1)
                wait(pe, "pt_dve" if t % 2 == 0 else "pt_act", 2 * h + t // 2)
                for c in range(t + 1):
                    a = AT_OF[t] + c * P
                    ins = pe.transpose(bank(6 + t % 2)[:, c * P:(c + 1) * P], PR[p][:, a:a + P], ident[:, :])
                ins.then_inc(sem("p_T"), 1)

            def product(t, h, col):
                pe.wait_ge(sem("pt_dve" if t % 2 == 0 else "pt_act"), 2 * h + t // 2 + 1)
                if t == 0:
                    wait(pe, "mixed", h)
                for c in range(t + 1):
                    part = PT[:, PT_AT[t] + c * P:PT_AT[t] + (c + 1) * P]
                    ins = pe.matmul(bank(3)[:, t * VD:(t + 1) * VD], part, V[:, c, bass.ds(col, VD)],
                                    start=(c == 0), stop=(c == t))
                ins.then_inc(sem("o_done"), 1)

            def head_step(p, h, after, before, col):
                if h is not None:
                    head_scores(p, h)
                if before is not None:
                    turn(0, 1 - p, before)
                    turn(1, 1 - p, before)
                if after is not None:
                    head_query(1 - p, after)
                if before is not None:
                    turn(2, 1 - p, before)
                if after is not None:
                    head_key(1 - p, after)
                if before is not None:
                    product(0, before, col)
                    product(1, before, col)
                    turn(3, 1 - p, before)
                    product(2, before, col)
                    product(3, before, col)

            head_query(0, 0)
            head_key(0, 0)
            head_step(0, 0, 1, None, None)
            head_step(1, 1, 2, 0, 0)
            with pe.Fori(0, H // 2 - 2) as i:
                for p in range(2):
                    head_step(p, pe.snap(2 * i + (2 + p)), pe.snap(2 * i + (3 + p)), pe.snap(2 * i + (1 + p)),
                              pe.snap(2 * VD * i + (1 + p) * VD))
            head_step(0, H - 2, H - 1, H - 3, (H - 3) * VD)
            head_step(1, H - 1, None, H - 2, (H - 2) * VD)
            head_step(0, None, None, H - 1, (H - 1) * VD)
            pe.wait_ge(sem("mixed"), H)
            output_projection(0)
            router(0)
            experts(0)
            norm_turned(3)

            def zp_free(t, j):
                if t >= 2:
                    pe.wait_ge(sem("u_act" if j == 0 else "u_dve"), t - 1 if j == 0 else 2 * (t - 1))

            project([(TOK_HI, W_HI), (TOK_HI, POOL_LO), (TOK_LO, W_HI)], ((0, 512), (512, D)),
                    lambda t, j: 2 + 2 * (t % 2) + j, "zp_full", zp_free, lambda k: wait_parts(1, k))
            pe.wait_ge(sem("u_act"), NT)
            pe.wait_ge(sem("u_dve"), 2 * NT)
            for m in range(XW // P):
                for t in range(NT):
                    ins = pe.transpose(bank(m)[:, t * P:(t + 1) * P], QC[:, t, m * P:(m + 1) * P], ident[:, :])
                ins.then_inc(sem("qcT_full1"), 1)
            pe.wait_ge(sem("bands_ready"), 3 * len(WINDOWS))
            for j in range(2 * len(WINDOWS)):
                g, b = j // 2, bank(6 + j % 2)[0:HW, :]
                if j >= 2:
                    pe.wait_ge(sem("d_act" if j % 2 == 0 else "d_dve"), j // 2)
                for t in range(NT):
                    lhs = U[:, t, j * HW:(j + 1) * HW]
                    if t == 0:
                        pe.matmul(b[:, 0:16], lhs, band0[:, g, :], start=True, stop=False, skip_group_check=True)
                        pe.matmul(b[:, 16:HALO], lhs, band[:, g, 16:HALO], start=False, stop=False,
                                  skip_group_check=True)
                    else:
                        end = min(S, t * P + HALO)
                        ins = pe.matmul(b[:, t * P:end], lhs, band[:, g, 0:end - t * P], start=False,
                                        stop=(t == NT - 1), skip_group_check=True)
                ins.then_inc(sem("d_full"), 1)
            pe.wait_ge(sem("u_act"), NT + 1)
            pe.wait_ge(sem("u_dve"), 2 * NT + 1)
            x_scores(1, 0)
            pe.wait_ge(sem("w_mix_in"), 32)
            pe.wait_ge(sem("d_act"), len(WINDOWS))
            pe.wait_ge(sem("d_dve"), len(WINDOWS))
            for t in range(NT):
                for j in range(2):
                    if t >= 2:
                        pe.wait_ge(sem("pool_mixed"), 2 * (t - 2) + j + 1)
                    for g in range(2):
                        for c in range(2):
                            jj = 2 * (2 * j + g) + c
                            ins = pe.matmul(bank(2 + 2 * (t % 2) + j)[:, g * GW:(g + 1) * GW],
                                            dT[0:HW, jj, t * P:(t + 1) * P], w_mix[0:HW, jj, :],
                                            start=(c == 0), stop=(c == 1))
                    ins.then_inc(sem("y_pool"), 1)
            pe.wait_ge(sem("pool_mixed"), 2 * NT)
            cross_attention(1)
            output_projection(1)
            router(1)
            experts(1)


_INS = ['x', 'mem', 'positions', 'g_mix', 'w_in_mla', 'g_q_lat', 'w_uq', 'g_kv_lat', 'w_ukv', 'w_in_pool',
        'w_pool_mix', 'pool_scale', 'g_mem', 'w_mem_kv', 'w_o', 'g_ffn', 'w_router_group', 'b_router_group',
        'w_router_expert', 'b_router_expert', 'w_expert_gate', 'w_expert_up', 'w_expert_down', 'g_final']


def kernel(**inputs):
    import numpy as _np
    import concourse.bacc as _bacc
    from concourse import mybir as _mybir
    from concourse.bass_utils import run_bass_kernel_spmd as _run

    nc = _bacc.Bacc("TRN2", target_bir_lowering=False, num_devices=1)
    arrays, args = {}, []
    for name in _INS:
        a = _np.ascontiguousarray(inputs[name])
        arrays[f"in_{name}_dram"] = a
        args.append(nc.dram_tensor(f"in_{name}_dram", a.shape, _mybir.dt.from_np(a.dtype), kind="ExternalInput").ap())
    shape = inputs['x'].shape
    out = nc.dram_tensor("out_0_dram", shape, _mybir.dt.float32, kind="ExternalOutput").ap()
    program(nc, *args, out)
    r = _run(nc, [arrays], core_ids=[0])
    return r.results[0]["out_0_dram"]
```
